# Optimizing a Trainium2 kernel written in Bass

```python
import math
import jax, jax.numpy as jnp
from jax import lax
import numpy as np

D_MODEL = 1024
BATCH = 1
SEQ = 256
DEPTH = 2

N_EVEN = (DEPTH + 1) // 2
N_ODD = DEPTH // 2

D_A = D_MODEL // 2
A_CONV = 3
D_B = D_MODEL // 2
POOL_WINDOWS = (2, 4, 8, 16)
POOL_GROUPS = len(POOL_WINDOWS)
POOL_GC = D_B // POOL_GROUPS
EV_IN = 3 * D_A + D_B
EV_MIX = D_A + D_B

D_C = D_MODEL // 2
HEAD_DIM = 64
H_C = D_C // HEAD_DIM
Q_BLOCK = 128
D_D = D_MODEL // 2
D_CONV = 31
OD_IN = 3 * D_C + H_C + 2 * D_D
OD_MIX = D_C + D_D

D_FF = int(math.ceil((8 * D_MODEL / 3) / 256) * 256)

ALPHA = (2.0 * DEPTH) ** 0.25
BETA = (8.0 * DEPTH) ** -0.25
LN_EPS = 1e-5


def layer_norm(x, g, b):
    x32 = x.astype(jnp.float32)
    mu = jnp.mean(x32, axis=-1, keepdims=True)
    var = jnp.mean(jnp.square(x32 - mu), axis=-1, keepdims=True)
    y = (x32 - mu) * lax.rsqrt(var + LN_EPS)
    return (y * g.astype(jnp.float32) + b.astype(jnp.float32)).astype(x.dtype)

def causal_dwconv(x, w):
    k = w.shape[0]
    return lax.conv_general_dilated(
        x, w[:, None, :].astype(x.dtype), window_strides=(1,), padding=[(k - 1, 0)],
        dimension_numbers=("NWC", "WIO", "NWC"), feature_group_count=x.shape[-1])

def short_gated_conv(p_a, conv_w):
    b_gate = p_a[..., :D_A]
    c_gate = p_a[..., D_A:2 * D_A]
    val = p_a[..., 2 * D_A:]
    return b_gate * causal_dwconv(c_gate * val, conv_w)

def multiscale_pool(u, w_grp, scale):
    bsz, s, _ = u.shape
    u32 = u.astype(jnp.float32).reshape(bsz, s, POOL_GROUPS, POOL_GC)
    cs = jnp.cumsum(u32, axis=1)
    pos = jnp.arange(s)
    pooled = []
    for g, win in enumerate(POOL_WINDOWS):
        c = cs[:, :, g]
        lagged = jnp.pad(c, ((0, 0), (win, 0), (0, 0)))[:, :s]
        cnt = jnp.minimum(pos + 1, win).astype(jnp.float32)[None, :, None]
        pooled.append((c - lagged) / cnt)
    pooled = (jnp.stack(pooled, axis=2) - u32).astype(u.dtype)
    y = jnp.einsum("bsgc,gcd->bsgd", pooled, w_grp).reshape(bsz, s, D_B)
    return y * scale

def forgetting_attention(q, k, v, log_f):
    s_len = q.shape[1]
    cum = jnp.cumsum(log_f.astype(jnp.float32), axis=1).transpose(0, 2, 1)
    scale = 1.0 / math.sqrt(HEAD_DIM)
    outs = []
    for blk in range(s_len // Q_BLOCK):
        q0, q1 = blk * Q_BLOCK, (blk + 1) * Q_BLOCK
        logits = jnp.einsum("bqhd,bkhd->bhqk", q[:, q0:q1], k[:, :q1]).astype(jnp.float32) * scale
        logits = logits + cum[:, :, q0:q1, None] - cum[:, :, None, :q1]
        mask = jnp.arange(q0, q1)[:, None] >= jnp.arange(q1)[None, :]
        logits = jnp.where(mask[None, None], logits, -1e30)
        probs = jax.nn.softmax(logits, axis=-1).astype(v.dtype)
        outs.append(jnp.einsum("bhqk,bkhd->bqhd", probs, v[:, :q1]))
    return jnp.concatenate(outs, axis=1)

def conformer_conv(p_d, dw_w, dw_b, cn_g, cn_b):
    h = p_d[..., :D_D] * jax.nn.sigmoid(p_d[..., D_D:])
    h = causal_dwconv(h, dw_w) + dw_b
    h = layer_norm(h, cn_g, cn_b)
    return jax.nn.silu(h)

def even_mixer(x, w_in, conv_w, pool_w, pool_scale, w_out):
    p = x @ w_in
    y_a = short_gated_conv(p[..., :3 * D_A], conv_w)
    y_b = multiscale_pool(p[..., 3 * D_A:], pool_w, pool_scale)
    return jnp.concatenate([y_a, y_b], axis=-1) @ w_out

def odd_mixer(x, w_in, forget_b, dw_w, dw_b, cn_g, cn_b, w_out):
    bsz, s, _ = x.shape
    p = x @ w_in
    q = p[..., :D_C].reshape(bsz, s, H_C, HEAD_DIM)
    k = p[..., D_C:2 * D_C].reshape(bsz, s, H_C, HEAD_DIM)
    v = p[..., 2 * D_C:3 * D_C].reshape(bsz, s, H_C, HEAD_DIM)
    log_f = jax.nn.log_sigmoid((p[..., 3 * D_C:3 * D_C + H_C] + forget_b).astype(jnp.float32))
    y_c = forgetting_attention(q, k, v, log_f).reshape(bsz, s, D_C)
    y_d = conformer_conv(p[..., 3 * D_C + H_C:], dw_w, dw_b, cn_g, cn_b)
    return jnp.concatenate([y_c, y_d], axis=-1) @ w_out

def swiglu(x, w_in, w_out):
    h = x @ w_in
    return (jax.nn.silu(h[..., :D_FF]) * h[..., D_FF:]) @ w_out

def first_inputs(seed: int = 0) -> dict:
    key = jax.random.key(seed)
    ks = jax.random.split(key, 24)
    f32 = jnp.float32
    nrm = lambda k, shape, s: jax.random.normal(k, shape, f32) * s
    x = jax.random.normal(ks[0], (BATCH, SEQ, D_MODEL), f32)
    ev_w_in = nrm(ks[1], (N_EVEN, D_MODEL, EV_IN), D_MODEL ** -0.5)
    ev_conv_w = nrm(ks[2], (N_EVEN, A_CONV, D_A), A_CONV ** -0.5)
    ev_pool_w = nrm(ks[3], (N_EVEN, POOL_GROUPS, POOL_GC, POOL_GC), POOL_GC ** -0.5)
    ev_pool_scale = 1.0 + nrm(ks[4], (N_EVEN, D_B), 0.1)
    ev_w_out = nrm(ks[5], (N_EVEN, EV_MIX, D_MODEL), EV_MIX ** -0.5 * BETA)
    col_scale = jnp.ones((OD_IN,), f32).at[2 * D_C:3 * D_C].set(BETA)
    od_w_in = nrm(ks[6], (N_ODD, D_MODEL, OD_IN), D_MODEL ** -0.5) * col_scale
    od_forget_b = jax.random.uniform(ks[7], (N_ODD, H_C), f32, 1.0, 4.0)
    od_dw_w = nrm(ks[8], (N_ODD, D_CONV, D_D), D_CONV ** -0.5)
    od_dw_b = nrm(ks[9], (N_ODD, D_D), 0.02)
    od_cn_g = 1.0 + nrm(ks[10], (N_ODD, D_D), 0.05)
    od_cn_b = nrm(ks[11], (N_ODD, D_D), 0.02)
    od_w_out = nrm(ks[12], (N_ODD, OD_MIX, D_MODEL), OD_MIX ** -0.5 * BETA)
    ln_mix_g = 1.0 + nrm(ks[13], (DEPTH, D_MODEL), 0.05)
    ln_mix_b = nrm(ks[14], (DEPTH, D_MODEL), 0.02)
    ln_ffn_g = 1.0 + nrm(ks[15], (DEPTH, D_MODEL), 0.05)
    ln_ffn_b = nrm(ks[16], (DEPTH, D_MODEL), 0.02)
    ffn_w_in = nrm(ks[17], (DEPTH, D_MODEL, 2 * D_FF), D_MODEL ** -0.5)
    ffn_w_out = nrm(ks[18], (DEPTH, D_FF, D_MODEL), D_FF ** -0.5 * BETA)
    return {"x": x, "ev_w_in": ev_w_in, "ev_conv_w": ev_conv_w, "ev_pool_w": ev_pool_w,
            "ev_pool_scale": ev_pool_scale, "ev_w_out": ev_w_out, "od_w_in": od_w_in,
            "od_forget_b": od_forget_b, "od_dw_w": od_dw_w, "od_dw_b": od_dw_b,
            "od_cn_g": od_cn_g, "od_cn_b": od_cn_b, "od_w_out": od_w_out,
            "ln_mix_g": ln_mix_g, "ln_mix_b": ln_mix_b, "ln_ffn_g": ln_ffn_g,
            "ln_ffn_b": ln_ffn_b, "ffn_w_in": ffn_w_in, "ffn_w_out": ffn_w_out}

def first_block(x, ev_w_in, ev_conv_w, ev_pool_w, ev_pool_scale, ev_w_out, od_w_in,
              od_forget_b, od_dw_w, od_dw_b, od_cn_g, od_cn_b, od_w_out,
              ln_mix_g, ln_mix_b, ln_ffn_g, ln_ffn_b, ffn_w_in, ffn_w_out):
    for layer in range(DEPTH):
        i = layer // 2
        if layer % 2 == 0:
            mix = even_mixer(x, ev_w_in[i], ev_conv_w[i], ev_pool_w[i], ev_pool_scale[i], ev_w_out[i])
        else:
            mix = odd_mixer(x, od_w_in[i], od_forget_b[i], od_dw_w[i], od_dw_b[i],
                            od_cn_g[i], od_cn_b[i], od_w_out[i])
        x = layer_norm(ALPHA * x + mix, ln_mix_g[layer], ln_mix_b[layer])
        x = layer_norm(ALPHA * x + swiglu(x, ffn_w_in[layer], ffn_w_out[layer]),
                       ln_ffn_g[layer], ln_ffn_b[layer])
    return x


ATTN_HEADS = 8
ATTN_WIDTH = ATTN_HEADS * HEAD_DIM
GLA_HEADS = 4
GLA_DK = 64
GLA_DV = 128
GLA_K_WIDTH = GLA_HEADS * GLA_DK
GLA_V_WIDTH = GLA_HEADS * GLA_DV
GLA_GATE_RANK = 16
GLA_TAU = 16.0
GLA_CHUNK = 64
MIX_WIDTH = ATTN_WIDTH + GLA_V_WIDTH
IN_WIDTH = 3 * ATTN_WIDTH + 2 * GLA_K_WIDTH + 2 * GLA_V_WIDTH + GLA_GATE_RANK
D_FF_2 = -(-8 * D_MODEL // (3 * 256)) * 256
ROPE_THETA = 500000.0
ROPE_DIM = HEAD_DIM // 4
DILATED_PATTERNS = ((128, 1), (512, 4), (2048, 16))
N_PATTERNS = len(DILATED_PATTERNS)
N_KEYS = DILATED_PATTERNS[0][0] // DILATED_PATTERNS[0][1] + 1
RMS_EPS = 1e-6


F32 = jnp.float32

def rmsnorm(x, g):
    xf = x.astype(F32)
    y = xf * lax.rsqrt(jnp.mean(xf * xf, axis=-1, keepdims=True) + RMS_EPS)
    return (y * g.astype(F32)).astype(x.dtype)

def rope_partial(x, pos):
    half = ROPE_DIM // 2
    inv = ROPE_THETA ** (-(jnp.arange(half, dtype=F32) * 2.0) / ROPE_DIM)
    ang = pos.astype(F32)[:, None] * inv[None, :]
    cos = jnp.cos(ang)[None, :, None, :]
    sin = jnp.sin(ang)[None, :, None, :]
    xr = x[..., :ROPE_DIM].astype(F32)
    x1, x2 = xr[..., :half], xr[..., half:]
    rot = jnp.concatenate([x1 * cos - x2 * sin, x2 * cos + x1 * sin], axis=-1).astype(x.dtype)
    return jnp.concatenate([rot, x[..., ROPE_DIM:]], axis=-1)

def dilated_attention(q, k, v):
    B, S, H, hd = q.shape
    nblk = S // Q_BLOCK
    dists = jnp.concatenate([d * jnp.arange(w // d + 1) for (w, d) in DILATED_PATTERNS])
    q_blocks = q.reshape(B, nblk, Q_BLOCK, H, hd).transpose(1, 0, 2, 3, 4)
    starts = jnp.arange(nblk) * Q_BLOCK
    scale = hd ** -0.5

    def block(args):
        q_blk, start = args
        pos = start + jnp.arange(Q_BLOCK)
        idx = pos[:, None] - dists[None, :]
        valid = idx >= 0
        idx_c = jnp.maximum(idx, 0)
        kg = jnp.take(k, idx_c, axis=1).astype(F32)
        vg = jnp.take(v, idx_c, axis=1).astype(F32)
        s = jnp.einsum('bqhd,bqnhd->bhqn', q_blk.astype(F32), kg) * scale
        s = jnp.where(valid[None, None], s, -jnp.inf)
        s = s.reshape(B, H, Q_BLOCK, N_PATTERNS, N_KEYS)
        lse = jax.nn.logsumexp(s, axis=-1, keepdims=True)
        p = jnp.exp(s - lse)
        o_pat = jnp.einsum('bhqpn,bqpnhd->bhqpd', p,
                           vg.reshape(B, Q_BLOCK, N_PATTERNS, N_KEYS, H, hd))
        w = jax.nn.softmax(lse, axis=-2)
        o = jnp.sum(w * o_pat, axis=-2)
        return o.transpose(0, 2, 1, 3).astype(q.dtype)

    out = lax.map(block, (q_blocks, starts))
    return out.transpose(1, 0, 2, 3, 4).reshape(B, S, H, hd)

def gla_chunked(q, k, v, g):
    B, S, H, dk = q.shape
    dv = v.shape[-1]
    C = GLA_CHUNK
    nc = S // C

    def chunks(t):
        return t.astype(F32).reshape(B, nc, C, H, t.shape[-1]).transpose(1, 0, 3, 2, 4)

    causal = jnp.tril(jnp.ones((C, C), dtype=bool))

    def step(state, inp):
        qc, kc, vc, gc = inp
        b = jnp.cumsum(gc, axis=-2)
        o_inter = jnp.einsum('bhtk,bhkv->bhtv', qc * jnp.exp(b), state)
        diff = b[:, :, :, None, :] - b[:, :, None, :, :]
        decay = jnp.exp(jnp.where(causal[None, None, :, :, None], diff, -jnp.inf))
        attn = jnp.einsum('bhtk,bhsk,bhtsk->bhts', qc, kc, decay)
        o_intra = jnp.einsum('bhts,bhsv->bhtv', attn, vc)
        b_last = b[:, :, -1:, :]
        state = jnp.exp(b_last[:, :, 0, :])[..., None] * state + \
            jnp.einsum('bhsk,bhsv->bhkv', kc * jnp.exp(b_last - b), vc)
        return state, o_intra + o_inter

    s0 = jnp.zeros((B, H, dk, dv), F32)
    _, o = lax.scan(step, s0, (chunks(q) * (dk ** -0.5), chunks(k), chunks(v), chunks(g)))
    return o.transpose(1, 0, 3, 2, 4).reshape(B, S, H, dv).astype(v.dtype)

def hybrid_mixer(h, w_in, gla_w_gate_up, gla_b_gate, gla_out_norm, attn_out_norm, w_out):
    B, S, _ = h.shape
    proj = h @ w_in
    cuts = [ATTN_WIDTH, 2 * ATTN_WIDTH, 3 * ATTN_WIDTH,
            3 * ATTN_WIDTH + GLA_K_WIDTH, 3 * ATTN_WIDTH + 2 * GLA_K_WIDTH,
            3 * ATTN_WIDTH + 2 * GLA_K_WIDTH + GLA_V_WIDTH,
            3 * ATTN_WIDTH + 2 * GLA_K_WIDTH + 2 * GLA_V_WIDTH]
    aq, ak, av, gq, gk, gv, gr, g_low = jnp.split(proj, cuts, axis=-1)

    pos = jnp.arange(S)
    aq = rope_partial(aq.reshape(B, S, ATTN_HEADS, HEAD_DIM), pos)
    ak = rope_partial(ak.reshape(B, S, ATTN_HEADS, HEAD_DIM), pos)
    av = av.reshape(B, S, ATTN_HEADS, HEAD_DIM)
    a_out = dilated_attention(aq, ak, av).reshape(B, S, ATTN_WIDTH)
    a_out = rmsnorm(a_out, attn_out_norm)

    z = g_low @ gla_w_gate_up + gla_b_gate
    log_alpha = jax.nn.log_sigmoid(z.astype(F32)) / GLA_TAU
    o = gla_chunked(gq.reshape(B, S, GLA_HEADS, GLA_DK),
                    gk.reshape(B, S, GLA_HEADS, GLA_DK),
                    gv.reshape(B, S, GLA_HEADS, GLA_DV),
                    log_alpha.reshape(B, S, GLA_HEADS, GLA_DK))
    o = rmsnorm(o, gla_out_norm.reshape(GLA_HEADS, GLA_DV)).reshape(B, S, GLA_V_WIDTH)
    g_out = o * jax.nn.silu(gr)

    mixed = jnp.concatenate([a_out, g_out], axis=-1)
    return mixed @ w_out

def swiglu_2(h, w_gate, w_up, w_down):
    return (jax.nn.silu(h @ w_gate) * (h @ w_up)) @ w_down

def second_inputs(seed: int = 0) -> dict:
    key = jax.random.key(seed)
    ks = jax.random.split(key, 16)
    L, D = DEPTH, D_MODEL

    def nrm(k, shape, fan_in):
        return jax.random.normal(k, shape, F32) * (fan_in ** -0.5)

    def gain(k, shape):
        return 1.0 + 0.05 * jax.random.normal(k, shape, F32)

    return {
        "x": jax.random.normal(ks[0], (BATCH, SEQ, D), F32),
        "mix_pre_norm": gain(ks[1], (L, D)),
        "mix_post_norm": gain(ks[2], (L, D)),
        "ffn_pre_norm": gain(ks[3], (L, D)),
        "ffn_post_norm": gain(ks[4], (L, D)),
        "w_in": nrm(ks[5], (L, D, IN_WIDTH), D),
        "gla_w_gate_up": nrm(ks[6], (L, GLA_GATE_RANK, GLA_K_WIDTH), GLA_GATE_RANK),
        "gla_b_gate": 0.1 * jax.random.normal(ks[7], (L, GLA_K_WIDTH), F32),
        "gla_out_norm": gain(ks[8], (L, GLA_V_WIDTH)),
        "attn_out_norm": gain(ks[9], (L, ATTN_WIDTH)),
        "w_out": nrm(ks[10], (L, MIX_WIDTH, D), MIX_WIDTH),
        "w_gate": nrm(ks[11], (L, D, D_FF_2), D),
        "w_up": nrm(ks[12], (L, D, D_FF_2), D),
        "w_down": nrm(ks[13], (L, D_FF_2, D), D_FF_2),
    }

def second_block(x, mix_pre_norm, mix_post_norm, ffn_pre_norm, ffn_post_norm, w_in,
              gla_w_gate_up, gla_b_gate, gla_out_norm, attn_out_norm, w_out,
              w_gate, w_up, w_down):
    h = x
    for l in range(DEPTH):
        m = hybrid_mixer(rmsnorm(h, mix_pre_norm[l]), w_in[l], gla_w_gate_up[l], gla_b_gate[l],
                         gla_out_norm[l], attn_out_norm[l], w_out[l])
        h = h + rmsnorm(m, mix_post_norm[l])
        f = swiglu_2(rmsnorm(h, ffn_pre_norm[l]), w_gate[l], w_up[l], w_down[l])
        h = h + rmsnorm(f, ffn_post_norm[l])
    return h


def setup_inputs(seed=0):
    out = dict(first_inputs(seed))
    for name, value in second_inputs(seed + 1).items():
        if name != "x":
            out[name + "_2"] = value
    return out


def reference(
    x, ev_w_in, ev_conv_w, ev_pool_w, ev_pool_scale, ev_w_out, od_w_in, od_forget_b, od_dw_w,
    od_dw_b, od_cn_g, od_cn_b, od_w_out, ln_mix_g, ln_mix_b, ln_ffn_g, ln_ffn_b, ffn_w_in,
    ffn_w_out, mix_pre_norm_2, mix_post_norm_2, ffn_pre_norm_2, ffn_post_norm_2, w_in_2,
    gla_w_gate_up_2, gla_b_gate_2, gla_out_norm_2, attn_out_norm_2, w_out_2, w_gate_2, w_up_2,
    w_down_2,
):
    x = first_block(
        x, ev_w_in, ev_conv_w, ev_pool_w, ev_pool_scale, ev_w_out, od_w_in, od_forget_b,
        od_dw_w, od_dw_b, od_cn_g, od_cn_b, od_w_out, ln_mix_g, ln_mix_b, ln_ffn_g, ln_ffn_b,
        ffn_w_in, ffn_w_out,
    )
    return second_block(
        x, mix_pre_norm_2, mix_post_norm_2, ffn_pre_norm_2, ffn_post_norm_2, w_in_2,
        gla_w_gate_up_2, gla_b_gate_2, gla_out_norm_2, attn_out_norm_2, w_out_2, w_gate_2,
        w_up_2, w_down_2,
    )


_drawn_inputs = setup_inputs


def setup_inputs(seed=0):
    import zlib

    import numpy as np

    out = dict(_drawn_inputs(seed))
    spreads = {}
    factors = {'od_cn_b': 3.993}
    for name, (base, spread) in spreads.items():
        noise = np.random.default_rng([zlib.crc32(name.encode()), seed]).standard_normal(out[name].shape)
        drawn = base * np.exp(spread * noise) if base else spread * noise
        out[name] = __import__('jax').numpy.asarray(drawn.astype(out[name].dtype))
    for name, factor in factors.items():
        out[name] = (out[name] * factor).astype(out[name].dtype)
    return out
```

```python
from contextlib import ExitStack

import concourse.bass as bass
from concourse import mybir

ALU = mybir.AluOpType
ACT = mybir.ActivationFunctionType
AX_X = mybir.AxisListType.X
F32 = mybir.dt.float32
F32R = mybir.dt.float32r
I32 = mybir.dt.int32

P = 128
D = 1024
SEQ = 256
NT = SEQ // P
KD = D // P
CH = 512
D_FF = 2816
FC = 256
NC = D_FF // FC
KF = D_FF // P
HALF = D // 2
DEPTH = 2
ALPHA = (2.0 * DEPTH) ** 0.25
LN_EPS = 1e-5
RMS_EPS = 1e-6
HEADS = 8
HD = 64
SCALE = HD ** -0.5
MASKED = -1e30
TAPS = 31
ROPE_HALF = 8
ROPE_THETA = 500000.0
RANK = 16
GLA_H = 4
GLA_DK = 64
GLA_DV = 128
GLA_SCALE = GLA_DK ** -0.5
GLA_TAU = 16.0
DILATED = ((128, 1), (512, 4), (2048, 16))
WINDOWS = (2, 4, 8, 16)
PAD = 16

LAYERS = ("even", "odd", "hyb", "hyb")
EV_COLS = (512, 1024, 1536, 0)
OD_COLS = (1544, 2056, 0, 512, 1024)
HY_COLS = (1536, 0, 512, 1024, 2048, 2560)
COLS = (EV_COLS, OD_COLS, HY_COLS, HY_COLS)
OD_F = 1536
HY_LOW = 3072
GATES = 8
TINY = {1: (0, GATES), 2: (GATES, RANK), 3: (GATES + RANK, RANK)}
TINY_W = GATES + 2 * RANK

LEVELS = (128, 64, 32, 16, 8, 4, 2, 1)

C_IDENT = 0
C_TRI = C_IDENT + P
C_CAUSAL = C_TRI + 2 * P
C_DIL = C_CAUSAL + P
C_COS = C_DIL + 3 * P
C_SIN = C_COS + NT * ROPE_HALF
C_LEVEL = C_SIN + NT * ROPE_HALF
C_POOL = C_LEVEL + (len(LEVELS) - 1) * P
N_CONST = C_POOL + len(WINDOWS) * PAD

R_EVCONV, R_PSCALE, R_DW, R_DWB, R_CNG, R_CNB, R_GLAB = 0, 3, 4, 35, 36, 37, 38
N_ROWS = 39

PARAMS = 16 * 13

N_RAW = 4
N_W = 12
LOOP = 3


def shape_constants():
    import numpy as np

    c = np.zeros((P, N_CONST), np.float32)
    i = np.arange(P)
    c[:, C_IDENT:C_IDENT + P] = np.eye(P)
    c[:, C_TRI:C_TRI + P] = i[:, None] <= i[None, :]
    c[:, C_TRI + P:C_TRI + 2 * P] = 1.0
    c[:, C_CAUSAL:C_CAUSAL + P] = np.where(i[:, None] >= i[None, :], 0.0, MASKED / SCALE)

    def dilated(dist):
        n = sum(((dist >= 0) & (dist <= w) & (dist % d == 0)).astype(np.int64) for w, d in DILATED)
        return np.where(n > 0, np.log(np.maximum(n, 1)), MASKED) / SCALE

    near = i[:, None] - i[None, :]
    c[:, C_DIL:C_DIL + P] = dilated(near)
    c[:, C_DIL + P:C_DIL + 2 * P] = dilated(near + P)
    c[:, C_DIL + 2 * P:C_DIL + 3 * P] = dilated(near)
    inv = np.float32(ROPE_THETA) ** (-(np.arange(ROPE_HALF, dtype=np.float32) * 2.0) / np.float32(2 * ROPE_HALF))
    ang = np.arange(SEQ, dtype=np.float32)[:, None] * inv.astype(np.float32)[None, :]
    for t in range(NT):
        c[:, C_COS + ROPE_HALF * t:C_COS + ROPE_HALF * (t + 1)] = np.cos(ang[P * t:P * (t + 1)])
        c[:, C_SIN + ROPE_HALF * t:C_SIN + ROPE_HALF * (t + 1)] = np.sin(ang[P * t:P * (t + 1)])
    for n, m in enumerate(LEVELS[1:]):
        blk = i // (2 * m)
        right = i // m % 2
        c[:, C_LEVEL + P * n:C_LEVEL + P * (n + 1)] = (
            (blk[:, None] == blk[None, :]) & (right[:, None] == 0) & (right[None, :] == 1))
    for g, w in enumerate(WINDOWS):
        c[:, C_POOL + PAD * g:C_POOL + PAD * (g + 1)] = 1.0 / np.minimum(np.arange(PAD) + 1, w)
    return c


class Stage:

    def __init__(self, sem, per, layers):
        self.sem, self.per, self.layers = sem, per, layers

    def at(self, layer, i):
        return self.layers.index(layer) * self.per + i + 1


class Chain:

    def __init__(self, eng, sem):
        self.eng, self.sem, self.n = eng, sem, 0

    def step(self, ins):
        self.n += 1
        ins.then_inc(self.sem, 1)
        return self.n

    def settle(self, n=None):
        self.eng.wait_ge(self.sem, self.n if n is None else n)


class Unit:

    def __init__(self, u, j=0):
        self.raw = u % N_RAW
        self.slot = u % N_W
        self.loads = u // N_RAW + (N_W // N_RAW) * j + 1
        self.n = u + N_W * j
        self.first = u < N_RAW
        self.fresh = u < N_W


def blocks_kernel(nc, a, out):
    ctx = ExitStack()
    with ctx:
        top = [2048]

        def place(name, shape, dt, at=None):
            size = 4
            for n in shape[1:]:
                size *= n
            if at is None:
                at = top[0]
                top[0] += (size + 31) // 32 * 32
            return nc.alloc_sbuf_tensor_at(name, list(shape), dt, offset=at), at

        raw, _ = place("raw", [P, N_RAW, 2 * CH], F32)
        w_hi, _ = place("w_hi", [P, N_W, 2 * CH], F32R)
        w_lo, _ = place("w_lo", [P, N_W, 2 * CH], F32R)
        x, _ = place("x", [P, NT, D], F32)
        a_hi, at_a = place("a_hi", [P, KD, SEQ], F32R)
        a_lo, _ = place("a_lo", [P, KD, SEQ], F32R)
        h_hi, at_h = place("h_hi", [P, KF, SEQ], F32R)
        h_lo, _ = place("h_lo", [P, KF, SEQ], F32R)
        rows, _ = place("rows", [P, 3, D], F32)
        nbuf, _ = place("nbuf", [P, D], F32)
        const, _ = place("const", [P, N_CONST], F32)
        pcol, _ = place("pcol", [P, 4, N_ROWS], F32)
        w_up, _ = place("w_up", [RANK, 2, SEQ], F32)
        tiny_hi, _ = place("tiny_hi", [P, KD, TINY_W], F32R)
        tiny_lo, _ = place("tiny_lo", [P, KD, TINY_W], F32R)
        fbias, _ = place("fbias", [P, GATES], F32)
        stat, _ = place("stat", [P, 160], F32)
        silu, at_s = place("silu", [P, 2, NT, FC], F32)
        glu, _ = place("glu", [P, 2, NT, FC], F32)
        assert top[0] <= nc.SBUF_PARTITION_SIZE_BYTES, top[0]

        tiny_raw, _ = place("tiny_raw", [P, KD, TINY_W], F32, at_s)
        prow, _ = place("prow", [N_ROWS, HALF], F32, at_s + 4096)
        squares, _ = place("squares", [P, D], F32, at_s)
        Y_LO = KF - KD
        at_m = at_h + KD * SEQ * 4

        def scratch(name, shape, slot):
            return place(name, shape, F32, int(at_m + 4096 * slot))[0]

        def late(name, shape, byte):
            return place(name, shape, F32, at_a + byte)[0]

        p_qk = scratch("p_qk", [P, NT, D], 0)
        qkT = scratch("qkT", [P, 2 * 4, SEQ], 0)
        p_v = scratch("p_v", [P, NT, CH], 2)
        y_tok = scratch("y_tok", [P, NT, CH], 6)
        probs = late("probs", [P, 2, 3 * P], 0)
        probsT = late("probsT", [P, 2, 3 * P], 3072)
        e_pc = scratch("e_pc", [P, NT, CH], 0)
        e_cT = scratch("e_cT", [P, 4, SEQ], 0)
        e_pv = scratch("e_pv", [P, NT, CH], 1)
        e_m = scratch("e_m", [P, 4, SEQ], 1)
        e_pu = scratch("e_pu", [P, NT, CH], 2)
        e_pb = scratch("e_pb", [P, NT, CH], 3)
        w_grp = scratch("w_grp", [P, 4, P], 4)
        e_sB = scratch("e_sB", [P, 4, PAD + SEQ], 4.5)
        e_pool = scratch("e_pool", [P, 4, SEQ], 5.75)
        e_y = scratch("e_y", [P, 4, SEQ], 0)
        e_u = late("e_u", [P, 4, PAD + SEQ], 4096)
        e_sA = late("e_sA", [P, 4, PAD + SEQ], 8448)
        e_edge = late("e_edge", [P, 4, PAD], 12800)
        PADT = TAPS - 1
        o_d1 = scratch("o_d1", [P, NT, CH], 3)
        o_d2 = scratch("o_d2", [P, NT, CH], 4)
        o_pad = scratch("o_pad", [P, 4, PADT + SEQ], 3)
        o_acc = scratch("o_acc", [P, 4, SEQ], 5)
        o_z = late("o_z", [P, NT, CH], 6144)
        o_y = late("o_y", [P, NT, 4, P], 10240)
        o_f, _ = place("o_f", [P, 4, NT, GATES], F32, at_s)
        o_cum, _ = place("o_cum", [GATES, SEQ], F32, at_s + 2048)
        g_pqk = scratch("g_pqk", [P, NT, CH], 3)
        g_qkT = scratch("g_qkT", [P, 4, SEQ], 3)
        g_v = scratch("g_v", [P, NT, CH], 4)
        g_r = scratch("g_r", [P, NT, CH], 5)
        g_o = scratch("g_o", [P, NT, CH], 0)
        g_z, _ = place("g_z", [P, 2, SEQ], F32, at_s)
        g_e, _ = place("g_e", [P, 2, SEQ], F32, at_s + 2048)
        g_b, _ = place("g_b", [P, 2, SEQ], F32, at_s + 4096)
        g_low, _ = place("g_low", [P, NT, RANK], F32, at_s + 6144)
        g_lowT, _ = place("g_lowT", [RANK, SEQ], F32, at_s + 6400)
        g_x = late("g_x", [P, 2, 2, SEQ], 6144)
        g_att = late("g_att", [P, 2 * GLA_H, P], 10240)
        g_far = late("g_far", [P, GLA_H, P], 14336)

        ident = const[:, C_IDENT:C_IDENT + P]
        bn = stat[:, 0:24].rearrange("p (t h s) -> p t h s", t=NT, h=2)
        mv = stat[:, 24:28].rearrange("p (t s) -> p t s", t=NT)
        rstd = stat[:, 28:30]
        ssq = stat[:, 30:32]
        ssq2 = stat[:, 32:34]
        rstd2 = stat[:, 34:36]
        minus_half = stat[:, 36:44]
        peak = stat[:, 44:48].rearrange("p (b t) -> p b t", b=2)
        npeak = stat[:, 48:52].rearrange("p (b t) -> p b t", b=2)
        total = stat[:, 52:68].rearrange("p (t h) -> p t h", t=NT)
        share_of = stat[:, 68:84].rearrange("p (t h) -> p t h", t=NT)
        a_ssq = stat[:, 84:86]
        a_rstd = stat[:, 86:88]
        g_ssq = stat[:, 88:96].rearrange("p (t h) -> p t h", t=NT)
        g_rstd = stat[:, 96:104].rearrange("p (t h) -> p t h", t=NT)
        c_bn = stat[:, 104:116].rearrange("p (t s) -> p t s", t=NT)
        c_mv = stat[:, 116:120].rearrange("p (t s) -> p t s", t=NT)
        c_rstd = stat[:, 120:122]

        ps = ctx.enter_context(nc.psum_tensor("ps", [P, 8, CH], F32))
        acc, tb = ps[:, 0:4, :], ps[:, 4:8, :]
        IN_BANK = ((0, 2), (1, 3))
        FFN_BANK = ((0, 2), (6, 7), (1, 3))
        FFN_BUF = (0, 1, 0)

        NA = [len(c) for c in COLS]
        U_A, U_B, U_C, U_D, u = [], [], [], [], 0
        for l in range(len(LAYERS)):
            U_A.append(u)
            U_B.append(U_A[l] + 4 * NA[l])
            U_C.append(U_B[l] + KD)
            U_D.append(U_C[l] + 4 * NC)
            u = U_D[l] + KF
        U_END = u
        ACC0 = [sum(NA[:l]) + (NC + 2) * l for l in range(len(LAYERS))]

        def acc_at(l, phase, c=0):
            return ACC0[l] + {"A": 0, "B": NA[l], "C": NA[l] + 1, "D": NA[l] + 1 + NC}[phase] + c + 1

        def out_at(l, c, t):
            return 2 * sum(NA[:l]) + (2 * t + c if c < 2 else 2 * c + t) + 1

        def glu_at(l, c, t):
            if isinstance(c, int) and c < 2:
                return 2 * NC * l + 2 * t + c + 1
            return c * 2 + (2 * NC * l + t + 1)

        NB = 2 * len(LAYERS)
        is_ln = [LAYERS[k // 2] != "hyb" for k in range(NB)]
        pre = [k + 1 < NB and LAYERS[(k + 1) // 2] == "hyb" for k in range(NB)]

        def sem(name):
            return ctx.enter_context(nc.semaphore(name))

        every = list(range(len(LAYERS)))
        attn = [1, 2, 3]
        hyb = [2, 3]

        def stage(name, per, layers=None):
            return Stage(sem(name), per, every if layers is None else layers)

        raw_in = [sem(f"raw_in{i}") for i in range(N_RAW)]
        x_in = [sem(f"x_in{t}") for t in range(NT)]
        const_in, params_in, rows_in, out_done = sem("const_in"), sem("params_in"), sem("rows_in"), sem("out_done")
        w_high, w_low, w_used = sem("w_high"), sem("w_low"), sem("w_used")
        acc_done = sem("acc_done")
        a_out = sem("a_out")
        silu_done, glu_done = sem("silu_done"), sem("glu_done")
        h_turned, h_high, h_low = stage("h_turned", NC), stage("h_high", NC), stage("h_low", NC)
        bounds = list(range(NB))
        x_turned, x_high, x_low = (stage(n, 4, bounds) for n in ("x_turned", "x_high", "x_low"))
        acc_read = stage("acc_read", NT, bounds)
        spread = stage("spread", NT, [k for k in bounds if is_ln[k]])
        squared = stage("squared", NT, [k for k in bounds if not is_ln[k]])
        scaled = stage("scaled", NT, bounds)
        spread2 = stage("spread2", NT, [k for k in bounds if pre[k]])
        scaled2 = stage("scaled2", NT, [k for k in bounds if pre[k]])
        x_sum = stage("x_sum", NT, [k for k in bounds if pre[k]])
        x_ready = stage("x_ready", NT, bounds)
        act_step, dve_step, pool_step = sem("act_step"), sem("dve_step"), sem("pool_step")
        set_up, tiny_high, params_turned, params_out = sem("set_up"), sem("tiny_high"), sem("params_turned"), sem("params_out")
        tiny_done = sem("tiny_done")
        e_turned, e_act, e_dve = stage("e_turned", 10, [0]), stage("e_act", 4, [0]), stage("e_dve", 4, [0])
        e_pooled, e_high, e_low = stage("e_pooled", 1, [0]), stage("e_high", 6, [0]), stage("e_low", 6, [0])
        o_gated, o_turned, o_padded = stage("o_gated", 1, [1]), stage("o_turned", 2, [1]), stage("o_padded", 2, [1])
        o_fsum, o_fbiased, o_flog, o_fcum, o_cumT = (stage(n, 1, [1]) for n in ("o_fsum", "o_fbiased", "o_flog", "o_fcum", "o_cumT"))
        o_soft = stage("o_soft", 1, [1])
        o_conv, o_back, o_spread, o_scaled = stage("o_conv", 1, [1]), stage("o_back", NT, [1]), stage("o_spread", NT, [1]), stage("o_scaled", NT, [1])
        o_normed, o_silu = stage("o_normed", NT, [1]), stage("o_silu", NT, [1])
        roped = stage("roped", 1, hyb)
        qk_turned, q_out, k_out = stage("qk_turned", 4, attn), stage("q_out", 2, attn), stage("k_out", 2, attn)
        logits, peaks, weighed = stage("logits", HEADS, attn), stage("peaks", HEADS, attn), stage("weighed", HEADS, attn)
        p_turned, p_out, attended = stage("p_turned", HEADS, attn), stage("p_out", HEADS, attn), stage("attended", HEADS, attn)
        shared = stage("shared", NT, attn)
        a_spread, a_scaled, a_normed = (stage(n, NT, hyb) for n in ("a_spread", "a_scaled", "a_normed"))
        y_turned, y_high, y_low = stage("y_turned", 4, attn), stage("y_high", 4, attn), stage("y_low", 4, attn)
        l_sum, l_out, l_turned, l_outT, z_done, z_out, z_log, decay = (
            stage(n, 1, hyb) for n in ("l_sum", "l_out", "l_turned", "l_outT", "z_done", "z_out", "z_log", "decay"))
        gqk_turned, gqk_out = stage("gqk_turned", 2, hyb), stage("gqk_out", 2, hyb)
        NL = len(LEVELS)
        g_diff, g_exp, g_scaled = (stage(n, NL, hyb) for n in ("g_diff", "g_exp", "g_scaled"))
        g_pair, g_kept = stage("g_pair", NL + 1, hyb), stage("g_kept", NL + 1, hyb)
        g_done, g_spread, g_rooted, g_normed = stage("g_done", NT, hyb), stage("g_spread", 1, hyb), stage("g_rooted", 1, hyb), stage("g_normed", NT, hyb)

        def w_in(l):
            return a["ev_w_in"][0] if l == 0 else a["od_w_in"][0] if l == 1 else a["w_in_2"][l - 2]

        def w_out(l):
            return a["ev_w_out"][0] if l == 0 else a["od_w_out"][0] if l == 1 else a["w_out_2"][l - 2]

        def w_ffn(l):
            if l < 2:
                both = a["ffn_w_in"][l].rearrange("(k p) (h c n) -> h p k c n", p=P, h=2, n=FC)
                return both[0], both[1]
            return tuple(a[n][l - 2].rearrange("(k p) (c n) -> p k c n", p=P, n=FC) for n in ("w_gate_2", "w_up_2"))

        def w_down(l):
            return a["ffn_w_out"][l] if l < 2 else a["w_down_2"][l - 2]

        def norm_rows(k):
            l, ffn = divmod(k, 2)
            if is_ln[k]:
                g, b = ("ln_ffn_g", "ln_ffn_b") if ffn else ("ln_mix_g", "ln_mix_b")
                r = [(0, 0, a[g][l]), (1, 0, a[b][l])]
                if pre[k]:
                    r.append((2, 0, a["mix_pre_norm_2"][0]))
                return r
            j = l - 2
            r = [(0, 0, a["ffn_post_norm_2" if ffn else "mix_post_norm_2"][j])]
            if pre[k]:
                r.append((1, 0, a["mix_pre_norm_2"][j + 1] if ffn else a["ffn_pre_norm_2"][j]))
            if not ffn:
                r += [(2, 0, a["attn_out_norm_2"][j]), (2, HALF, a["gla_out_norm_2"][j])]
            return r

        def rows_at(k):
            return 16 * sum(len(norm_rows(i)) for i in range(k + 1))

        def pre_row(k):
            return rows[:, 2 if is_ln[k] else 1, :]

        def heads(ap, n):
            return ap.rearrange("p (h d) -> p h d", h=n)

        def level_view(ap, m):
            return ap.rearrange("p b (j s m) -> p (b j) s m", s=2, m=m)

        def tile_done(eng, t, l, phase, c=0):
            if t == 0:
                eng.wait_ge(acc_done, acc_at(l, phase, c))
            else:
                last = {"A": U_A[l] + 3, "B": U_B[l] + KD - 1, "C": U_C[l] + 3, "D": U_D[l] + KF - 1}[phase]
                eng.wait_ge(w_used, c * 4 + (last + 1) if phase in "AC" else last + 1)

        def level_rows(h):
            return slice(GLA_DK * (h % 2), GLA_DK * (h % 2 + 1)), h // 2

        def kept_at(h, t):
            return 4 * (h % 2) + 2 * (h // 2) + t

        def far_at(h):
            return 2 * (h % 2) + h // 2

        block = ctx.enter_context(nc.Block())

        @block.sync
        def _(sp):
            def load(v, left, right, split):
                if not v.first:
                    sp.wait_ge(w_low, v.n - N_RAW + 1)
                dst = raw[:, v.raw, :].rearrange("p (i h n) -> p i h n", i=2, h=2) if split else raw[:, v.raw, :]
                sp.dma_start(dst[:, :, 0, :] if split else dst[:, 0:CH], left).then_inc(raw_in[v.raw], 16)
                sp.dma_start(dst[:, :, 1, :] if split else dst[:, CH:2 * CH], right).then_inc(raw_in[v.raw], 16)

            def ffn_chunk(l, c, j, unit0):
                gate, up = w_ffn(l)
                for q in range(4):
                    k = slice(2 * q, 2 * q + 2)
                    load(Unit(unit0 + q, j), gate[:, k, c, :], up[:, k, c, :], True)

            for t in range(NT):
                sp.dma_start(x[:, t, :], a["x"][0, P * t:P * (t + 1), :]).then_inc(x_in[t], 16)
            sp.dma_start(const[:], a["shape_consts"]).then_inc(const_in, 16)
            for l in every:
                win = w_in(l).rearrange("(k p) n -> k p n", p=P)
                for c, col in enumerate(COLS[l]):
                    for q in range(4):
                        load(Unit(U_A[l] + 4 * c + q), win[2 * q, :, col:col + CH], win[2 * q + 1, :, col:col + CH], False)
                wo = w_out(l).rearrange("(k p) n -> k p n", p=P)
                for k in range(KD):
                    load(Unit(U_B[l] + k), wo[k, :, 0:CH], wo[k, :, CH:D], False)
                for c in range(2):
                    ffn_chunk(l, c, 0, U_C[l] + 4 * c)
                with sp.Fori(0, (NC - 2) // LOOP) as j:
                    for r in range(LOOP):
                        ffn_chunk(l, j * LOOP + (2 + r), j, U_C[l] + 4 * (2 + r))
                wd = w_down(l).rearrange("(k p) n -> k p n", p=P)
                for k in range(KF):
                    load(Unit(U_D[l] + k), wd[k, :, 0:CH], wd[k, :, CH:D], False)
            for t in range(NT):
                sp.wait_ge(x_ready.sem, x_ready.at(NB - 1, t))
                sp.dma_start(out[0, P * t:P * (t + 1), :], x[:, t, :]).then_inc(out_done, 16)
            sp.wait_ge(out_done, 16 * NT)

        @block.tensor
        def _(pe):
            def three_passes(bank, hi, lo, v, part, first, last):
                wh, wl = w_hi[:, v.slot, part], w_lo[:, v.slot, part]
                nc.tensor.matmul(ps[:, bank, :], hi, wh, start=first, stop=False)
                nc.tensor.matmul(ps[:, bank, :], hi, wl, start=False, stop=False)
                return nc.tensor.matmul(ps[:, bank, :], lo, wh, start=False, stop=last)

            def in_unit(v, q, bank, t):
                tok = slice(P * t, P * (t + 1))
                for i in range(2):
                    k = 2 * q + i
                    mm = three_passes(bank, a_hi[:, k, tok], a_lo[:, k, tok], v,
                                      slice(CH * i, CH * (i + 1)), k == 0, k == KD - 1)
                return mm

            def out_unit(v, k, kn, hi, lo, t):
                for h in range(2):
                    mm = three_passes(2 * t + h, hi, lo, v, slice(CH * h, CH * (h + 1)), k == 0, k == kn - 1)
                return mm

            def joint_chunk(units, c, banks, free_bank, hook):
                for t in range(NT):
                    free_bank(c, t)
                for q, v in enumerate(units):
                    pe.wait_ge(w_low, v.n + 1)
                    mm = in_unit(v, q, banks[0], 0)
                    if q == 3:
                        mm.then_inc(acc_done, 1)
                    in_unit(v, q, banks[1], 1).then_inc(w_used, 1)
                    if q == 1:
                        hook(c)

            def first_chunks(l, phase, u0, banks, free_bank, hook):
                kk = 2 * l + (phase == "C")
                for t in range(NT):
                    pe.wait_ge(x_low.sem, x_low.at(kk, 2 * t + 1))
                    for c in range(2):
                        free_bank(c, t)
                        for q in range(4):
                            v = Unit(u0 + 4 * c + q)
                            pe.wait_ge(w_low, v.n + 1)
                            mm = in_unit(v, q, banks[c][t], t)
                            if t == 1:
                                mm.then_inc(w_used, 1)
                            elif q == 3:
                                mm.then_inc(acc_done, 1)
                            if t == 0 and c == 1 and q == 2 and kk > 0:
                                turn_x(kk, 1)
                            if t == 1 and q == 1:
                                hook(c)

            def summed(u0, kn, hi, lo, lo0, kk, ready):
                joint = kn - KD
                for k in range(joint):
                    v = Unit(u0 + k)
                    pe.wait_ge(w_low, v.n + 1)
                    ready(k)
                    for t in range(NT):
                        tok = slice(P * t, P * (t + 1))
                        mm = out_unit(v, k, kn, hi[:, k, tok], lo[:, lo0 + k, tok], t)
                    mm.then_inc(w_used, 1)
                for t in range(NT):
                    tok = slice(P * t, P * (t + 1))
                    for k in range(joint, kn):
                        v = Unit(u0 + k)
                        pe.wait_ge(w_low, v.n + 1)
                        ready(k)
                        mm = out_unit(v, k, kn, hi[:, k, tok], lo[:, lo0 + k, tok], t)
                        if t == 1:
                            mm.then_inc(w_used, 1)
                        elif k == kn - 1:
                            mm.then_inc(acc_done, 1)
                        if t == 1 and k == kn - 2 and kk < NB:
                            turn_x(kk, 0)

            def turn_x(kk, t):
                if kk == 0:
                    pe.wait_ge(x_in[t], 16)
                    pe.wait_ge(const_in, 16)
                else:
                    pe.wait_ge(x_ready.sem, x_ready.at(kk - 1, t))
                src = nbuf[:, :] if kk > 0 and pre[kk - 1] else x[:, t, :]
                for h in range(2):
                    for b in range(4):
                        tr = nc.tensor.transpose(tb[:, h, P * b:P * (b + 1)],
                                                 src[:, CH * h + P * b:CH * h + P * (b + 1)], ident)
                    tr.then_inc(x_turned.sem, 1)

            def turn_blocks(bank, src, col, st):
                for b in range(2):
                    for t in range(NT):
                        tr = nc.tensor.transpose(tb[:, bank, SEQ * b + P * t:SEQ * b + P * (t + 1)],
                                                 src[:, t, col + P * b:col + P * (b + 1)], ident)
                tr.then_inc(st.sem, 1)

            def turn_tile(bank, src, st):
                for b in range(4):
                    tr = nc.tensor.transpose(tb[:, bank, P * b:P * (b + 1)], src[:, P * b:P * (b + 1)], ident)
                tr.then_inc(st.sem, 1)

            def tiny(l, bank, st):
                c0, w = TINY[l]
                pe.wait_ge(tiny_done, 1)
                for t in range(NT):
                    tok = slice(P * t, P * (t + 1))
                    o = tb[:, bank, w * t:w * (t + 1)]
                    for k in range(KD):
                        wh, wl = tiny_hi[:, k, c0:c0 + w], tiny_lo[:, k, c0:c0 + w]
                        nc.tensor.matmul(o, a_hi[:, k, tok], wh, start=(k == 0), stop=False)
                        nc.tensor.matmul(o, a_hi[:, k, tok], wl, start=False, stop=False)
                        mm = nc.tensor.matmul(o, a_lo[:, k, tok], wh, start=False, stop=(k == KD - 1))
                mm.then_inc(st.sem, 1)

            def even_hook(c):
                if c == 3:
                    pe.wait_ge(a_out, out_at(0, 1, 1))
                    for i in range(2):
                        turn_blocks(i, e_pc, 2 * P * i, e_turned)
                    for i in range(2):
                        turn_blocks(2 + i, e_pv, 2 * P * i, e_turned)

            def even_rest():
                for i in range(2):
                    pe.wait_ge(a_out, out_at(0, 2, 1))
                    pe.wait_ge(e_act.sem, e_act.at(0, i))
                    turn_blocks(i, e_pu, 2 * P * i, e_turned)
                for i in range(2):
                    pe.wait_ge(a_out, out_at(0, 3, 1))
                    pe.wait_ge(e_dve.sem, e_dve.at(0, i))
                    turn_blocks(2 + i, e_pb, 2 * P * i, e_turned)
                pe.wait_ge(e_pooled.sem, e_pooled.at(0, 0))
                pe.wait_ge(e_act.sem, e_act.at(0, 3))
                pe.wait_ge(params_in, PARAMS)
                for i in range(2):
                    for g in range(2 * i, 2 * i + 2):
                        mm = nc.tensor.matmul(tb[:, i, SEQ * (g % 2):SEQ * (g % 2 + 1)], w_grp[:, g, :], e_pool[:, g, :],
                                              start=True, stop=True)
                    mm.then_inc(e_turned.sem, 1)

            def odd_hook(c):
                if c == 2:
                    pe.wait_ge(o_gated.sem, o_gated.at(1, 0))
                    for i in range(2):
                        turn_blocks(i, o_d1, 2 * P * i, o_turned)
                if c == 3:
                    tiny(1, 2, o_fsum)
                if c == 4:
                    pe.wait_ge(o_flog.sem, o_flog.at(1, 0))
                    tri = const[:, C_TRI:C_TRI + P]
                    nc.tensor.matmul(tb[0:GATES, 3, 0:SEQ], o_f[:, 0, 0, :], const[:, C_TRI:C_TRI + SEQ], start=True, stop=False)
                    nc.tensor.matmul(tb[0:GATES, 3, P:SEQ], o_f[:, 0, 1, :], tri, start=False, stop=True).then_inc(o_fcum.sem, 1)

            def odd_rest():
                for i in range(2):
                    pe.wait_ge(o_padded.sem, o_padded.at(1, i))
                pe.wait_ge(o_cumT.sem, o_cumT.at(1, 0))
                pe.wait_ge(a_out, out_at(1, 3, 1))
                turn_qk(1)
                attention(1, None)
                turn_y(1, shared)
                pe.wait_ge(o_conv.sem, o_conv.at(1, 0))
                for t in range(NT):
                    for b in range(4):
                        tr = nc.tensor.transpose(tb[:, 2 + t, P * b:P * (b + 1)], o_acc[:, b, P * t:P * (t + 1)], ident)
                    tr.then_inc(o_back.sem, 1)
                for t in range(NT):
                    pe.wait_ge(o_normed.sem, o_normed.at(1, t))
                    pe.wait_ge(y_low.sem, y_low.at(1, t))
                    turn_tile(t, o_z[:, t, :], y_turned)

            def hyb_hook(l):
                def hook(c):
                    if c == 1:
                        tiny(l, 0, l_sum)
                    if c == 2:
                        pe.wait_ge(l_out.sem, l_out.at(l, 0))
                        for t in range(NT):
                            tr = nc.tensor.transpose(tb[0:RANK, 1, P * t:P * (t + 1)], g_low[:, t, :], ident)
                        tr.then_inc(l_turned.sem, 1)
                    if c == 3:
                        pe.wait_ge(l_outT.sem, l_outT.at(l, 0))
                        for b in range(2):
                            mm = nc.tensor.matmul(tb[:, 2, SEQ * b:SEQ * (b + 1)], w_up[:, l - 2, P * b:P * (b + 1)], g_lowT[:, :],
                                                  start=True, stop=True)
                        mm.then_inc(z_done.sem, 1)
                        pe.wait_ge(a_out, out_at(l, 0, 1))
                        for i in range(2):
                            turn_blocks(i, g_pqk, 2 * P * i, gqk_turned)
                    if c == 4:
                        pe.wait_ge(gqk_out.sem, gqk_out.at(l, 1))
                        pe.wait_ge(z_out.sem, z_out.at(l, 0))
                        pe.wait_ge(roped.sem, roped.at(l, 0))
                        turn_qk(l)
                return hook

            def level(l, n):
                if n:
                    pe.wait_ge(g_scaled.sem, g_scaled.at(l, n - 1))
                    pe.wait_ge(g_kept.sem, g_kept.at(l, n - 1))
                for h in range(GLA_H):
                    r, b = level_rows(h)
                    for t in range(1 if n == 1 else NT):
                        tok = slice(P * t, P * (t + 1))
                        if n == 0:
                            ks, qs = g_qkT[r, 2 + b, tok], g_qkT[r, b, tok]
                        elif n == 1:
                            ks, qs = g_x[r, 1, b, 0:P], g_x[r, 1, b, P:SEQ]
                        else:
                            ks = qs = g_x[r, n % 2, b, tok]
                        at = far_at(h) % 2 if n == 1 else kept_at(h, t) % 4
                        mm = nc.tensor.matmul(acc[:, 1 + 2 * (h % 2), P * at:P * (at + 1)], ks, qs, start=True, stop=True)
                mm.then_inc(g_pair.sem, 1)

            def hyb_rest(l):
                for c in range(4, NA[l]):
                    pe.wait_ge(a_out, out_at(l, c, 1))
                level(l, 0)
                attention(l, level)
                pe.wait_ge(g_kept.sem, g_kept.at(l, NL))
                for t in range(NT):
                    for h in range(GLA_H):
                        cols = slice(GLA_DV * h, GLA_DV * (h + 1))
                        if t == 1:
                            nc.tensor.matmul(acc[:, 3, cols], g_far[:, far_at(h), :], g_v[:, 0, cols], start=True, stop=False)
                        mm = nc.tensor.matmul(acc[:, 1 + 2 * t, cols], g_att[:, kept_at(h, t), :], g_v[:, t, cols],
                                              start=(t == 0), stop=True)
                    mm.then_inc(g_done.sem, 1)
                turn_y(l, a_normed)
                for t in range(NT):
                    pe.wait_ge(g_normed.sem, g_normed.at(l, t))
                    turn_tile(2 + t, g_o[:, t, :], y_turned)

            def turn_qk(l):
                for i in range(4):
                    turn_blocks(i, p_qk, 2 * P * i, qk_turned)

            def head_logits(l, h):
                bank, r, b = h % 2, slice(HD * (h % 2), HD * (h % 2 + 1)), h // 2
                if h >= 2:
                    pe.wait_ge(weighed.sem, weighed.at(l, h - 2))
                near, wide, late_half = tb[:, bank, 0:P], tb[:, bank, P:3 * P], tb[:, bank, 2 * P:3 * P]
                if l == 1:
                    one_hot = ident[0:GATES, h:h + 1].broadcast_to([GATES, P])
                    causal = const[:, C_CAUSAL:C_CAUSAL + P]
                    nc.tensor.matmul(near, ident, causal, start=True, stop=False)
                    nc.tensor.matmul(near, one_hot, o_cum[:, 0:P], start=False, stop=False)
                else:
                    nc.tensor.matmul(near, ident, const[:, C_DIL:C_DIL + P], start=True, stop=False)
                nc.tensor.matmul(near, qkT[r, b, 0:P], qkT[r, 4 + b, 0:P], start=False, stop=True)
                if l == 1:
                    nc.tensor.matmul(wide, one_hot, o_cum[:, :], start=True, stop=False)
                    nc.tensor.matmul(late_half, ident, causal, start=False, stop=False)
                else:
                    nc.tensor.matmul(wide, ident, const[:, C_DIL + P:C_DIL + 3 * P], start=True, stop=False)
                nc.tensor.matmul(wide, qkT[r, b, P:SEQ], qkT[r, 4 + b, :], start=False, stop=True).then_inc(logits.sem, 1)

            def head_turn(l, h):
                pe.wait_ge(weighed.sem, weighed.at(l, h))
                if h >= 2:
                    pe.wait_ge(p_out.sem, p_out.at(l, h - 2))
                for i in range(3):
                    tr = nc.tensor.transpose(tb[:, 2 + h % 2, P * i:P * (i + 1)], probs[:, h % 2, P * i:P * (i + 1)], ident)
                tr.then_inc(p_turned.sem, 1)

            def head_values(l, h):
                pe.wait_ge(p_out.sem, p_out.at(l, h))
                cols = slice(HD * h, HD * (h + 1))
                pT = probsT[:, h % 2, :]
                nc.tensor.matmul(acc[:, 0, cols], pT[:, 0:P], p_v[:, 0, cols], start=True, stop=True)
                nc.tensor.matmul(acc[:, 2, cols], pT[:, P:2 * P], p_v[:, 0, cols], start=True, stop=False)
                nc.tensor.matmul(acc[:, 2, cols], pT[:, 2 * P:3 * P], p_v[:, 1, cols], start=False,
                                 stop=True).then_inc(attended.sem, 1)

            def attention(l, level):
                pe.wait_ge(a_out, out_at(l, NA[l] - 1, 1))
                pe.wait_ge(q_out.sem, q_out.at(l, 1))
                pe.wait_ge(k_out.sem, k_out.at(l, 1))
                head_logits(l, 0)
                head_logits(l, 1)
                for h in range(HEADS):
                    head_turn(l, h)
                    if h + 2 < HEADS:
                        head_logits(l, h + 2)
                    if level:
                        level(l, h + 1)
                    head_values(l, h)

            def turn_y(l, ready):
                for t in range(NT):
                    pe.wait_ge(ready.sem, ready.at(l, t))
                    turn_tile(t, y_tok[:, t, :], y_turned)

            def turn_ffn(l, c, buf):
                pe.wait_ge(glu_done, glu_at(l, c, 1))
                if not isinstance(c, int) or c > 0:
                    pe.wait_ge(h_low.sem, c + h_low.at(l, 0) - 1)
                for b in range(2):
                    for t in range(NT):
                        tr = nc.tensor.transpose(tb[:, 0, SEQ * b + P * t:SEQ * b + P * (t + 1)],
                                                 glu[:, buf, t, P * b:P * (b + 1)], ident)
                tr.then_inc(h_turned.sem, 1)

            turn_x(0, 0)
            pe.wait_ge(x_low.sem, x_low.at(0, 1))
            turn_x(0, 1)
            pe.wait_ge(params_in, PARAMS)
            pe.wait_ge(x_low.sem, x_low.at(0, 2))
            for b in range(4):
                tr = nc.tensor.transpose(tb[:, 0, N_ROWS * b:N_ROWS * (b + 1)], prow[:, P * b:P * (b + 1)], ident[0:N_ROWS, 0:N_ROWS])
            tr.then_inc(params_turned, 1)

            for l in every:
                hook = {"even": even_hook, "odd": odd_hook, "hyb": hyb_hook(l)}[LAYERS[l]]

                def free_in(c, t):
                    if c >= 2:
                        pe.wait_ge(a_out, out_at(l, c - 2, t))
                    elif l > 0:
                        pe.wait_ge(acc_read.sem, acc_read.at(2 * l - 1, t))

                first_chunks(l, "A", U_A[l], IN_BANK, free_in, hook)
                for c in range(2, NA[l]):
                    joint_chunk([Unit(U_A[l] + 4 * c + q) for q in range(4)], c, IN_BANK[c % 2], free_in, hook)
                if LAYERS[l] == "even":
                    even_rest()
                    pe.wait_ge(e_low.sem, e_low.at(l, 5))
                elif LAYERS[l] == "odd":
                    odd_rest()
                    pe.wait_ge(y_low.sem, y_low.at(l, 3))
                else:
                    hyb_rest(l)
                    pe.wait_ge(y_low.sem, y_low.at(l, 3))
                summed(U_B[l], KD, h_hi, h_lo, Y_LO, 2 * l + 1, lambda k: None)

                def free_ffn(c, t):
                    if isinstance(c, int):
                        pe.wait_ge(acc_read.sem, acc_read.at(2 * l, t))
                    else:
                        pe.wait_ge(glu_done, c * 2 + (2 * NC * l + t - 3))

                first_chunks(l, "C", U_C[l], FFN_BANK, free_ffn, lambda c: turn_ffn(l, 0, 0) if c == 1 else None)
                with pe.Fori(0, (NC - 2) // LOOP) as j:
                    for r in range(LOOP):
                        units = [Unit(U_C[l] + 4 * (2 + r) + q, j) for q in range(4)]
                        before = FFN_BUF[(1 + r) % LOOP]
                        joint_chunk(units, j * LOOP + (2 + r), FFN_BANK[(2 + r) % LOOP], free_ffn,
                                    lambda c: turn_ffn(l, j * LOOP + (1 + r), before))

                def ffn_ready(k):
                    if k == 0:
                        pe.wait_ge(glu_done, glu_at(l, NC - 2, 1))
                    if k == 2:
                        turn_ffn(l, NC - 1, FFN_BUF[(NC - 1) % LOOP])
                    if k % 2 == 0:
                        pe.wait_ge(h_low.sem, h_low.at(l, k // 2))

                summed(U_D[l], KF, h_hi, h_lo, 0, 2 * l + 2, ffn_ready)

        @block.scalar
        def _(act):
            chain = Chain(act, act_step)
            fed = [0]

            def high(v):
                act.wait_ge(raw_in[v.raw], v.loads * 32)
                if not v.fresh:
                    act.wait_ge(w_used, v.n - N_W + 1)
                nc.scalar.activation(w_hi[:, v.slot, :], raw[:, v.raw, :], ACT.Copy).then_inc(w_high, 1)

            def feed(n):
                for u in range(fed[0], min(n, U_END)):
                    high(Unit(u))
                fed[0] = max(fed[0], min(n, U_END))

            def x_split(kk, t):
                for h in range(2):
                    act.wait_ge(x_turned.sem, x_turned.at(kk, 2 * t + h))
                    nc.scalar.activation(a_hi[:, 4 * h:4 * h + 4, P * t:P * (t + 1)],
                                         tb[:, h, :].rearrange("p (b n) -> p b n", b=4), ACT.Copy).then_inc(x_high.sem, 1)

            def load_rows(k):
                if k >= NB:
                    return
                if k:
                    act.wait_ge(x_ready.sem, x_ready.at(k - 1, 1))
                for slot, col, row in norm_rows(k):
                    act.dma_start(rows[:, slot, col:col + row.shape[0]], row.partition_broadcast(P)).then_inc(rows_in, 16)

            def boundary(k, t):
                l, ffn = divmod(k, 2)
                def settle(before):
                    if pre[k]:
                        act.wait_ge(spread2.sem, spread2.at(k, before))
                    elif not is_ln[k]:
                        act.wait_ge(squared.sem, squared.at(k, before))

                if t == 1:
                    settle(0)
                if not is_ln[k]:
                    tile_done(act, t, l, "D" if ffn else "B")
                    nc.scalar.activation(squares[:, :], acc[:, 2 * t:2 * t + 2, :].rearrange("p h n -> p (h n)"), ACT.Square,
                                         accum_out=ssq[:, t:t + 1]).then_inc(squared.sem, 1)
                if pre[k]:
                    act.wait_ge(x_sum.sem, x_sum.at(k, t))
                    if not is_ln[k]:
                        act.wait_ge(squared.sem, squared.at(k, t))
                    nc.scalar.activation(squares[:, :], x[:, t, :], ACT.Square,
                                         accum_out=ssq2[:, t:t + 1]).then_inc(spread2.sem, 1)
                if t == 1:
                    settle(1)

            def after_boundary(k, end):
                boundary(k, 0)
                feed(end + 4)
                if k + 1 < NB:
                    x_split(k + 1, 0)
                feed(end + 8)
                boundary(k, 1)

            def chunk_out(l, c, t):
                tile_done(act, t, l, "A", c)
                bank, f = acc[:, IN_BANK[c % 2][t], :], ACT.Copy
                if l == 0:
                    dst = (e_pc, e_pv, e_pu, e_pb)[c][:, t, :]
                elif l == 1:
                    dst = (o_d1[:, t, :], o_d2[:, t, :], p_qk[:, t, 0:CH], p_qk[:, t, CH:D], p_v[:, t, :])[c]
                    f = ACT.Sigmoid if c == 1 else f
                else:
                    dst = (g_pqk[:, t, :], p_qk[:, t, 0:CH], p_qk[:, t, CH:D], p_v[:, t, :], g_v[:, t, :], g_r[:, t, :])[c]
                    f = ACT.Silu if c == 5 else f
                nc.scalar.activation(dst, bank, f).then_inc(a_out, 1)

            def blocks(bank):
                return tb[:, bank, :].rearrange("p (b n) -> p b n", b=2)

            def even_rest():
                act.wait_ge(e_turned.sem, e_turned.at(0, 1))
                for i in range(2):
                    nc.scalar.activation(e_cT[:, 2 * i:2 * i + 2, :], blocks(i), ACT.Copy).then_inc(e_act.sem, 1)
                for i in range(2):
                    act.wait_ge(e_turned.sem, e_turned.at(0, 4 + i))
                    nc.scalar.activation(e_u[:, 2 * i:2 * i + 2, PAD:], blocks(i), ACT.Copy).then_inc(e_act.sem, 1)
                for i in range(2):
                    act.wait_ge(e_dve.sem, e_dve.at(0, 2 + i))
                    nc.scalar.activation(h_hi[:, 2 * i:2 * i + 2, :], e_y[:, 2 * i:2 * i + 2, :], ACT.Copy).then_inc(e_high.sem, 1)
                for g in range(4):
                    act.wait_ge(e_turned.sem, e_turned.at(0, 8 + g // 2))
                    nc.scalar.activation(h_hi[:, 4 + g, :], tb[:, g // 2, SEQ * (g % 2):SEQ * (g % 2 + 1)], ACT.Copy,
                                         scale=pcol[:, g, R_PSCALE:R_PSCALE + 1]).then_inc(e_high.sem, 1)

            def odd_step(c):
                if c == 2:
                    act.wait_ge(o_turned.sem, o_turned.at(1, 1))
                    for i in range(2):
                        nc.scalar.activation(o_pad[:, 2 * i:2 * i + 2, PADT:], blocks(i), ACT.Copy).then_inc(o_padded.sem, 1)
                if c == 3:
                    log_sigmoid_part(o_f[:, 0], o_f[:, 1], o_f[:, 2], o_f[:, 3], o_fbiased, o_soft, 1)
                if c == 4:
                    act.wait_ge(o_fcum.sem, o_fcum.at(1, 0))
                    nc.scalar.activation(o_cum[:, :], tb[0:GATES, 3, 0:SEQ], ACT.Copy, scale=-1.0 / SCALE).then_inc(o_cumT.sem, 1)

            def log_sigmoid_part(z, z_abs, e, soft, ready, done, l):
                act.wait_ge(ready.sem, ready.at(l, 0))
                chain.step(nc.scalar.activation(z_abs, z, ACT.Abs))
                chain.settle()
                chain.step(nc.scalar.activation(e, z_abs, ACT.Exp, scale=-1.0))
                chain.settle()
                nc.scalar.activation(soft, e, ACT.Ln, bias=1.0).then_inc(done.sem, 1)

            def odd_rest():
                attention(1, None)
                split_y(1, (0, 1))
                for t in range(NT):
                    act.wait_ge(y_turned.sem, y_turned.at(1, 2 + t))
                    for b in range(4):
                        ins = nc.scalar.activation(o_y[:, t, b, :], tb[:, t, P * b:P * (b + 1)], ACT.Silu,
                                                   scale=pcol[:, b, R_CNG:R_CNG + 1], bias=pcol[:, b, R_CNB:R_CNB + 1])
                        n = chain.step(ins) if b < 3 else None
                    ins.then_inc(o_silu.sem, 1)
                for t in range(NT):
                    chain.settle()
                    act.wait_ge(o_silu.sem, o_silu.at(1, t))
                    nc.scalar.activation(h_hi[:, 4:8, P * t:P * (t + 1)], o_y[:, t, :, :], ACT.Copy).then_inc(y_high.sem, 1)

            def hyb_step(l, c):
                if c == 1:
                    act.wait_ge(l_sum.sem, l_sum.at(l, 0))
                    nc.scalar.activation(g_low[:, :, :], tb[:, 0, 0:NT * RANK].rearrange("p (t r) -> p t r", t=NT),
                                         ACT.Copy).then_inc(l_out.sem, 1)
                if c == 2:
                    act.wait_ge(l_turned.sem, l_turned.at(l, 0))
                    nc.scalar.activation(g_lowT[:, :], tb[0:RANK, 1, 0:SEQ], ACT.Copy).then_inc(l_outT.sem, 1)
                if c == 3:
                    act.wait_ge(z_done.sem, z_done.at(l, 0))
                    for b in range(2):
                        col = 2 * (l - 2) + b
                        ins = nc.scalar.activation(g_z[:, b, :], tb[:, 2, SEQ * b:SEQ * (b + 1)], ACT.Identity,
                                                   bias=pcol[:, col, R_GLAB:R_GLAB + 1])
                        if b == 0:
                            chain.step(ins)
                    ins.then_inc(z_out.sem, 1)
                    for i in range(2):
                        act.wait_ge(gqk_turned.sem, gqk_turned.at(l, 1))
                        nc.scalar.activation(g_qkT[:, 2 * i:2 * i + 2, :], blocks(i), ACT.Copy,
                                             scale=GLA_SCALE if i == 0 else 1.0).then_inc(gqk_out.sem, 1)
                    chain.settle()
                    log_sigmoid_part(g_z[:, :, :], g_e[:, :, :], g_b[:, :, :], g_e[:, :, :], z_out, z_log, l)

            def level_decay(l, n):
                act.wait_ge(g_diff.sem, g_diff.at(l, n))
                if n:
                    act.wait_ge(g_scaled.sem, g_scaled.at(l, n - 1))
                nc.scalar.activation(g_e[:, :, :], g_z[:, :, :], ACT.Exp, scale=1.0 / GLA_TAU).then_inc(g_exp.sem, 1)

            def hyb_rest(l):
                attention(l, level_decay)
                for t in range(NT):
                    act.wait_ge(shared.sem, shared.at(l, t))
                    nc.scalar.activation(nbuf[:, 0:CH], y_tok[:, t, :], ACT.Square, accum_out=a_ssq[:, t:t + 1]).then_inc(a_spread.sem, 1)
                    act.wait_ge(a_spread.sem, a_spread.at(l, t))
                for t in range(NT):
                    act.wait_ge(g_done.sem, g_done.at(l, t))
                    for h in range(GLA_H):
                        ins = nc.scalar.activation(nbuf[:, CH + P * h:CH + P * (h + 1)] if t == 0 else nbuf[:, P * h:P * (h + 1)],
                                                   acc[:, 1 + 2 * t, GLA_DV * h:GLA_DV * (h + 1)], ACT.Square,
                                                   accum_out=g_ssq[:, t, h:h + 1])
                ins.then_inc(g_spread.sem, 1)
                split_y(l, (0, 1, 2, 3))

            def attention(l, decay_of):
                act.wait_ge(qk_turned.sem, qk_turned.at(l, 3))
                for i in range(2):
                    nc.scalar.activation(qkT[:, 2 * i:2 * i + 2, :], blocks(i), ACT.Copy).then_inc(q_out.sem, 1)
                for h in range(HEADS):
                    if decay_of:
                        decay_of(l, h)
                    bank = tb[:, h % 2, :]
                    act.wait_ge(peaks.sem, peaks.at(l, h))
                    if h >= 2:
                        act.wait_ge(p_turned.sem, p_turned.at(l, h - 2))
                    nc.scalar.activation(probs[:, h % 2, 0:P], bank[:, 0:P], ACT.Exp, scale=SCALE,
                                         bias=npeak[:, h % 2, 0:1], accum_out=total[:, 0, h:h + 1])
                    nc.scalar.activation(probs[:, h % 2, P:3 * P], bank[:, P:3 * P], ACT.Exp, scale=SCALE,
                                         bias=npeak[:, h % 2, 1:2], accum_out=total[:, 1, h:h + 1]).then_inc(weighed.sem, 1)

            def split_y(l, which):
                for i in which:
                    b, t = 4 * (i // 2), i % 2
                    act.wait_ge(y_turned.sem, y_turned.at(l, i))
                    nc.scalar.activation(h_hi[:, b:b + 4, P * t:P * (t + 1)],
                                         tb[:, i, :].rearrange("p (b n) -> p b n", b=4), ACT.Copy).then_inc(y_high.sem, 1)

            def silu_part(l, c, r, t):
                tile_done(act, t, l, "C", c)
                if not isinstance(c, int):
                    act.wait_ge(glu_done, c * 2 + (2 * NC * l + t - 1))
                nc.scalar.activation(silu[:, FFN_BUF[r], t, :], ps[:, FFN_BANK[r][t], 0:FC], ACT.Silu).then_inc(silu_done, 1)

            def ffn_split(l, c):
                act.wait_ge(h_turned.sem, c + h_turned.at(l, 0))
                dst = h_hi[:, :, :].rearrange("p (c b) n -> p c b n", b=2)[:, c, :, :]
                nc.scalar.activation(dst, blocks(0), ACT.Copy).then_inc(h_high.sem, 1)

            for row, src in ((R_EVCONV, a["ev_conv_w"][0]), (R_PSCALE, a["ev_pool_scale"]), (R_DW, a["od_dw_w"][0]),
                             (R_DWB, a["od_dw_b"]), (R_CNG, a["od_cn_g"]), (R_CNB, a["od_cn_b"]),
                             (R_GLAB, a["gla_b_gate_2"].rearrange("(o l) n -> o (l n)", o=1))):
                act.dma_start(prow[row:row + src.shape[0], :], src).then_inc(params_in, 16)
            for l, col in ((1, OD_F), (2, HY_LOW), (3, HY_LOW)):
                c0, w = TINY[l]
                act.dma_start(tiny_raw[:, :, c0:c0 + w],
                              w_in(l)[:, col:col + w].rearrange("(k p) n -> p k n", p=P)).then_inc(params_in, 16)
            act.dma_start(fbias[:, :], a["od_forget_b"][0].partition_broadcast(P)).then_inc(params_in, 16)
            act.dma_start(w_up[:, :, :], a["gla_w_gate_up_2"].rearrange("l k n -> k l n")).then_inc(params_in, 16)
            act.dma_start(w_grp[:, :, :], a["ev_pool_w"][0].rearrange("g c d -> c g d")).then_inc(params_in, 16)
            load_rows(0)
            for t in range(NT):
                x_split(0, t)
            feed(4)
            act.wait_ge(params_in, PARAMS)
            nc.scalar.activation(tiny_hi[:, :, :], tiny_raw[:, :, :], ACT.Copy).then_inc(tiny_high, 1)
            act.wait_ge(params_turned, 1)
            nc.scalar.activation(pcol[:, :, :], tb[:, 0, 0:4 * N_ROWS].rearrange("p (b r) -> p b r", b=4), ACT.Copy).then_inc(params_out, 1)
            act.wait_ge(params_out, 1)
            feed(N_W)
            for l in every:
                order = [(0, 0), (1, 0), (0, 1), (1, 1)] + [(c, t) for c in range(2, NA[l]) for t in range(NT)]
                for c, t in order:
                    chunk_out(l, c, t)
                    if (c, t) == (0, 0) and l > 0:
                        x_split(2 * l, 1)
                    if t == 1:
                        if c == 1:
                            load_rows(2 * l) if l else None
                        if LAYERS[l] == "odd":
                            odd_step(c)
                        elif LAYERS[l] == "hyb":
                            hyb_step(l, c)
                        feed(U_A[l] + 4 * (c + 1) + N_W)
                if LAYERS[l] == "even":
                    even_rest()
                elif LAYERS[l] == "odd":
                    odd_rest()
                else:
                    hyb_rest(l)
                after_boundary(2 * l, U_C[l])
                silu_part(l, 0, 0, 0)
                feed(U_C[l] + N_W)
                x_split(2 * l + 1, 1)
                silu_part(l, 1, 1, 0)
                silu_part(l, 0, 0, 1)
                feed(U_C[l] + 4 + N_W)
                ffn_split(l, 0)
                silu_part(l, 1, 1, 1)
                feed(U_C[l] + 8 + N_W)
                load_rows(2 * l + 1)
                with act.Fori(0, (NC - 2) // LOOP) as j:
                    for r in range(LOOP):
                        c = j * LOOP + (2 + r)
                        ffn_split(l, j * LOOP + (1 + r))
                        for t in range(NT):
                            silu_part(l, c, (2 + r) % LOOP, t)
                        for q in range(4):
                            high(Unit(U_C[l] + 4 * (2 + r) + N_W + q, j))
                fed[0] += 4 * (NC - 2)
                ffn_split(l, NC - 1)
                feed(U_D[l] + KF - KD + N_W)
                after_boundary(2 * l + 1, U_D[l] + KF)
                feed(U_D[l] + KF + N_W)

        @block.vector
        def _(dve):
            chain = Chain(dve, dve_step)
            fed = [0]
            V = nc.vector

            def low(v):
                dve.wait_ge(w_high, v.n + 1)
                V.tensor_tensor(w_lo[:, v.slot, :], raw[:, v.raw, :], w_hi[:, v.slot, :].bitcast(F32), ALU.subtract).then_inc(w_low, 1)

            def feed(n):
                for u in range(fed[0], min(n, U_END)):
                    low(Unit(u))
                fed[0] = max(fed[0], min(n, U_END))

            def x_split(kk, t):
                for h in range(2):
                    dve.wait_ge(x_high.sem, x_high.at(kk, 2 * t + h))
                    part = slice(4 * h, 4 * h + 4), slice(P * t, P * (t + 1))
                    V.tensor_tensor(a_lo[:, part[0], part[1]], tb[:, h, :].rearrange("p (b n) -> p b n", b=4),
                                    a_hi[:, part[0], part[1]].bitcast(F32), ALU.subtract).then_inc(x_low.sem, 1)

            def boundary(k, t):
                l, ffn = divmod(k, 2)
                xt = x[:, t, :]
                dve.wait_ge(rows_in, rows_at(k))
                tile_done(dve, t, l, "D" if ffn else "B")
                if is_ln[k]:
                    for h in range(2):
                        xh = x[:, t, CH * h:CH * (h + 1)]
                        ins = V.scalar_tensor_tensor(xh, xh, ALPHA, acc[:, 2 * t + h, :], ALU.mult, ALU.add)
                        if h == 0:
                            chain.step(ins)
                    ins.then_inc(acc_read.sem, 1)
                    for h in range(2):
                        if h == 0:
                            chain.settle()
                        else:
                            dve.wait_ge(acc_read.sem, acc_read.at(k, t))
                        chain.step(V.bn_stats(bn[:, t, h, :], x[:, t, CH * h:CH * (h + 1)]))
                    chain.settle()
                    V.bn_aggr(mv[:, t, :], bn[:, t, :, :].rearrange("p h s -> p (h s)")).then_inc(spread.sem, 1)
                    dve.wait_ge(spread.sem, spread.at(k, t))
                    chain.step(V.scalar_tensor_tensor(xt, xt, mv[:, t, 0:1], rows[:, 0, :], ALU.subtract, ALU.mult))
                    chain.settle()
                    dve.wait_ge(scaled.sem, scaled.at(k, t))
                    ins = V.scalar_tensor_tensor(xt, xt, rstd[:, t:t + 1], rows[:, 1, :], ALU.mult, ALU.add)
                else:
                    if t == 1 and k + 1 < NB:
                        dve.wait_ge(x_turned.sem, x_turned.at(k + 1, 1))
                    dve.wait_ge(scaled.sem, scaled.at(k, t))
                    chain.settle()
                    V.scalar_tensor_tensor(nbuf[:, :], acc[:, 2 * t:2 * t + 2, :].rearrange("p h n -> p (h n)"), rstd[:, t:t + 1],
                                           rows[:, 0, :], ALU.mult, ALU.mult).then_inc(acc_read.sem, 1)
                    dve.wait_ge(acc_read.sem, acc_read.at(k, t))
                    ins = V.tensor_tensor(xt, xt, nbuf[:, :], ALU.add)
                if not pre[k]:
                    ins.then_inc(x_ready.sem, 1)
                    dve.wait_ge(x_ready.sem, x_ready.at(k, t))
                else:
                    ins.then_inc(x_sum.sem, 1)
                    dve.wait_ge(x_sum.sem, x_sum.at(k, t))
                    if is_ln[k] and t == 1:
                        dve.wait_ge(x_turned.sem, x_turned.at(k + 1, 1))
                    dve.wait_ge(scaled2.sem, scaled2.at(k, t))
                    V.scalar_tensor_tensor(nbuf[:, :], xt, rstd2[:, t:t + 1], pre_row(k), ALU.mult, ALU.mult).then_inc(x_ready.sem, 1)

            def after_boundary(k, end):
                boundary(k, 0)
                feed(end + 4)
                if k + 1 < NB:
                    x_split(k + 1, 0)
                feed(end + 8)
                boundary(k, 1)

            def blocks(bank):
                return tb[:, bank, :].rearrange("p (b n) -> p b n", b=2)

            def even_rest():
                for i in range(2):
                    dve.wait_ge(e_act.sem, e_act.at(0, i))
                    dve.wait_ge(e_turned.sem, e_turned.at(0, 3))
                    V.tensor_tensor(e_m[:, 2 * i:2 * i + 2, :], blocks(2 + i), e_cT[:, 2 * i:2 * i + 2, :], ALU.mult).then_inc(e_dve.sem, 1)
                dve.wait_ge(e_dve.sem, e_dve.at(0, 1))
                for tap in range(3):
                    chain.settle()
                    for b in range(4):
                        w = pcol[:, b, R_EVCONV + 2 - tap:R_EVCONV + 3 - tap]
                        if tap == 0:
                            chain.step(V.tensor_scalar(e_y[:, b, :], e_m[:, b, :], w, None, ALU.mult))
                        else:
                            chain.step(V.scalar_tensor_tensor(e_y[:, b, tap:], e_m[:, b, 0:SEQ - tap], w, e_y[:, b, tap:],
                                                              ALU.mult, ALU.add))
                dve.wait_ge(e_turned.sem, e_turned.at(0, 4))
                chain.step(V.memset(e_u[:, :, 0:PAD], 0.0))
                chain.step(V.memset(e_sA[:, :, 0:1], 0.0))
                dve.wait_ge(e_act.sem, e_act.at(0, 3))
                chain.settle()
                W = PAD + SEQ
                chain.step(V.tensor_tensor(e_sA[:, :, 1:W], e_u[:, :, 1:W], e_u[:, :, 0:W - 1], ALU.add))
                chain.settle()
                chain.step(V.tensor_tensor(e_sB[:, 1:4, 3:W], e_sA[:, 1:4, 3:W], e_sA[:, 1:4, 1:W - 2], ALU.add))
                chain.settle()
                chain.step(V.tensor_tensor(e_sA[:, 2:4, 7:W], e_sB[:, 2:4, 7:W], e_sB[:, 2:4, 3:W - 4], ALU.add))
                chain.settle()
                chain.step(V.tensor_tensor(e_sB[:, 3, 15:W], e_sA[:, 3, 15:W], e_sA[:, 3, 7:W - 8], ALU.add))
                chain.settle()
                sums = (e_sA, e_sB, e_sA, e_sB)
                for g in range(4):
                    chain.step(V.tensor_tensor(e_edge[:, g, :], sums[g][:, g, PAD:2 * PAD],
                                               const[:, C_POOL + PAD * g:C_POOL + PAD * (g + 1)], ALU.mult))
                    chain.step(V.scalar_tensor_tensor(e_pool[:, g, :], sums[g][:, g, PAD:], 1.0 / WINDOWS[g], e_u[:, g, PAD:],
                                                      ALU.mult, ALU.subtract))
                chain.settle()
                V.tensor_tensor(e_pool[:, :, 0:PAD], e_edge[:, :, :], e_u[:, :, PAD:2 * PAD], ALU.subtract).then_inc(e_pooled.sem, 1)
                for i in range(2):
                    dve.wait_ge(e_turned.sem, e_turned.at(0, 6 + i))
                    V.tensor_tensor(e_y[:, 2 * i:2 * i + 2, :], blocks(2 + i), e_y[:, 2 * i:2 * i + 2, :], ALU.mult).then_inc(e_dve.sem, 1)
                for i in range(2):
                    dve.wait_ge(e_high.sem, e_high.at(0, i))
                    V.tensor_tensor(h_lo[:, Y_LO + 2 * i:Y_LO + 2 * i + 2, :], e_y[:, 2 * i:2 * i + 2, :],
                                    h_hi[:, 2 * i:2 * i + 2, :].bitcast(F32), ALU.subtract).then_inc(e_low.sem, 1)
                for g in range(4):
                    dve.wait_ge(e_high.sem, e_high.at(0, 3 + 2 * (g // 2)))
                    V.scalar_tensor_tensor(h_lo[:, Y_LO + 4 + g, :], tb[:, g // 2, SEQ * (g % 2):SEQ * (g % 2 + 1)],
                                           pcol[:, g, R_PSCALE:R_PSCALE + 1], h_hi[:, 4 + g, :].bitcast(F32),
                                           ALU.mult, ALU.subtract).then_inc(e_low.sem, 1)

            taps = [(k, b) for k in range(TAPS) for b in range(4)]
            tap_step = {}

            def convolve(n):
                for _ in range(min(n, len(taps))):
                    k, b = taps.pop(0)
                    w, src = pcol[:, b, R_DW + k:R_DW + k + 1], o_pad[:, b, k:k + SEQ]
                    if k == 0:
                        ins = V.tensor_scalar(o_acc[:, b, :], src, w, pcol[:, b, R_DWB:R_DWB + 1], ALU.mult, ALU.add)
                    else:
                        chain.settle(tap_step[b])
                        ins = V.scalar_tensor_tensor(o_acc[:, b, :], src, w, o_acc[:, b, :], ALU.mult, ALU.add)
                    if taps:
                        tap_step[b] = chain.step(ins)
                    else:
                        ins.then_inc(o_conv.sem, 1)

            def odd_step(c):
                if c == 1:
                    dve.wait_ge(a_out, out_at(1, 1, 1))
                    V.tensor_tensor(o_d1[:, :, :], o_d1[:, :, :], o_d2[:, :, :], ALU.mult).then_inc(o_gated.sem, 1)
                if c == 2:
                    dve.wait_ge(o_turned.sem, o_turned.at(1, 1))
                    chain.step(V.memset(o_pad[:, :, 0:PADT], 0.0))
                    chain.settle()
                    dve.wait_ge(o_padded.sem, o_padded.at(1, 1))
                    convolve(12)
                if c == 3:
                    dve.wait_ge(o_fsum.sem, o_fsum.at(1, 0))
                    V.tensor_tensor(o_f[:, 0, :, :], tb[:, 2, 0:NT * GATES].rearrange("p (t g) -> p t g", t=NT),
                                    fbias[:, :].unsqueeze(1).broadcast_to([P, NT, GATES]), ALU.add).then_inc(o_fbiased.sem, 1)
                    convolve(8)
                    dve.wait_ge(o_soft.sem, o_soft.at(1, 0))
                    V.scalar_tensor_tensor(o_f[:, 0, :, :].rearrange("p t g -> p (t g)"), o_f[:, 0, :, :].rearrange("p t g -> p (t g)"),
                                           0.0, o_f[:, 3, :, :].rearrange("p t g -> p (t g)"), ALU.min,
                                           ALU.subtract).then_inc(o_flog.sem, 1)
                    convolve(8)
                if c == 4:
                    convolve(12)

            def odd_rest():
                attention(1, lambda h, part: convolve(4) if part else None)
                share(1)
                convolve(40)
                split_y(1, (0, 1))
                convolve(len(taps))
                for t in range(NT):
                    dve.wait_ge(o_back.sem, o_back.at(1, t))
                    chain.step(V.bn_stats(c_bn[:, t, :], tb[:, 2 + t, :]))
                    chain.settle()
                    V.bn_aggr(c_mv[:, t, :], c_bn[:, t, :]).then_inc(o_spread.sem, 1)
                for t in range(NT):
                    dve.wait_ge(o_scaled.sem, o_scaled.at(1, t))
                    dve.wait_ge(o_spread.sem, o_spread.at(1, t))
                    V.tensor_scalar(o_z[:, t, :], tb[:, 2 + t, :], c_mv[:, t, 0:1], c_rstd[:, t:t + 1], ALU.subtract,
                                    ALU.mult).then_inc(o_normed.sem, 1)
                for t in range(NT):
                    dve.wait_ge(y_high.sem, y_high.at(1, 2 + t))
                    tok = slice(P * t, P * (t + 1))
                    V.tensor_tensor(h_lo[:, Y_LO + 4:Y_LO + 8, tok], o_y[:, t, :, :], h_hi[:, 4:8, tok].bitcast(F32),
                                    ALU.subtract).then_inc(y_low.sem, 1)

            def hyb_step(l, c):
                if c == 2:
                    dve.wait_ge(a_out, out_at(l, 2, 1))
                    v = p_qk[:, :, :].rearrange("p t (h d) -> p t h d", d=HD)
                    x1, x2 = v[:, :, :, 0:ROPE_HALF], v[:, :, :, ROPE_HALF:2 * ROPE_HALF]
                    full = [P, NT, 2 * HEADS, ROPE_HALF]

                    def table(at):
                        return const[:, at:at + NT * ROPE_HALF].rearrange("p (t d) -> p t d", t=NT).unsqueeze(2).broadcast_to(full)

                    prod = nbuf[:, :].rearrange("p (i t h d) -> p i t h d", i=4, t=NT, h=2 * HEADS)
                    for i, (u, at) in enumerate(((x1, C_COS), (x2, C_SIN), (x2, C_COS), (x1, C_SIN))):
                        chain.step(V.tensor_tensor(prod[:, i], u, table(at), ALU.mult))
                    chain.settle()
                    chain.step(V.tensor_tensor(x1, prod[:, 0], prod[:, 1], ALU.subtract))
                    V.tensor_tensor(x2, prod[:, 2], prod[:, 3], ALU.add).then_inc(roped.sem, 1)
                if c == 3:
                    dve.wait_ge(z_log.sem, z_log.at(l, 0))
                    chain.step(V.scalar_tensor_tensor(g_z[:, :, :], g_z[:, :, :], 0.0, g_e[:, :, :], ALU.min, ALU.subtract))
                    chain.settle()
                    ones = const[:, C_TRI + P:C_TRI + P + 1].broadcast_to([P, SEQ])
                    for b in range(2):
                        chain.step(V.tensor_tensor_scan(g_b[:, b, :], ones, g_z[:, b, :], 0.0, ALU.mult, ALU.add))
                if c == 5:
                    dve.wait_ge(a_out, out_at(l, 5, 1))
                    dve.wait_ge(rows_in, rows_at(2 * l))
                    chain.step(V.tensor_tensor(g_r[:, :, :], g_r[:, :, :],
                                               rows[:, 2, HALF:D].unsqueeze(1).broadcast_to([P, NT, HALF]), ALU.mult))

            def level_part(l):
                def part(n, second):
                    m = LEVELS[n]
                    b, z, e = (level_view(u[:, :, :], m) for u in (g_b, g_z, g_e))
                    count = NT * P // m
                    if not second:
                        mid = b[:, :, 0, m - 1:m].broadcast_to([P, count, m])
                        if n == 0:
                            chain.settle()
                        else:
                            dve.wait_ge(g_exp.sem, g_exp.at(l, n - 1))
                        chain.step(V.tensor_tensor(z[:, :, 1, :], b[:, :, 1, :], mid, ALU.subtract))
                        V.tensor_tensor(z[:, :, 0, :], mid, b[:, :, 0, :], ALU.subtract).then_inc(g_diff.sem, 1)
                        keep(l, n)
                        return
                    slot = (n + 1) % 2
                    o = level_view(g_x[:, slot, :, :], m)
                    q, k = level_view(g_qkT[:, 0:2, :], m), level_view(g_qkT[:, 2:4, :], m)
                    dve.wait_ge(g_exp.sem, g_exp.at(l, n))
                    if n >= 2:
                        dve.wait_ge(g_pair.sem, g_pair.at(l, n - 1))
                    chain.step(V.tensor_tensor(o[:, :, 1, :], e[:, :, 1, :], q[:, :, 1, :], ALU.mult))
                    V.tensor_tensor(o[:, :, 0, :], e[:, :, 0, :], k[:, :, 0, :], ALU.mult).then_inc(g_scaled.sem, 1)
                return part

            def keep(l, n):
                dve.wait_ge(g_pair.sem, g_pair.at(l, n))
                if n == 1:
                    for par in range(2):
                        ins = V.tensor_copy(g_far[:, 2 * par:2 * par + 2, :], acc[:, 1 + 2 * par, 0:2 * P].rearrange("p (i n) -> p i n", i=2))
                        if par == 0:
                            chain.step(ins)
                else:
                    for par in range(2):
                        dst = g_att[:, 4 * par:4 * par + 4, :]
                        src = acc[:, 1 + 2 * par, :].rearrange("p (i n) -> p i n", i=4)
                        if n == 0:
                            ins = V.tensor_tensor(dst, src, ident.unsqueeze(1).broadcast_to([P, 4, P]), ALU.mult)
                        else:
                            mask = const[:, C_LEVEL + P * (n - 2):C_LEVEL + P * (n - 1)].bitcast(I32)
                            ins = V.copy_predicated(dst, mask.unsqueeze(1).broadcast_to([P, 4, P]), src)
                        if par == 0:
                            chain.step(ins)
                ins.then_inc(g_kept.sem, 1)
                dve.wait_ge(g_kept.sem, g_kept.at(l, n))

            def hyb_rest(l):
                attention(l, level_part(l))
                keep(l, NL)
                share(l)
                for t in range(NT):
                    dve.wait_ge(a_scaled.sem, a_scaled.at(l, t))
                    V.scalar_tensor_tensor(y_tok[:, t, :], y_tok[:, t, :], a_rstd[:, t:t + 1], rows[:, 2, 0:HALF], ALU.mult,
                                           ALU.mult).then_inc(a_normed.sem, 1)
                for t in range(NT):
                    dve.wait_ge(g_rooted.sem, g_rooted.at(l, 0))
                    chain.step(V.tensor_tensor(heads(g_o[:, t, :], GLA_H), heads(acc[:, 1 + 2 * t, :], GLA_H),
                                               g_rstd[:, t, :].unsqueeze(2).broadcast_to([P, GLA_H, GLA_DV]), ALU.mult))
                    chain.settle()
                    V.tensor_tensor(g_o[:, t, :], g_o[:, t, :], g_r[:, t, :], ALU.mult).then_inc(g_normed.sem, 1)
                split_y(l, (0, 1, 2, 3))

            def attention(l, beside):
                dve.wait_ge(qk_turned.sem, qk_turned.at(l, 3))
                for i in range(2, 4):
                    V.tensor_copy(qkT[:, 2 * i:2 * i + 2, :], blocks(i)).then_inc(k_out.sem, 1)
                for h in range(HEADS):
                    if h == 0:
                        tile_done(dve, 1, l, "A", NA[l] - 1)
                    beside(h, 0)
                    bank = tb[:, h % 2, :]
                    dve.wait_ge(logits.sem, logits.at(l, h))
                    if h >= 2:
                        dve.wait_ge(weighed.sem, weighed.at(l, h - 2))
                    chain.step(V.reduce_max(peak[:, h % 2, 0:1], bank[:, 0:P], AX_X))
                    chain.step(V.reduce_max(peak[:, h % 2, 1:2], bank[:, P:3 * P], AX_X))
                    chain.settle()
                    V.tensor_scalar(npeak[:, h % 2, :], peak[:, h % 2, :], -SCALE, None, ALU.mult).then_inc(peaks.sem, 1)
                    beside(h, 1)
                    dve.wait_ge(p_turned.sem, p_turned.at(l, h))
                    if h >= 2:
                        dve.wait_ge(attended.sem, attended.at(l, h - 2))
                    V.tensor_copy(probsT[:, h % 2, :], tb[:, 2 + h % 2, 0:3 * P]).then_inc(p_out.sem, 1)

            def share(l):
                dve.wait_ge(weighed.sem, weighed.at(l, HEADS - 1))
                chain.step(V.reciprocal(share_of[:, :, :], total[:, :, :]))
                chain.settle()
                dve.wait_ge(attended.sem, attended.at(l, HEADS - 1))
                for t in range(NT):
                    V.tensor_tensor(heads(y_tok[:, t, :], HEADS), heads(acc[:, 2 * t, :], HEADS),
                                    share_of[:, t, :].unsqueeze(2).broadcast_to([P, HEADS, HD]), ALU.mult).then_inc(shared.sem, 1)

            def split_y(l, which):
                for i in which:
                    b, tok = 4 * (i // 2), slice(P * (i % 2), P * (i % 2 + 1))
                    dve.wait_ge(y_high.sem, y_high.at(l, i))
                    V.tensor_tensor(h_lo[:, Y_LO + b:Y_LO + b + 4, tok], tb[:, i, :].rearrange("p (b n) -> p b n", b=4),
                                    h_hi[:, b:b + 4, tok].bitcast(F32), ALU.subtract).then_inc(y_low.sem, 1)

            def glu_part(l, c, r, t):
                dve.wait_ge(silu_done, glu_at(l, c, t))
                if not isinstance(c, int):
                    dve.wait_ge(h_turned.sem, c + (h_turned.at(l, 0) - 1))
                V.tensor_tensor(glu[:, FFN_BUF[r], t, :], silu[:, FFN_BUF[r], t, :], ps[:, FFN_BANK[r][t], FC:2 * FC],
                                ALU.mult).then_inc(glu_done, 1)

            def ffn_split(l, c):
                dve.wait_ge(h_high.sem, c + h_high.at(l, 0))
                hi, lo = (u[:, :, :].rearrange("p (c b) n -> p c b n", b=2)[:, c, :, :] for u in (h_hi, h_lo))
                V.tensor_tensor(lo, blocks(0), hi.bitcast(F32), ALU.subtract).then_inc(h_low.sem, 1)

            for t in range(NT):
                x_split(0, t)
            feed(4)
            dve.wait_ge(tiny_high, 1)
            V.tensor_tensor(tiny_lo[:, :, :], tiny_raw[:, :, :], tiny_hi[:, :, :].bitcast(F32), ALU.subtract).then_inc(tiny_done, 1)
            dve.wait_ge(params_out, 1)
            feed(N_W)
            for l in every:
                if l > 0:
                    feed(U_A[l] + N_W)
                    x_split(2 * l, 1)
                for c in range(1, NA[l]):
                    if LAYERS[l] == "odd":
                        odd_step(c)
                    elif LAYERS[l] == "hyb":
                        hyb_step(l, c)
                    feed(U_A[l] + 4 * (c + 1) + N_W)
                if LAYERS[l] == "even":
                    even_rest()
                elif LAYERS[l] == "odd":
                    odd_rest()
                else:
                    hyb_rest(l)
                after_boundary(2 * l, U_C[l])
                glu_part(l, 0, 0, 0)
                feed(U_C[l] + N_W)
                x_split(2 * l + 1, 1)
                glu_part(l, 1, 1, 0)
                glu_part(l, 0, 0, 1)
                feed(U_C[l] + 4 + N_W)
                ffn_split(l, 0)
                glu_part(l, 1, 1, 1)
                feed(U_C[l] + 8 + N_W)
                with dve.Fori(0, (NC - 2) // LOOP) as j:
                    for r in range(LOOP):
                        ffn_split(l, j * LOOP + (1 + r))
                        for t in range(NT):
                            glu_part(l, j * LOOP + (2 + r), (2 + r) % LOOP, t)
                        for q in range(4):
                            low(Unit(U_C[l] + 4 * (2 + r) + N_W + q, j))
                fed[0] += 4 * (NC - 2)
                ffn_split(l, NC - 1)
                feed(U_D[l] + KF - KD + N_W)
                after_boundary(2 * l + 1, U_D[l] + KF)

        @block.gpsimd
        def _(pool):
            chain = Chain(pool, pool_step)
            nc.gpsimd.memset(minus_half, -0.5).then_inc(set_up, 1)
            pool.wait_ge(set_up, 1)

            def root(dst, src, scale, eps, st, n):
                chain.step(nc.gpsimd.tensor_scalar(dst, src, scale, eps, ALU.mult, ALU.add))
                chain.settle()
                nc.gpsimd.tensor_tensor(dst, dst, minus_half[:, 0:n], ALU.pow).then_inc(st.sem, 1)

            def boundary(k):
                for t in range(NT):
                    one = slice(t, t + 1)
                    if is_ln[k]:
                        pool.wait_ge(spread.sem, spread.at(k, t))
                        root(rstd[:, one], mv[:, t, 1:2], 1.0, LN_EPS, scaled, 1)
                    else:
                        pool.wait_ge(squared.sem, squared.at(k, t))
                        root(rstd[:, one], ssq[:, one], 1.0 / D, RMS_EPS, scaled, 1)
                    if pre[k]:
                        pool.wait_ge(spread2.sem, spread2.at(k, t))
                        root(rstd2[:, one], ssq2[:, one], 1.0 / D, RMS_EPS, scaled2, 1)

            for l in every:
                if LAYERS[l] == "odd":
                    for t in range(NT):
                        pool.wait_ge(o_spread.sem, o_spread.at(l, t))
                        root(c_rstd[:, t:t + 1], c_mv[:, t, 1:2], 1.0, LN_EPS, o_scaled, 1)
                if LAYERS[l] == "hyb":
                    for t in range(NT):
                        pool.wait_ge(a_spread.sem, a_spread.at(l, t))
                        root(a_rstd[:, t:t + 1], a_ssq[:, t:t + 1], 1.0 / HALF, RMS_EPS, a_scaled, 1)
                    pool.wait_ge(g_spread.sem, g_spread.at(l, 0))
                    root(g_rstd.rearrange("p t h -> p (t h)"), g_ssq.rearrange("p t h -> p (t h)"), 1.0 / GLA_DV, RMS_EPS,
                         g_rooted, NT * GLA_H)
                boundary(2 * l)
                boundary(2 * l + 1)


INPUTS = (
    "x", "ev_w_in", "ev_conv_w", "ev_pool_w", "ev_pool_scale", "ev_w_out", "od_w_in", "od_forget_b", "od_dw_w",
    "od_dw_b", "od_cn_g", "od_cn_b", "od_w_out", "ln_mix_g", "ln_mix_b", "ln_ffn_g", "ln_ffn_b", "ffn_w_in",
    "ffn_w_out", "mix_pre_norm_2", "mix_post_norm_2", "ffn_pre_norm_2", "ffn_post_norm_2", "w_in_2",
    "gla_w_gate_up_2", "gla_b_gate_2", "gla_out_norm_2", "attn_out_norm_2", "w_out_2", "w_gate_2", "w_up_2",
    "w_down_2",
)


def kernel(**inputs):
    import concourse.bacc as bacc
    import numpy as np
    from concourse.bass_utils import run_bass_kernel_spmd

    nc = bacc.Bacc("TRN2", target_bir_lowering=False, num_devices=1, dynamic_dma_scratch_size=1024)
    arrays = {name: np.ascontiguousarray(inputs[name]) for name in INPUTS}
    arrays["shape_consts"] = shape_constants()
    aps = {name: nc.dram_tensor(name, v.shape, mybir.dt.from_np(v.dtype), kind="ExternalInput").ap() for name, v in arrays.items()}
    out = nc.dram_tensor("out", (1, SEQ, D), F32, kind="ExternalOutput").ap()
    blocks_kernel(nc, aps, out)
    result = run_bass_kernel_spmd(nc, [arrays], core_ids=[0])
    return result.results[0]["out"]
```

```python
from contextlib import ExitStack

import concourse.bass as bass
from concourse import mybir

ALU = mybir.AluOpType
ACT = mybir.ActivationFunctionType
AX_X = mybir.AxisListType.X
F32 = mybir.dt.float32
F32R = mybir.dt.float32r
I32 = mybir.dt.int32

P = 128
D = 1024
SEQ = 256
NT = SEQ // P
KD = D // P
CH = 512
D_FF = 2816
FC = 256
NC = D_FF // FC
KF = D_FF // P
HALF = D // 2
DEPTH = 2
ALPHA = (2.0 * DEPTH) ** 0.25
LN_EPS = 1e-5
RMS_EPS = 1e-6
HEADS = 8
HD = 64
SCALE = HD ** -0.5
MASKED = -1e30
TAPS = 31
ROPE_HALF = 8
ROPE_THETA = 500000.0
RANK = 16
GLA_H = 4
GLA_DK = 64
GLA_DV = 128
GLA_SCALE = GLA_DK ** -0.5
GLA_TAU = 16.0
DILATED = ((128, 1), (512, 4), (2048, 16))
WINDOWS = (2, 4, 8, 16)
PAD = 16

LAYERS = ("even", "odd", "hyb", "hyb")
EV_COLS = (512, 1024, 1536, 0)
OD_COLS = (1544, 2056, 0, 512, 1024)
HY_COLS = (1536, 0, 512, 1024, 2048, 2560)
COLS = (EV_COLS, OD_COLS, HY_COLS, HY_COLS)
OD_F = 1536
HY_LOW = 3072
GATES = 8
TINY = {1: (0, GATES), 2: (GATES, RANK), 3: (GATES + RANK, RANK)}
TINY_W = GATES + 2 * RANK

LEVELS = (128, 64, 32, 16, 8, 4, 2, 1)

C_IDENT = 0
C_TRI = C_IDENT + P
C_CAUSAL = C_TRI + 2 * P
C_DIL = C_CAUSAL + P
C_COS = C_DIL + 3 * P
C_SIN = C_COS + NT * ROPE_HALF
C_LEVEL = C_SIN + NT * ROPE_HALF
C_POOL = C_LEVEL + (len(LEVELS) - 1) * P
N_CONST = C_POOL + len(WINDOWS) * PAD

R_EVCONV, R_PSCALE, R_DW, R_DWB, R_CNG, R_CNB, R_GLAB = 0, 3, 4, 35, 36, 37, 38
N_ROWS = 39

PARAMS = 16 * 13

N_RAW = 4
N_W = 12
LOOP = 3


def shape_constants():
    import numpy as np

    c = np.zeros((P, N_CONST), np.float32)
    i = np.arange(P)
    c[:, C_IDENT:C_IDENT + P] = np.eye(P)
    c[:, C_TRI:C_TRI + P] = i[:, None] <= i[None, :]
    c[:, C_TRI + P:C_TRI + 2 * P] = 1.0
    c[:, C_CAUSAL:C_CAUSAL + P] = np.where(i[:, None] >= i[None, :], 0.0, -MASKED)

    def dilated(dist):
        n = sum(((dist >= 0) & (dist <= w) & (dist % d == 0)).astype(np.int64) for w, d in DILATED)
        return np.where(n > 0, -np.log(np.maximum(n, 1)), -MASKED)

    near = i[:, None] - i[None, :]
    c[:, C_DIL:C_DIL + P] = dilated(near)
    c[:, C_DIL + P:C_DIL + 2 * P] = dilated(near + P)
    c[:, C_DIL + 2 * P:C_DIL + 3 * P] = dilated(near)
    inv = np.float32(ROPE_THETA) ** (-(np.arange(ROPE_HALF, dtype=np.float32) * 2.0) / np.float32(2 * ROPE_HALF))
    ang = np.arange(SEQ, dtype=np.float32)[:, None] * inv.astype(np.float32)[None, :]
    for t in range(NT):
        c[:, C_COS + ROPE_HALF * t:C_COS + ROPE_HALF * (t + 1)] = np.cos(ang[P * t:P * (t + 1)])
        c[:, C_SIN + ROPE_HALF * t:C_SIN + ROPE_HALF * (t + 1)] = np.sin(ang[P * t:P * (t + 1)])
    for n, m in enumerate(LEVELS[1:]):
        blk = i // (2 * m)
        right = i // m % 2
        c[:, C_LEVEL + P * n:C_LEVEL + P * (n + 1)] = (
            (blk[:, None] == blk[None, :]) & (right[:, None] == 0) & (right[None, :] == 1))
    for g, w in enumerate(WINDOWS):
        c[:, C_POOL + PAD * g:C_POOL + PAD * (g + 1)] = 1.0 / np.minimum(np.arange(PAD) + 1, w)
    return c


class Stage:

    def __init__(self, sem, per, layers):
        self.sem, self.per, self.layers = sem, per, layers

    def at(self, layer, i):
        return self.layers.index(layer) * self.per + i + 1


class Chain:

    def __init__(self, eng, sem):
        self.eng, self.sem, self.n = eng, sem, 0

    def step(self, ins):
        self.n += 1
        ins.then_inc(self.sem, 1)
        return self.n

    def settle(self, n=None):
        self.eng.wait_ge(self.sem, self.n if n is None else n)


class Unit:

    def __init__(self, u, j=0):
        self.raw = u % N_RAW
        self.slot = u % N_W
        self.loads = u // N_RAW + (N_W // N_RAW) * j + 1
        self.n = u + N_W * j
        self.first = u < N_RAW
        self.fresh = u < N_W


def blocks_kernel(nc, a, out):
    ctx = ExitStack()
    with ctx:
        top = [1280]

        def place(name, shape, dt, at=None):
            size = 4
            for n in shape[1:]:
                size *= n
            if at is None:
                at = top[0]
                top[0] += (size + 31) // 32 * 32
            return nc.alloc_sbuf_tensor_at(name, list(shape), dt, offset=at), at

        raw, _ = place("raw", [P, N_RAW, 2 * CH], F32)
        w_hi, _ = place("w_hi", [P, N_W, 2 * CH], F32R)
        w_lo, _ = place("w_lo", [P, N_W, 2 * CH], F32R)
        x, _ = place("x", [P, NT, D], F32)
        a_hi, at_a = place("a_hi", [P, KD, SEQ], F32R)
        a_lo, _ = place("a_lo", [P, KD, SEQ], F32R)
        h_hi, at_h = place("h_hi", [P, KF, SEQ], F32R)
        h_lo, at_hl = place("h_lo", [P, KF, SEQ], F32R)
        rows, _ = place("rows", [P, 3, D], F32)
        nbuf, _ = place("nbuf", [P, D], F32)
        const, _ = place("const", [P, N_CONST], F32)
        pcol, _ = place("pcol", [P, 4, N_ROWS], F32)
        w_up, _ = place("w_up", [RANK, 2, SEQ], F32)
        tiny_hi, _ = place("tiny_hi", [P, KD, TINY_W], F32R)
        tiny_lo, _ = place("tiny_lo", [P, KD, TINY_W], F32R)
        bias_hi, _ = place("bias_hi", [P, 4 * P], F32R)
        bias_lo, _ = place("bias_lo", [P, 3 * P], F32R)
        ident_r, _ = place("ident_r", [P, P], F32R)
        fbias, _ = place("fbias", [P, GATES], F32)
        stat, _ = place("stat", [P, 160], F32)
        silu, at_s = place("silu", [P, 2, NT, FC], F32)
        glu, _ = place("glu", [P, 2, NT, FC], F32)
        assert top[0] <= nc.SBUF_PARTITION_SIZE_BYTES, top[0]

        tiny_raw, _ = place("tiny_raw", [P, KD, TINY_W], F32, at_s)
        prow, _ = place("prow", [N_ROWS, HALF], F32, at_s + 4096)
        squares, _ = place("squares", [P, D], F32, at_s)
        Y_LO = KF - KD
        at_m = at_h + KD * SEQ * 4

        def scratch(name, shape, slot):
            return place(name, shape, F32, int(at_m + 4096 * slot))[0]

        def late(name, shape, byte):
            return place(name, shape, F32, at_a + byte)[0]

        p_qk = scratch("p_qk", [P, NT, D], 0)
        qT, _ = place("qT", [P, 4, SEQ], F32, at_hl + Y_LO * SEQ * 4)
        kT, _ = place("kT", [P, 4, SEQ], F32, at_h)
        p_v = scratch("p_v", [P, NT, CH], 2)
        y_tok = scratch("y_tok", [P, NT, CH], 6)
        probs = late("probs", [P, 2, 3 * P], 0)
        probsT = late("probsT", [P, 2, 3 * P], 3072)
        e_pc = scratch("e_pc", [P, NT, CH], 0)
        e_cT = scratch("e_cT", [P, 4, SEQ], 0)
        e_pv = scratch("e_pv", [P, NT, CH], 1)
        e_m = scratch("e_m", [P, 4, SEQ], 1)
        e_pu = scratch("e_pu", [P, NT, CH], 2)
        e_pb = scratch("e_pb", [P, NT, CH], 3)
        w_grp = scratch("w_grp", [P, 4, P], 4)
        e_sB = scratch("e_sB", [P, 4, PAD + SEQ], 4.5)
        e_pool = scratch("e_pool", [P, 4, SEQ], 5.75)
        e_y = scratch("e_y", [P, 4, SEQ], 0)
        e_u = late("e_u", [P, 4, PAD + SEQ], 4096)
        e_sA = late("e_sA", [P, 4, PAD + SEQ], 8448)
        e_edge = late("e_edge", [P, 4, PAD], 12800)
        PADT = TAPS - 1
        o_d1 = scratch("o_d1", [P, NT, CH], 3)
        o_d2 = scratch("o_d2", [P, NT, CH], 4)
        o_pad = scratch("o_pad", [P, 4, PADT + SEQ], 3)
        o_acc = scratch("o_acc", [P, 4, SEQ], 5)
        o_z = late("o_z", [P, NT, CH], 6144)
        o_y = late("o_y", [P, NT, 4, P], 10240)
        o_f, _ = place("o_f", [P, 4, NT, GATES], F32, at_s)
        o_cum, _ = place("o_cum", [GATES, 2, 3 * P], F32R, at_s + 2048)
        g_pqk = scratch("g_pqk", [P, NT, CH], 3)
        g_qkT = scratch("g_qkT", [P, 4, SEQ], 3)
        g_v = scratch("g_v", [P, NT, CH], 4)
        g_r = scratch("g_r", [P, NT, CH], 5)
        g_o = scratch("g_o", [P, NT, CH], 0)
        g_z, _ = place("g_z", [P, 2, SEQ], F32, at_s)
        g_e, _ = place("g_e", [P, 2, SEQ], F32, at_s + 2048)
        g_b, _ = place("g_b", [P, 2, SEQ], F32, at_s + 4096)
        g_low, _ = place("g_low", [P, NT, RANK], F32, at_s + 6144)
        g_lowT, _ = place("g_lowT", [RANK, SEQ], F32, at_s + 6400)
        g_x = scratch("g_x", [P, 2, 2, SEQ], 6)
        g_att, _ = place("g_att", [P, 2 * GLA_H, P], F32, at_h + 4 * SEQ * 4)
        g_far, _ = place("g_far", [P, GLA_H, P], F32, at_hl + (Y_LO + 4) * SEQ * 4)

        ident = const[:, C_IDENT:C_IDENT + P]
        bn = stat[:, 0:24].rearrange("p (t h s) -> p t h s", t=NT, h=2)
        mv = stat[:, 24:28].rearrange("p (t s) -> p t s", t=NT)
        rstd = stat[:, 28:30]
        ssq = stat[:, 30:32]
        ssq2 = stat[:, 32:34]
        rstd2 = stat[:, 34:36]
        minus_half = stat[:, 36:44]
        low_of = stat[:, 48:52].rearrange("p (b t) -> p b t", b=2)
        total = stat[:, 52:68].rearrange("p (t h) -> p t h", t=NT)
        share_of = stat[:, 68:84].rearrange("p (t h) -> p t h", t=NT)
        a_ssq = stat[:, 84:86]
        a_rstd = stat[:, 86:88]
        g_ssq = stat[:, 88:96].rearrange("p (t h) -> p t h", t=NT)
        g_rstd = stat[:, 96:104].rearrange("p (t h) -> p t h", t=NT)
        c_bn = stat[:, 104:116].rearrange("p (t s) -> p t s", t=NT)
        c_mv = stat[:, 116:120].rearrange("p (t s) -> p t s", t=NT)
        c_rstd = stat[:, 120:122]

        ps = ctx.enter_context(nc.psum_tensor("ps", [P, 8, CH], F32))
        acc, tb = ps[:, 0:4, :], ps[:, 4:8, :]
        IN_BANK = ((0, 2), (1, 3))
        FFN_BANK = ((0, 2), (6, 7), (1, 3))
        FFN_BUF = (0, 1, 0)

        NA = [len(c) for c in COLS]
        U_A, U_B, U_C, U_D, u = [], [], [], [], 0
        for l in range(len(LAYERS)):
            U_A.append(u)
            U_B.append(U_A[l] + 4 * NA[l])
            U_C.append(U_B[l] + KD)
            U_D.append(U_C[l] + 4 * NC)
            u = U_D[l] + KF
        U_END = u
        ACC0 = [sum(NA[:l]) + (NC + 2) * l for l in range(len(LAYERS))]

        def acc_at(l, phase, c=0):
            return ACC0[l] + {"A": 0, "B": NA[l], "C": NA[l] + 1, "D": NA[l] + 1 + NC}[phase] + c + 1

        def out_at(l, c, t):
            return 2 * sum(NA[:l]) + (2 * t + c if c < 2 else 2 * c + t) + 1

        def glu_at(l, c, t):
            if isinstance(c, int) and c < 2:
                return 2 * NC * l + 2 * t + c + 1
            return c * 2 + (2 * NC * l + t + 1)

        NB = 2 * len(LAYERS)
        is_ln = [LAYERS[k // 2] != "hyb" for k in range(NB)]
        pre = [k + 1 < NB and LAYERS[(k + 1) // 2] == "hyb" for k in range(NB)]

        def sem(name):
            return ctx.enter_context(nc.semaphore(name))

        every = list(range(len(LAYERS)))
        attn = [1, 2, 3]
        hyb = [2, 3]

        def stage(name, per, layers=None):
            return Stage(sem(name), per, every if layers is None else layers)

        raw_in = [sem(f"raw_in{i}") for i in range(N_RAW)]
        x_in = [sem(f"x_in{t}") for t in range(NT)]
        const_in, params_in, rows_in, out_done = sem("const_in"), sem("params_in"), sem("rows_in"), sem("out_done")
        w_high, w_low, w_used = sem("w_high"), sem("w_low"), sem("w_used")
        acc_done = sem("acc_done")
        a_out = sem("a_out")
        silu_done, glu_done = sem("silu_done"), sem("glu_done")
        h_turned, h_high, h_low = stage("h_turned", NC), stage("h_high", NC), stage("h_low", NC)
        bounds = list(range(NB))
        x_turned, x_high, x_low = (stage(n, 4, bounds) for n in ("x_turned", "x_high", "x_low"))
        acc_read = stage("acc_read", NT, bounds)
        spread = stage("spread", NT, [k for k in bounds if is_ln[k]])
        squared = stage("squared", NT, [k for k in bounds if not is_ln[k]])
        scaled = stage("scaled", NT, bounds)
        spread2 = stage("spread2", NT, [k for k in bounds if pre[k]])
        scaled2 = stage("scaled2", NT, [k for k in bounds if pre[k]])
        x_sum = stage("x_sum", NT, [k for k in bounds if pre[k]])
        x_ready = stage("x_ready", NT, bounds)
        act_step, dve_step, pool_step = sem("act_step"), sem("dve_step"), sem("pool_step")
        set_up, tiny_high, params_turned, params_out = sem("set_up"), sem("tiny_high"), sem("params_turned"), sem("params_out")
        tiny_done = sem("tiny_done")
        e_turned, e_act, e_dve = stage("e_turned", 10, [0]), stage("e_act", 4, [0]), stage("e_dve", 4, [0])
        e_pooled, e_high, e_low = stage("e_pooled", 1, [0]), stage("e_high", 6, [0]), stage("e_low", 6, [0])
        o_gated, o_turned, o_padded = stage("o_gated", 1, [1]), stage("o_turned", 2, [1]), stage("o_padded", 2, [1])
        o_fsum, o_fbiased, o_flog, o_fcum, o_cumT = (stage(n, 1, [1]) for n in ("o_fsum", "o_fbiased", "o_flog", "o_fcum", "o_cumT"))
        o_soft, o_cumhigh = stage("o_soft", 1, [1]), stage("o_cumhigh", 1, [1])
        o_conv, o_back, o_spread, o_scaled = stage("o_conv", 1, [1]), stage("o_back", NT, [1]), stage("o_spread", NT, [1]), stage("o_scaled", NT, [1])
        o_normed, o_silu = stage("o_normed", NT, [1]), stage("o_silu", NT, [1])
        roped = stage("roped", 1, hyb)
        qk_turned, q_out, k_out = stage("qk_turned", 4, attn), stage("q_out", 2, attn), stage("k_out", 2, attn)
        logits, lows, weighed = stage("logits", HEADS, attn), stage("lows", HEADS, attn), stage("weighed", HEADS, attn)
        p_turned, p_out, attended = stage("p_turned", HEADS, attn), stage("p_out", HEADS, attn), stage("attended", HEADS, attn)
        shared = stage("shared", NT, attn)
        a_spread, a_scaled, a_normed = (stage(n, NT, hyb) for n in ("a_spread", "a_scaled", "a_normed"))
        y_turned, y_high, y_low = stage("y_turned", 4, attn), stage("y_high", 4, attn), stage("y_low", 4, attn)
        l_sum, l_out, l_turned, l_outT, z_done, z_out, z_log, decay = (
            stage(n, 1, hyb) for n in ("l_sum", "l_out", "l_turned", "l_outT", "z_done", "z_out", "z_log", "decay"))
        gqk_turned, gqk_out = stage("gqk_turned", 2, hyb), stage("gqk_out", 2, hyb)
        NL = len(LEVELS)
        g_diff, g_exp, g_scaled = (stage(n, NL, hyb) for n in ("g_diff", "g_exp", "g_scaled"))
        g_pair, g_kept = stage("g_pair", NL + 1, hyb), stage("g_kept", NL + 1, hyb)
        g_done, g_spread, g_rooted, g_normed = stage("g_done", NT, hyb), stage("g_spread", 1, hyb), stage("g_rooted", 1, hyb), stage("g_normed", NT, hyb)

        def w_in(l):
            return a["ev_w_in"][0] if l == 0 else a["od_w_in"][0] if l == 1 else a["w_in_2"][l - 2]

        def w_out(l):
            return a["ev_w_out"][0] if l == 0 else a["od_w_out"][0] if l == 1 else a["w_out_2"][l - 2]

        def w_ffn(l):
            if l < 2:
                both = a["ffn_w_in"][l].rearrange("(k p) (h c n) -> h p k c n", p=P, h=2, n=FC)
                return both[0], both[1]
            return tuple(a[n][l - 2].rearrange("(k p) (c n) -> p k c n", p=P, n=FC) for n in ("w_gate_2", "w_up_2"))

        def w_down(l):
            return a["ffn_w_out"][l] if l < 2 else a["w_down_2"][l - 2]

        def norm_rows(k):
            l, ffn = divmod(k, 2)
            if is_ln[k]:
                g, b = ("ln_ffn_g", "ln_ffn_b") if ffn else ("ln_mix_g", "ln_mix_b")
                r = [(0, 0, a[g][l]), (1, 0, a[b][l])]
                if pre[k]:
                    r.append((2, 0, a["mix_pre_norm_2"][0]))
                return r
            j = l - 2
            r = [(0, 0, a["ffn_post_norm_2" if ffn else "mix_post_norm_2"][j])]
            if pre[k]:
                r.append((1, 0, a["mix_pre_norm_2"][j + 1] if ffn else a["ffn_pre_norm_2"][j]))
            if not ffn:
                r += [(2, 0, a["attn_out_norm_2"][j]), (2, HALF, a["gla_out_norm_2"][j])]
            return r

        def rows_at(k):
            return 16 * sum(len(norm_rows(i)) for i in range(k + 1))

        def pre_row(k):
            return rows[:, 2 if is_ln[k] else 1, :]

        def heads(ap, n):
            return ap.rearrange("p (h d) -> p h d", h=n)

        def level_view(ap, m):
            return ap.rearrange("p b (j s m) -> p (b j) s m", s=2, m=m)

        def tile_done(eng, t, l, phase, c=0):
            if t == 0:
                eng.wait_ge(acc_done, acc_at(l, phase, c))
            else:
                last = {"A": U_A[l] + 3, "B": U_B[l] + KD - 1, "C": U_C[l] + 3, "D": U_D[l] + KF - 1}[phase]
                eng.wait_ge(w_used, c * 4 + (last + 1) if phase in "AC" else last + 1)

        def out_order(l):
            return (4, 5, 6, 7, 0, 1, 2, 3) if LAYERS[l] == "hyb" else range(KD)

        def y_part(l, i):
            t = i % 2
            if LAYERS[l] == "hyb":
                return (4, t, 1 + 2 * t) if i < 2 else (0, t, 4 + t)
            return (0 if i < 2 else 4), t, 4 + t

        LEVEL_STEP = ((3, 0), (3, 1), (3, 2), (3, 3), (4, 1), (4, 2), (4, 3), (5, 1), (5, 2))

        LEVELS_AFTER = {2: (0, 1, 2), 3: (3, 4, 5), 4: (6, 7)}

        def right(ap, m):
            return ap.rearrange("p (j s m) -> p j s m", s=2, m=m)[:, :, 1, :]

        def level_rows(h):
            return slice(GLA_DK * (h % 2), GLA_DK * (h % 2 + 1)), h // 2

        def kept_at(h, t):
            return 4 * (h % 2) + 2 * (h // 2) + t

        def far_at(h):
            return 2 * (h % 2) + h // 2

        block = ctx.enter_context(nc.Block())

        @block.sync
        def _(sp):
            def load(v, left, right, split):
                if not v.first:
                    sp.wait_ge(w_low, v.n - N_RAW + 1)
                dst = raw[:, v.raw, :].rearrange("p (i h n) -> p i h n", i=2, h=2) if split else raw[:, v.raw, :]
                sp.dma_start(dst[:, :, 0, :] if split else dst[:, 0:CH], left).then_inc(raw_in[v.raw], 16)
                sp.dma_start(dst[:, :, 1, :] if split else dst[:, CH:2 * CH], right).then_inc(raw_in[v.raw], 16)

            def ffn_chunk(l, c, j, unit0):
                gate, up = w_ffn(l)
                for q in range(4):
                    k = slice(2 * q, 2 * q + 2)
                    load(Unit(unit0 + q, j), gate[:, k, c, :], up[:, k, c, :], True)

            for t in range(NT):
                sp.dma_start(x[:, t, :], a["x"][0, P * t:P * (t + 1), :]).then_inc(x_in[t], 16)
            sp.dma_start(const[:], a["shape_consts"]).then_inc(const_in, 16)
            for l in every:
                win = w_in(l).rearrange("(k p) n -> k p n", p=P)
                for c, col in enumerate(COLS[l]):
                    for q in range(4):
                        load(Unit(U_A[l] + 4 * c + q), win[2 * q, :, col:col + CH], win[2 * q + 1, :, col:col + CH], False)
                wo = w_out(l).rearrange("(k p) n -> k p n", p=P)
                for i, k in enumerate(out_order(l)):
                    load(Unit(U_B[l] + i), wo[k, :, 0:CH], wo[k, :, CH:D], False)
                for c in range(2):
                    ffn_chunk(l, c, 0, U_C[l] + 4 * c)
                with sp.Fori(0, (NC - 2) // LOOP) as j:
                    for r in range(LOOP):
                        ffn_chunk(l, j * LOOP + (2 + r), j, U_C[l] + 4 * (2 + r))
                wd = w_down(l).rearrange("(k p) n -> k p n", p=P)
                for k in range(KF):
                    load(Unit(U_D[l] + k), wd[k, :, 0:CH], wd[k, :, CH:D], False)
            for t in range(NT):
                sp.wait_ge(x_ready.sem, x_ready.at(NB - 1, t))
                sp.dma_start(out[0, P * t:P * (t + 1), :], x[:, t, :]).then_inc(out_done, 16)
            sp.wait_ge(out_done, 16 * NT)

        @block.tensor
        def _(pe):
            def three_passes(bank, hi, lo, v, part, first, last):
                wh, wl = w_hi[:, v.slot, part], w_lo[:, v.slot, part]
                nc.tensor.matmul(ps[:, bank, :], hi, wh, start=first, stop=False)
                nc.tensor.matmul(ps[:, bank, :], hi, wl, start=False, stop=False)
                return nc.tensor.matmul(ps[:, bank, :], lo, wh, start=False, stop=last)

            def in_unit(v, q, bank, t):
                tok = slice(P * t, P * (t + 1))
                for i in range(2):
                    k = 2 * q + i
                    mm = three_passes(bank, a_hi[:, k, tok], a_lo[:, k, tok], v,
                                      slice(CH * i, CH * (i + 1)), k == 0, k == KD - 1)
                return mm

            def rows_unit(v, hi, lo, first, last, tiles):
                pe.wait_ge(w_low, v.n + 1)
                for t in tiles:
                    tok = slice(P * t, P * (t + 1))
                    for h in range(2):
                        mm = three_passes(2 * t + h, hi[:, tok], lo[:, tok], v, slice(CH * h, CH * (h + 1)), first, last)
                return mm

            def joint_chunk(units, c, banks, free_bank, hook):
                for t in range(NT):
                    free_bank(c, t)
                for q, v in enumerate(units):
                    pe.wait_ge(w_low, v.n + 1)
                    mm = in_unit(v, q, banks[0], 0)
                    if q == 3:
                        mm.then_inc(acc_done, 1)
                    in_unit(v, q, banks[1], 1).then_inc(w_used, 1)
                    hook(c, q)

            def first_chunks(l, phase, u0, banks, free_bank, hook):
                kk = 2 * l + (phase == "C")
                for t in range(NT):
                    pe.wait_ge(x_low.sem, x_low.at(kk, 2 * t + 1))
                    for c in range(2):
                        free_bank(c, t)
                        for q in range(4):
                            v = Unit(u0 + 4 * c + q)
                            pe.wait_ge(w_low, v.n + 1)
                            mm = in_unit(v, q, banks[c][t], t)
                            if t == 1:
                                mm.then_inc(w_used, 1)
                            elif q == 3:
                                mm.then_inc(acc_done, 1)
                            if t == 0 and c == 1 and q == 2 and kk > 0:
                                turn_x(kk, 1)
                            if t == 1:
                                hook(c, q)

            def out_units(l, units, t):
                for i in units:
                    k = out_order(l)[i]
                    if t == 1 and i == KD - 1:
                        turn_x(2 * l + 1, 0)
                    mm = rows_unit(Unit(U_B[l] + i), h_hi[:, k, :], h_lo[:, Y_LO + k, :], i == 0, i == KD - 1, (t,))
                    if t == 1:
                        mm.then_inc(w_used, 1)
                    elif i == KD - 1:
                        mm.then_inc(acc_done, 1)

            def down(l):
                joint = KF - KD
                pe.wait_ge(glu_done, glu_at(l, NC - 2, 1))
                for k in range(joint):
                    if k == 2:
                        turn_ffn(l, NC - 1, FFN_BUF[(NC - 1) % LOOP])
                    if k % 2 == 0:
                        pe.wait_ge(h_low.sem, h_low.at(l, k // 2))
                    rows_unit(Unit(U_D[l] + k), h_hi[:, k, :], h_lo[:, k, :], k == 0, False, (0, 1)).then_inc(w_used, 1)
                for t in range(NT):
                    for k in range(joint, KF):
                        if t == 0 and k % 2 == 0:
                            pe.wait_ge(h_low.sem, h_low.at(l, k // 2))
                        if t == 1 and k == KF - 1 and l + 1 < len(LAYERS):
                            turn_x(2 * l + 2, 0)
                        mm = rows_unit(Unit(U_D[l] + k), h_hi[:, k, :], h_lo[:, k, :], False, k == KF - 1, (t,))
                        if t == 1:
                            mm.then_inc(w_used, 1)
                        elif k == KF - 1:
                            mm.then_inc(acc_done, 1)

            def turn_x(kk, t):
                if kk == 0:
                    pe.wait_ge(x_in[t], 16)
                    pe.wait_ge(const_in, 16)
                else:
                    pe.wait_ge(x_ready.sem, x_ready.at(kk - 1, t))
                src = nbuf[:, :] if kk > 0 and pre[kk - 1] else x[:, t, :]
                for h in range(2):
                    for b in range(4):
                        tr = nc.tensor.transpose(tb[:, h, P * b:P * (b + 1)],
                                                 src[:, CH * h + P * b:CH * h + P * (b + 1)], ident)
                    tr.then_inc(x_turned.sem, 1)

            def turn_blocks(bank, src, col, st):
                for b in range(2):
                    for t in range(NT):
                        tr = nc.tensor.transpose(tb[:, bank, SEQ * b + P * t:SEQ * b + P * (t + 1)],
                                                 src[:, t, col + P * b:col + P * (b + 1)], ident)
                tr.then_inc(st.sem, 1)

            def turn_tile(bank, src, st):
                for b in range(4):
                    tr = nc.tensor.transpose(ps[:, bank, P * b:P * (b + 1)], src[:, P * b:P * (b + 1)], ident)
                tr.then_inc(st.sem, 1)

            def tiny(l, bank, st):
                c0, w = TINY[l]
                pe.wait_ge(tiny_done, 1)
                for t in range(NT):
                    tok = slice(P * t, P * (t + 1))
                    o = tb[:, bank, w * t:w * (t + 1)]
                    for k in range(KD):
                        wh, wl = tiny_hi[:, k, c0:c0 + w], tiny_lo[:, k, c0:c0 + w]
                        nc.tensor.matmul(o, a_hi[:, k, tok], wh, start=(k == 0), stop=False)
                        nc.tensor.matmul(o, a_hi[:, k, tok], wl, start=False, stop=False)
                        mm = nc.tensor.matmul(o, a_lo[:, k, tok], wh, start=False, stop=(k == KD - 1))
                mm.then_inc(st.sem, 1)

            def even_hook(c, q):
                if (c, q) == (3, 1):
                    pe.wait_ge(a_out, out_at(0, 1, 1))
                    for i in range(2):
                        turn_blocks(i, e_pc, 2 * P * i, e_turned)
                    for i in range(2):
                        turn_blocks(2 + i, e_pv, 2 * P * i, e_turned)

            def even_rest():
                for i in range(2):
                    pe.wait_ge(a_out, out_at(0, 2, 1))
                    pe.wait_ge(e_act.sem, e_act.at(0, i))
                    turn_blocks(i, e_pu, 2 * P * i, e_turned)
                for i in range(2):
                    pe.wait_ge(a_out, out_at(0, 3, 1))
                    pe.wait_ge(e_dve.sem, e_dve.at(0, i))
                    turn_blocks(2 + i, e_pb, 2 * P * i, e_turned)
                pe.wait_ge(e_pooled.sem, e_pooled.at(0, 0))
                pe.wait_ge(e_act.sem, e_act.at(0, 3))
                pe.wait_ge(params_in, PARAMS)
                for i in range(2):
                    for g in range(2 * i, 2 * i + 2):
                        mm = nc.tensor.matmul(tb[:, i, SEQ * (g % 2):SEQ * (g % 2 + 1)], w_grp[:, g, :], e_pool[:, g, :],
                                              start=True, stop=True)
                    mm.then_inc(e_turned.sem, 1)

            def odd_hook(c, q):
                if (c, q) == (0, 1):
                    tiny(1, 2, o_fsum)
                if (c, q) == (2, 0):
                    pe.wait_ge(o_gated.sem, o_gated.at(1, 0))
                    for i in range(2):
                        turn_blocks(i, o_d1, 2 * P * i, o_turned)
                if (c, q) == (2, 3):
                    pe.wait_ge(o_flog.sem, o_flog.at(1, 0))
                    tri = const[:, C_TRI:C_TRI + P]
                    nc.tensor.matmul(tb[0:GATES, 3, 0:SEQ], o_f[:, 0, 0, :], const[:, C_TRI:C_TRI + SEQ], start=True, stop=False)
                    nc.tensor.matmul(tb[0:GATES, 3, P:SEQ], o_f[:, 0, 1, :], tri, start=False, stop=True).then_inc(o_fcum.sem, 1)
                if (c, q) == (3, 2):
                    pe.wait_ge(o_cumT.sem, o_cumT.at(1, 0))
                    pe.wait_ge(a_out, out_at(1, 2, 1))
                    turn_qk(1, 0)
                if (c, q) == (4, 1):
                    pe.wait_ge(a_out, out_at(1, 3, 1))
                    pe.wait_ge(q_out.sem, q_out.at(1, 1))
                    turn_qk(1, 1)

            def odd_rest():
                for i in range(2):
                    pe.wait_ge(o_padded.sem, o_padded.at(1, i))
                attention(1)
                turn_y(1, shared, 0)
                for t in range(NT):
                    pe.wait_ge(y_low.sem, y_low.at(1, t))
                    pe.wait_ge(shared.sem, shared.at(1, t))
                    out_units(1, range(4), t)
                pe.wait_ge(o_conv.sem, o_conv.at(1, 0))
                for t in range(NT):
                    for b in range(4):
                        tr = nc.tensor.transpose(tb[:, 2 + t, P * b:P * (b + 1)], o_acc[:, b, P * t:P * (t + 1)], ident)
                    tr.then_inc(o_back.sem, 1)
                for t in range(NT):
                    pe.wait_ge(o_normed.sem, o_normed.at(1, t))
                    turn_tile(y_part(1, 2 + t)[2], o_z[:, t, :], y_turned)
                for t in range(NT):
                    pe.wait_ge(y_low.sem, y_low.at(1, 2 + t))
                    out_units(1, range(4, KD), t)

            def hyb_hook(l):
                def hook(c, q):
                    if (c, q) == (0, 1):
                        tiny(l, 0, l_sum)
                    if (c, q) == (1, 1):
                        pe.wait_ge(l_out.sem, l_out.at(l, 0))
                        for t in range(NT):
                            tr = nc.tensor.transpose(tb[0:RANK, 1, P * t:P * (t + 1)], g_low[:, t, :], ident)
                        tr.then_inc(l_turned.sem, 1)
                    if (c, q) == (1, 3):
                        pe.wait_ge(l_outT.sem, l_outT.at(l, 0))
                        for b in range(2):
                            mm = nc.tensor.matmul(tb[:, 2, SEQ * b:SEQ * (b + 1)], w_up[:, l - 2, P * b:P * (b + 1)], g_lowT[:, :],
                                                  start=True, stop=True)
                        mm.then_inc(z_done.sem, 1)
                        pe.wait_ge(a_out, out_at(l, 0, 1))
                        for i in range(2):
                            turn_blocks(i, g_pqk, 2 * P * i, gqk_turned)
                    if (c, q) == (4, 0):
                        pe.wait_ge(z_out.sem, z_out.at(l, 0))
                        pe.wait_ge(roped.sem, roped.at(l, 0))
                        turn_qk(l, 0)
                    if (c, q) == (5, 0):
                        pe.wait_ge(q_out.sem, q_out.at(l, 1))
                        turn_qk(l, 1)
                    if (c, q) in LEVEL_STEP:
                        level(l, LEVEL_STEP.index((c, q)))
                return hook

            def level(l, n):
                if n:
                    pe.wait_ge(g_scaled.sem, g_scaled.at(l, n - 1))
                    pe.wait_ge(g_kept.sem, g_kept.at(l, n - 1))
                else:
                    pe.wait_ge(gqk_out.sem, gqk_out.at(l, 1))
                for h in range(GLA_H):
                    r, b = level_rows(h)
                    for t in range(1 if n == 1 else NT):
                        tok = slice(P * t, P * (t + 1))
                        if n == 0:
                            ks, qs, at, w = g_qkT[r, 2 + b, tok], g_qkT[r, b, tok], kept_at(h, t) % 4, P
                        elif n == 1:
                            ks, qs, at, w = g_x[r, 1, b, 0:P], g_x[r, 1, b, P:SEQ], far_at(h) % 2, P
                        else:
                            ks, at, w = g_x[r, n % 2, b, tok], kept_at(h, t) % 4, P // 2
                            qs = right(ks, LEVELS[n - 1])
                        mm = nc.tensor.matmul(tb[:, h % 2, w * at:w * (at + 1)], ks, qs, start=True, stop=True)
                mm.then_inc(g_pair.sem, 1)

            def hyb_rest(l):
                attention(l)
                pe.wait_ge(shared.sem, shared.at(l, 0))
                pe.wait_ge(y_low.sem, y_low.at(l, 0))
                out_units(l, range(4), 0)
                turn_y(l, a_normed, 2)
                pe.wait_ge(shared.sem, shared.at(l, 1))
                pe.wait_ge(y_low.sem, y_low.at(l, 1))
                out_units(l, range(2), 1)
                pe.wait_ge(y_low.sem, y_low.at(l, 2))
                out_units(l, range(4, KD), 0)
                pe.wait_ge(y_low.sem, y_low.at(l, 3))
                out_units(l, range(2, KD), 1)

            def linear_values(l):
                pe.wait_ge(g_kept.sem, g_kept.at(l, NL))
                pe.wait_ge(a_out, out_at(l, NA[l] - 1, 1))
                for t in range(NT):
                    for h in range(GLA_H):
                        cols = slice(GLA_DV * h, GLA_DV * (h + 1))
                        if t == 1:
                            nc.tensor.matmul(acc[:, 3, cols], g_far[:, far_at(h), :], g_v[:, 0, cols], start=True, stop=False)
                        mm = nc.tensor.matmul(acc[:, 1 + 2 * t, cols], g_att[:, kept_at(h, t), :], g_v[:, t, cols],
                                              start=(t == 0), stop=True)
                    mm.then_inc(g_done.sem, 1)

            def turn_qk(l, part):
                for i in range(2):
                    turn_blocks(2 + i, p_qk, CH * part + 2 * P * i, qk_turned)

            def head_logits(l, h):
                bank, r, b = h % 2, slice(HD * (h % 2), HD * (h % 2 + 1)), h // 2
                if h >= 2:
                    pe.wait_ge(weighed.sem, weighed.at(l, h - 2))
                near, wide, late_half = tb[:, bank, 0:P], tb[:, bank, P:3 * P], tb[:, bank, 2 * P:3 * P]
                every_key = tb[:, bank, 0:3 * P]
                if l == 1:
                    one_hot = ident_r[0:GATES, h:h + 1].broadcast_to([GATES, P])
                    nc.tensor.matmul(every_key, one_hot, o_cum[:, 0, :], start=True, stop=False)
                    nc.tensor.matmul(every_key, one_hot, o_cum[:, 1, :], start=False, stop=False)
                    for part in (near, late_half):
                        nc.tensor.matmul(part, ident_r[:, :], bias_hi[:, 0:P], start=False, stop=False)
                else:
                    nc.tensor.matmul(every_key, ident_r[:, :], bias_hi[:, P:4 * P], start=True, stop=False)
                    nc.tensor.matmul(every_key, ident_r[:, :], bias_lo[:, :], start=False, stop=False)
                nc.tensor.matmul(near, qT[r, b, 0:P], kT[r, b, 0:P], start=False, stop=False)
                nc.tensor.matmul(wide, qT[r, b, P:SEQ], kT[r, b, :], start=False, stop=True).then_inc(logits.sem, 1)

            def head_turn(l, h):
                pe.wait_ge(weighed.sem, weighed.at(l, h))
                if h >= 2:
                    pe.wait_ge(p_out.sem, p_out.at(l, h - 2))
                for i in range(3):
                    tr = nc.tensor.transpose(tb[:, 2 + h % 2, P * i:P * (i + 1)], probs[:, h % 2, P * i:P * (i + 1)], ident)
                tr.then_inc(p_turned.sem, 1)

            def head_values(l, h):
                pe.wait_ge(p_out.sem, p_out.at(l, h))
                cols = slice(HD * h, HD * (h + 1))
                pT = probsT[:, h % 2, :]
                nc.tensor.matmul(acc[:, 0, cols], pT[:, 0:P], p_v[:, 0, cols], start=True, stop=True)
                nc.tensor.matmul(acc[:, 2, cols], pT[:, P:2 * P], p_v[:, 0, cols], start=True, stop=False)
                nc.tensor.matmul(acc[:, 2, cols], pT[:, 2 * P:3 * P], p_v[:, 1, cols], start=False,
                                 stop=True).then_inc(attended.sem, 1)

            def attention(l):
                pe.wait_ge(q_out.sem, q_out.at(l, 1))
                pe.wait_ge(k_out.sem, k_out.at(l, 1))
                if LAYERS[l] == "hyb":
                    pe.wait_ge(g_kept.sem, g_kept.at(l, NL))
                head_logits(l, 0)
                head_logits(l, 1)
                if LAYERS[l] == "hyb":
                    linear_values(l)
                else:
                    pe.wait_ge(a_out, out_at(l, NA[l] - 1, 1))
                for h in range(HEADS):
                    head_turn(l, h)
                    if h + 2 < HEADS:
                        head_logits(l, h + 2)
                    if h:
                        head_values(l, h - 1)
                    if LAYERS[l] == "hyb" and h == HEADS - 2:
                        turn_y(l, g_normed, 0)
                head_values(l, HEADS - 1)

            def turn_y(l, ready, first):
                src = g_o if ready is g_normed else y_tok
                for t in range(NT):
                    pe.wait_ge(ready.sem, ready.at(l, t))
                    turn_tile(y_part(l, first + t)[2], src[:, t, :], y_turned)

            def turn_ffn(l, c, buf):
                pe.wait_ge(glu_done, glu_at(l, c, 1))
                if not isinstance(c, int) or c > 0:
                    pe.wait_ge(h_low.sem, c + h_low.at(l, 0) - 1)
                for b in range(2):
                    for t in range(NT):
                        tr = nc.tensor.transpose(tb[:, 0, SEQ * b + P * t:SEQ * b + P * (t + 1)],
                                                 glu[:, buf, t, P * b:P * (b + 1)], ident)
                tr.then_inc(h_turned.sem, 1)

            turn_x(0, 0)
            pe.wait_ge(x_low.sem, x_low.at(0, 1))
            turn_x(0, 1)
            pe.wait_ge(params_in, PARAMS)
            pe.wait_ge(x_low.sem, x_low.at(0, 2))
            for b in range(4):
                tr = nc.tensor.transpose(tb[:, 0, N_ROWS * b:N_ROWS * (b + 1)], prow[:, P * b:P * (b + 1)], ident[0:N_ROWS, 0:N_ROWS])
            tr.then_inc(params_turned, 1)

            for l in every:
                hook = {"even": even_hook, "odd": odd_hook, "hyb": hyb_hook(l)}[LAYERS[l]]

                def free_in(c, t):
                    if c >= 2:
                        pe.wait_ge(a_out, out_at(l, c - 2, t))
                    elif l > 0:
                        pe.wait_ge(acc_read.sem, acc_read.at(2 * l - 1, t))

                first_chunks(l, "A", U_A[l], IN_BANK, free_in, hook)
                for c in range(2, NA[l]):
                    joint_chunk([Unit(U_A[l] + 4 * c + q) for q in range(4)], c, IN_BANK[c % 2], free_in, hook)
                if LAYERS[l] == "even":
                    even_rest()
                    pe.wait_ge(e_low.sem, e_low.at(l, 5))
                    for t in range(NT):
                        out_units(l, range(KD), t)
                elif LAYERS[l] == "odd":
                    odd_rest()
                else:
                    hyb_rest(l)

                def free_ffn(c, t):
                    if isinstance(c, int):
                        pe.wait_ge(acc_read.sem, acc_read.at(2 * l, t))
                    else:
                        pe.wait_ge(glu_done, c * 2 + (2 * NC * l + t - 3))

                first_chunks(l, "C", U_C[l], FFN_BANK, free_ffn, lambda c, q: turn_ffn(l, 0, 0) if (c, q) == (1, 1) else None)
                with pe.Fori(0, (NC - 2) // LOOP) as j:
                    for r in range(LOOP):
                        units = [Unit(U_C[l] + 4 * (2 + r) + q, j) for q in range(4)]
                        before = FFN_BUF[(1 + r) % LOOP]
                        joint_chunk(units, j * LOOP + (2 + r), FFN_BANK[(2 + r) % LOOP], free_ffn,
                                    lambda c, q: turn_ffn(l, j * LOOP + (1 + r), before) if q == 1 else None)

                down(l)
        @block.scalar
        def _(act):
            chain = Chain(act, act_step)
            fed = [0]

            def high(v):
                act.wait_ge(raw_in[v.raw], v.loads * 32)
                if not v.fresh:
                    act.wait_ge(w_used, v.n - N_W + 1)
                nc.scalar.activation(w_hi[:, v.slot, :], raw[:, v.raw, :], ACT.Copy).then_inc(w_high, 1)

            def feed(n):
                for u in range(fed[0], min(n, U_END)):
                    high(Unit(u))
                fed[0] = max(fed[0], min(n, U_END))

            def x_split(kk, t):
                for h in range(2):
                    act.wait_ge(x_turned.sem, x_turned.at(kk, 2 * t + h))
                    nc.scalar.activation(a_hi[:, 4 * h:4 * h + 4, P * t:P * (t + 1)],
                                         tb[:, h, :].rearrange("p (b n) -> p b n", b=4), ACT.Copy).then_inc(x_high.sem, 1)

            def load_rows(k):
                if k >= NB:
                    return
                if k:
                    act.wait_ge(x_ready.sem, x_ready.at(k - 1, 1))
                for slot, col, row in norm_rows(k):
                    act.dma_start(rows[:, slot, col:col + row.shape[0]], row.partition_broadcast(P)).then_inc(rows_in, 16)

            def boundary(k, t):
                l, ffn = divmod(k, 2)
                def settle(before):
                    if pre[k]:
                        act.wait_ge(spread2.sem, spread2.at(k, before))
                    elif not is_ln[k]:
                        act.wait_ge(squared.sem, squared.at(k, before))

                if t == 1:
                    settle(0)
                if not is_ln[k]:
                    tile_done(act, t, l, "D" if ffn else "B")
                    nc.scalar.activation(squares[:, :], acc[:, 2 * t:2 * t + 2, :].rearrange("p h n -> p (h n)"), ACT.Square,
                                         accum_out=ssq[:, t:t + 1]).then_inc(squared.sem, 1)
                if pre[k]:
                    act.wait_ge(x_sum.sem, x_sum.at(k, t))
                    if not is_ln[k]:
                        act.wait_ge(squared.sem, squared.at(k, t))
                    nc.scalar.activation(squares[:, :], x[:, t, :], ACT.Square,
                                         accum_out=ssq2[:, t:t + 1]).then_inc(spread2.sem, 1)
                if t == 1:
                    settle(1)

            def after_boundary(k, end):
                boundary(k, 0)
                feed(end + 4)
                if k + 1 < NB:
                    x_split(k + 1, 0)
                feed(end + 8)
                boundary(k, 1)

            def chunk_out(l, c, t):
                tile_done(act, t, l, "A", c)
                bank, f = acc[:, IN_BANK[c % 2][t], :], ACT.Copy
                if l == 0:
                    dst = (e_pc, e_pv, e_pu, e_pb)[c][:, t, :]
                elif l == 1:
                    dst = (o_d1[:, t, :], o_d2[:, t, :], p_qk[:, t, 0:CH], p_qk[:, t, CH:D], p_v[:, t, :])[c]
                    f = ACT.Sigmoid if c == 1 else f
                else:
                    dst = (g_pqk[:, t, :], p_qk[:, t, 0:CH], p_qk[:, t, CH:D], p_v[:, t, :], g_v[:, t, :], g_r[:, t, :])[c]
                    f = ACT.Silu if c == 5 else f
                nc.scalar.activation(dst, bank, f).then_inc(a_out, 1)

            def blocks(bank):
                return tb[:, bank, :].rearrange("p (b n) -> p b n", b=2)

            def even_rest():
                act.wait_ge(e_turned.sem, e_turned.at(0, 1))
                for i in range(2):
                    nc.scalar.activation(e_cT[:, 2 * i:2 * i + 2, :], blocks(i), ACT.Copy).then_inc(e_act.sem, 1)
                for i in range(2):
                    act.wait_ge(e_turned.sem, e_turned.at(0, 4 + i))
                    nc.scalar.activation(e_u[:, 2 * i:2 * i + 2, PAD:], blocks(i), ACT.Copy).then_inc(e_act.sem, 1)
                for i in range(2):
                    act.wait_ge(e_dve.sem, e_dve.at(0, 2 + i))
                    nc.scalar.activation(h_hi[:, 2 * i:2 * i + 2, :], e_y[:, 2 * i:2 * i + 2, :], ACT.Copy).then_inc(e_high.sem, 1)
                for g in range(4):
                    act.wait_ge(e_turned.sem, e_turned.at(0, 8 + g // 2))
                    nc.scalar.activation(h_hi[:, 4 + g, :], tb[:, g // 2, SEQ * (g % 2):SEQ * (g % 2 + 1)], ACT.Copy,
                                         scale=pcol[:, g, R_PSCALE:R_PSCALE + 1]).then_inc(e_high.sem, 1)

            def odd_step(c, end):
                if c == 1:
                    log_sigmoid_part(o_f[:, 0], o_f[:, 1], o_f[:, 2], o_f[:, 3], o_fbiased, o_soft, 1)
                    act.wait_ge(o_turned.sem, o_turned.at(1, 1))
                    for i in range(2):
                        nc.scalar.activation(o_pad[:, 2 * i:2 * i + 2, PADT:], blocks(i), ACT.Copy).then_inc(o_padded.sem, 1)
                if c == 2:
                    act.wait_ge(o_fcum.sem, o_fcum.at(1, 0))
                    chain.step(nc.scalar.activation(o_cum[:, 0, 0:P], tb[0:GATES, 3, 0:P], ACT.Copy))
                    nc.scalar.activation(o_cum[:, 0, P:3 * P], tb[0:GATES, 3, 0:SEQ], ACT.Copy).then_inc(o_cumhigh.sem, 1)
                if c == 3:
                    feed(end - 2)
                    q_part(1)
                feed(end)

            def log_sigmoid_part(z, z_abs, e, soft, ready, done, l):
                act.wait_ge(ready.sem, ready.at(l, 0))
                chain.step(nc.scalar.activation(z_abs, z, ACT.Abs))
                chain.settle()
                chain.step(nc.scalar.activation(e, z_abs, ACT.Exp, scale=-1.0))
                chain.settle()
                nc.scalar.activation(soft, e, ACT.Ln, bias=1.0).then_inc(done.sem, 1)

            def odd_rest():
                attention(1)
                split_y(1, (0, 1))
                for t in range(NT):
                    act.wait_ge(y_turned.sem, y_turned.at(1, 2 + t))
                    for b in range(4):
                        ins = nc.scalar.activation(o_y[:, t, b, :], tb[:, t, P * b:P * (b + 1)], ACT.Silu,
                                                   scale=pcol[:, b, R_CNG:R_CNG + 1], bias=pcol[:, b, R_CNB:R_CNB + 1])
                        n = chain.step(ins) if b < 3 else None
                    ins.then_inc(o_silu.sem, 1)
                for t in range(NT):
                    chain.settle()
                    act.wait_ge(o_silu.sem, o_silu.at(1, t))
                    nc.scalar.activation(h_hi[:, 4:8, P * t:P * (t + 1)], o_y[:, t, :, :], ACT.Copy).then_inc(y_high.sem, 1)

            def hyb_step(l, c, end):
                if c == 0:
                    act.wait_ge(l_sum.sem, l_sum.at(l, 0))
                    nc.scalar.activation(g_low[:, :, :], tb[:, 0, 0:NT * RANK].rearrange("p (t r) -> p t r", t=NT),
                                         ACT.Copy).then_inc(l_out.sem, 1)
                    feed(end)
                    act.wait_ge(l_turned.sem, l_turned.at(l, 0))
                    nc.scalar.activation(g_lowT[:, :], tb[0:RANK, 1, 0:SEQ], ACT.Copy).then_inc(l_outT.sem, 1)
                if c == 1:
                    act.wait_ge(z_done.sem, z_done.at(l, 0))
                    for b in range(2):
                        col = 2 * (l - 2) + b
                        ins = nc.scalar.activation(g_z[:, b, :], tb[:, 2, SEQ * b:SEQ * (b + 1)], ACT.Identity,
                                                   bias=pcol[:, col, R_GLAB:R_GLAB + 1])
                        if b == 0:
                            chain.step(ins)
                    ins.then_inc(z_out.sem, 1)
                    chain.settle()
                    log_sigmoid_part(g_z[:, :, :], g_e[:, :, :], g_b[:, :, :], g_e[:, :, :], z_out, z_log, l)
                    for i in range(2):
                        act.wait_ge(gqk_turned.sem, gqk_turned.at(l, 1))
                        nc.scalar.activation(g_qkT[:, 2 * i:2 * i + 2, :], blocks(i), ACT.Copy,
                                             scale=GLA_SCALE if i == 0 else 1.0).then_inc(gqk_out.sem, 1)
                for n in LEVELS_AFTER.get(c, ()):
                    level_decay(l, n)
                    if n == 4:
                        q_part(l)
                    feed(fed[0] + 1)
                feed(end)

            def level_decay(l, n):
                act.wait_ge(g_diff.sem, g_diff.at(l, n))
                if n:
                    act.wait_ge(g_scaled.sem, g_scaled.at(l, n - 1))
                nc.scalar.activation(g_e[:, :, :], g_z[:, :, :], ACT.Exp, scale=1.0 / GLA_TAU).then_inc(g_exp.sem, 1)

            def hyb_rest(l):
                attention(l)
                split_y(l, (0, 1))
                for t in range(NT):
                    act.wait_ge(shared.sem, shared.at(l, t))
                    nc.scalar.activation(squares[:, CH * t:CH * (t + 1)], y_tok[:, t, :], ACT.Square,
                                         accum_out=a_ssq[:, t:t + 1]).then_inc(a_spread.sem, 1)
                split_y(l, (2, 3))
                act.wait_ge(a_spread.sem, a_spread.at(l, 1))

            def linear_squares(l):
                for t in range(NT):
                    act.wait_ge(g_done.sem, g_done.at(l, t))
                    for h in range(GLA_H):
                        ins = nc.scalar.activation(nbuf[:, CH * t + P * h:CH * t + P * (h + 1)],
                                                   acc[:, 1 + 2 * t, GLA_DV * h:GLA_DV * (h + 1)], ACT.Square,
                                                   accum_out=g_ssq[:, t, h:h + 1])
                ins.then_inc(g_spread.sem, 1)

            def q_part(l):
                for i in range(2):
                    act.wait_ge(qk_turned.sem, qk_turned.at(l, i))
                    nc.scalar.activation(qT[:, 2 * i:2 * i + 2, :], blocks(2 + i), ACT.Copy, scale=-SCALE).then_inc(q_out.sem, 1)

            def attention(l):
                for h in range(HEADS):
                    bank = tb[:, h % 2, :]
                    act.wait_ge(lows.sem, lows.at(l, h))
                    if h >= 2:
                        act.wait_ge(p_turned.sem, p_turned.at(l, h - 2))
                    nc.scalar.activation(probs[:, h % 2, 0:P], bank[:, 0:P], ACT.Exp, scale=-1.0,
                                         bias=low_of[:, h % 2, 0:1], accum_out=total[:, 0, h:h + 1])
                    nc.scalar.activation(probs[:, h % 2, P:3 * P], bank[:, P:3 * P], ACT.Exp, scale=-1.0,
                                         bias=low_of[:, h % 2, 1:2], accum_out=total[:, 1, h:h + 1]).then_inc(weighed.sem, 1)
                    if LAYERS[l] == "hyb" and h == 2:
                        linear_squares(l)

            def split_y(l, which):
                for i in which:
                    b, t, bank = y_part(l, i)
                    act.wait_ge(y_turned.sem, y_turned.at(l, i))
                    nc.scalar.activation(h_hi[:, b:b + 4, P * t:P * (t + 1)],
                                         ps[:, bank, :].rearrange("p (b n) -> p b n", b=4), ACT.Copy).then_inc(y_high.sem, 1)

            def silu_part(l, c, r, t):
                tile_done(act, t, l, "C", c)
                if not isinstance(c, int):
                    act.wait_ge(glu_done, c * 2 + (2 * NC * l + t - 1))
                nc.scalar.activation(silu[:, FFN_BUF[r], t, :], ps[:, FFN_BANK[r][t], 0:FC], ACT.Silu).then_inc(silu_done, 1)

            def ffn_split(l, c):
                act.wait_ge(h_turned.sem, c + h_turned.at(l, 0))
                dst = h_hi[:, :, :].rearrange("p (c b) n -> p c b n", b=2)[:, c, :, :]
                nc.scalar.activation(dst, blocks(0), ACT.Copy).then_inc(h_high.sem, 1)

            for row, src in ((R_EVCONV, a["ev_conv_w"][0]), (R_PSCALE, a["ev_pool_scale"]), (R_DW, a["od_dw_w"][0]),
                             (R_DWB, a["od_dw_b"]), (R_CNG, a["od_cn_g"]), (R_CNB, a["od_cn_b"]),
                             (R_GLAB, a["gla_b_gate_2"].rearrange("(o l) n -> o (l n)", o=1))):
                act.dma_start(prow[row:row + src.shape[0], :], src).then_inc(params_in, 16)
            for l, col in ((1, OD_F), (2, HY_LOW), (3, HY_LOW)):
                c0, w = TINY[l]
                act.dma_start(tiny_raw[:, :, c0:c0 + w],
                              w_in(l)[:, col:col + w].rearrange("(k p) n -> p k n", p=P)).then_inc(params_in, 16)
            act.dma_start(fbias[:, :], a["od_forget_b"][0].partition_broadcast(P)).then_inc(params_in, 16)
            act.dma_start(w_up[:, :, :], a["gla_w_gate_up_2"].rearrange("l k n -> k l n")).then_inc(params_in, 16)
            act.dma_start(w_grp[:, :, :], a["ev_pool_w"][0].rearrange("g c d -> c g d")).then_inc(params_in, 16)
            load_rows(0)
            for t in range(NT):
                x_split(0, t)
            feed(4)
            act.wait_ge(params_in, PARAMS)
            nc.scalar.activation(ident_r[:, :], ident, ACT.Copy)
            nc.scalar.activation(bias_hi[:, :], const[:, C_CAUSAL:C_CAUSAL + 4 * P], ACT.Copy)
            nc.scalar.activation(tiny_hi[:, :, :], tiny_raw[:, :, :], ACT.Copy).then_inc(tiny_high, 1)
            act.wait_ge(params_turned, 1)
            nc.scalar.activation(pcol[:, :, :], tb[:, 0, 0:4 * N_ROWS].rearrange("p (b r) -> p b r", b=4), ACT.Copy).then_inc(params_out, 1)
            act.wait_ge(params_out, 1)
            feed(N_W)
            for l in every:
                order = [(0, 0), (1, 0), (0, 1), (1, 1)] + [(c, t) for c in range(2, NA[l]) for t in range(NT)]
                for c, t in order:
                    chunk_out(l, c, t)
                    if (c, t) == (0, 0) and l > 0:
                        x_split(2 * l, 1)
                    if t == 1:
                        if c == 1:
                            load_rows(2 * l) if l else None
                        end = U_A[l] + 4 * (c + 1) + N_W
                        if LAYERS[l] == "odd":
                            odd_step(c, end)
                        elif LAYERS[l] == "hyb":
                            hyb_step(l, c, end)
                        else:
                            feed(end)
                if LAYERS[l] == "even":
                    even_rest()
                elif LAYERS[l] == "odd":
                    odd_rest()
                else:
                    hyb_rest(l)
                after_boundary(2 * l, U_C[l])
                silu_part(l, 0, 0, 0)
                feed(U_C[l] + N_W)
                x_split(2 * l + 1, 1)
                silu_part(l, 1, 1, 0)
                silu_part(l, 0, 0, 1)
                feed(U_C[l] + 4 + N_W)
                ffn_split(l, 0)
                silu_part(l, 1, 1, 1)
                feed(U_C[l] + 8 + N_W)
                load_rows(2 * l + 1)
                with act.Fori(0, (NC - 2) // LOOP) as j:
                    for r in range(LOOP):
                        c = j * LOOP + (2 + r)
                        ffn_split(l, j * LOOP + (1 + r))
                        for t in range(NT):
                            silu_part(l, c, (2 + r) % LOOP, t)
                        for q in range(4):
                            high(Unit(U_C[l] + 4 * (2 + r) + N_W + q, j))
                fed[0] += 4 * (NC - 2)
                ffn_split(l, NC - 1)
                feed(U_D[l] + KF - KD + N_W)
                after_boundary(2 * l + 1, U_D[l] + KF)
                feed(U_D[l] + KF + N_W)

        @block.vector
        def _(dve):
            chain = Chain(dve, dve_step)
            fed = [0]
            V = nc.vector

            def low(v):
                dve.wait_ge(w_high, v.n + 1)
                V.tensor_tensor(w_lo[:, v.slot, :], raw[:, v.raw, :], w_hi[:, v.slot, :].bitcast(F32), ALU.subtract).then_inc(w_low, 1)

            def feed(n):
                for u in range(fed[0], min(n, U_END)):
                    low(Unit(u))
                fed[0] = max(fed[0], min(n, U_END))

            def x_split(kk, t):
                for h in range(2):
                    dve.wait_ge(x_high.sem, x_high.at(kk, 2 * t + h))
                    part = slice(4 * h, 4 * h + 4), slice(P * t, P * (t + 1))
                    V.tensor_tensor(a_lo[:, part[0], part[1]], tb[:, h, :].rearrange("p (b n) -> p b n", b=4),
                                    a_hi[:, part[0], part[1]].bitcast(F32), ALU.subtract).then_inc(x_low.sem, 1)

            def boundary(k, t):
                l, ffn = divmod(k, 2)
                xt = x[:, t, :]
                dve.wait_ge(rows_in, rows_at(k))
                tile_done(dve, t, l, "D" if ffn else "B")
                if is_ln[k]:
                    for h in range(2):
                        xh = x[:, t, CH * h:CH * (h + 1)]
                        ins = V.scalar_tensor_tensor(xh, xh, ALPHA, acc[:, 2 * t + h, :], ALU.mult, ALU.add)
                        if h == 0:
                            chain.step(ins)
                    ins.then_inc(acc_read.sem, 1)
                    for h in range(2):
                        if h == 0:
                            chain.settle()
                        else:
                            dve.wait_ge(acc_read.sem, acc_read.at(k, t))
                        chain.step(V.bn_stats(bn[:, t, h, :], x[:, t, CH * h:CH * (h + 1)]))
                    chain.settle()
                    V.bn_aggr(mv[:, t, :], bn[:, t, :, :].rearrange("p h s -> p (h s)")).then_inc(spread.sem, 1)
                    dve.wait_ge(spread.sem, spread.at(k, t))
                    chain.step(V.scalar_tensor_tensor(xt, xt, mv[:, t, 0:1], rows[:, 0, :], ALU.subtract, ALU.mult))
                    chain.settle()
                    dve.wait_ge(scaled.sem, scaled.at(k, t))
                    ins = V.scalar_tensor_tensor(xt, xt, rstd[:, t:t + 1], rows[:, 1, :], ALU.mult, ALU.add)
                else:
                    if t == 1 and k + 1 < NB:
                        dve.wait_ge(x_turned.sem, x_turned.at(k + 1, 1))
                    dve.wait_ge(scaled.sem, scaled.at(k, t))
                    chain.settle()
                    V.scalar_tensor_tensor(nbuf[:, :], acc[:, 2 * t:2 * t + 2, :].rearrange("p h n -> p (h n)"), rstd[:, t:t + 1],
                                           rows[:, 0, :], ALU.mult, ALU.mult).then_inc(acc_read.sem, 1)
                    dve.wait_ge(acc_read.sem, acc_read.at(k, t))
                    ins = V.tensor_tensor(xt, xt, nbuf[:, :], ALU.add)
                if not pre[k]:
                    ins.then_inc(x_ready.sem, 1)
                    dve.wait_ge(x_ready.sem, x_ready.at(k, t))
                else:
                    ins.then_inc(x_sum.sem, 1)
                    dve.wait_ge(x_sum.sem, x_sum.at(k, t))
                    if is_ln[k] and t == 1:
                        dve.wait_ge(x_turned.sem, x_turned.at(k + 1, 1))
                    dve.wait_ge(scaled2.sem, scaled2.at(k, t))
                    V.scalar_tensor_tensor(nbuf[:, :], xt, rstd2[:, t:t + 1], pre_row(k), ALU.mult, ALU.mult).then_inc(x_ready.sem, 1)

            def after_boundary(k, end):
                boundary(k, 0)
                feed(end + 4)
                if k + 1 < NB:
                    x_split(k + 1, 0)
                feed(end + 8)
                boundary(k, 1)

            def blocks(bank):
                return tb[:, bank, :].rearrange("p (b n) -> p b n", b=2)

            def even_rest():
                for i in range(2):
                    dve.wait_ge(e_act.sem, e_act.at(0, i))
                    dve.wait_ge(e_turned.sem, e_turned.at(0, 3))
                    V.tensor_tensor(e_m[:, 2 * i:2 * i + 2, :], blocks(2 + i), e_cT[:, 2 * i:2 * i + 2, :], ALU.mult).then_inc(e_dve.sem, 1)
                dve.wait_ge(e_dve.sem, e_dve.at(0, 1))
                for tap in range(3):
                    chain.settle()
                    for b in range(4):
                        w = pcol[:, b, R_EVCONV + 2 - tap:R_EVCONV + 3 - tap]
                        if tap == 0:
                            chain.step(V.tensor_scalar(e_y[:, b, :], e_m[:, b, :], w, None, ALU.mult))
                        else:
                            chain.step(V.scalar_tensor_tensor(e_y[:, b, tap:], e_m[:, b, 0:SEQ - tap], w, e_y[:, b, tap:],
                                                              ALU.mult, ALU.add))
                dve.wait_ge(e_turned.sem, e_turned.at(0, 4))
                chain.step(V.memset(e_u[:, :, 0:PAD], 0.0))
                chain.step(V.memset(e_sA[:, :, 0:1], 0.0))
                dve.wait_ge(e_act.sem, e_act.at(0, 3))
                chain.settle()
                W = PAD + SEQ
                chain.step(V.tensor_tensor(e_sA[:, :, 1:W], e_u[:, :, 1:W], e_u[:, :, 0:W - 1], ALU.add))
                chain.settle()
                chain.step(V.tensor_tensor(e_sB[:, 1:4, 3:W], e_sA[:, 1:4, 3:W], e_sA[:, 1:4, 1:W - 2], ALU.add))
                chain.settle()
                chain.step(V.tensor_tensor(e_sA[:, 2:4, 7:W], e_sB[:, 2:4, 7:W], e_sB[:, 2:4, 3:W - 4], ALU.add))
                chain.settle()
                chain.step(V.tensor_tensor(e_sB[:, 3, 15:W], e_sA[:, 3, 15:W], e_sA[:, 3, 7:W - 8], ALU.add))
                chain.settle()
                sums = (e_sA, e_sB, e_sA, e_sB)
                for g in range(4):
                    chain.step(V.tensor_tensor(e_edge[:, g, :], sums[g][:, g, PAD:2 * PAD],
                                               const[:, C_POOL + PAD * g:C_POOL + PAD * (g + 1)], ALU.mult))
                    chain.step(V.scalar_tensor_tensor(e_pool[:, g, :], sums[g][:, g, PAD:], 1.0 / WINDOWS[g], e_u[:, g, PAD:],
                                                      ALU.mult, ALU.subtract))
                chain.settle()
                V.tensor_tensor(e_pool[:, :, 0:PAD], e_edge[:, :, :], e_u[:, :, PAD:2 * PAD], ALU.subtract).then_inc(e_pooled.sem, 1)
                for i in range(2):
                    dve.wait_ge(e_turned.sem, e_turned.at(0, 6 + i))
                    V.tensor_tensor(e_y[:, 2 * i:2 * i + 2, :], blocks(2 + i), e_y[:, 2 * i:2 * i + 2, :], ALU.mult).then_inc(e_dve.sem, 1)
                for i in range(2):
                    dve.wait_ge(e_high.sem, e_high.at(0, i))
                    V.tensor_tensor(h_lo[:, Y_LO + 2 * i:Y_LO + 2 * i + 2, :], e_y[:, 2 * i:2 * i + 2, :],
                                    h_hi[:, 2 * i:2 * i + 2, :].bitcast(F32), ALU.subtract).then_inc(e_low.sem, 1)
                for g in range(4):
                    dve.wait_ge(e_high.sem, e_high.at(0, 3 + 2 * (g // 2)))
                    V.scalar_tensor_tensor(h_lo[:, Y_LO + 4 + g, :], tb[:, g // 2, SEQ * (g % 2):SEQ * (g % 2 + 1)],
                                           pcol[:, g, R_PSCALE:R_PSCALE + 1], h_hi[:, 4 + g, :].bitcast(F32),
                                           ALU.mult, ALU.subtract).then_inc(e_low.sem, 1)

            taps = [(k, b) for k in range(TAPS) for b in range(4)]
            tap_step = {}

            def convolve(n):
                for _ in range(min(n, len(taps))):
                    k, b = taps.pop(0)
                    w, src = pcol[:, b, R_DW + k:R_DW + k + 1], o_pad[:, b, k:k + SEQ]
                    if k == 0:
                        ins = V.tensor_scalar(o_acc[:, b, :], src, w, pcol[:, b, R_DWB:R_DWB + 1], ALU.mult, ALU.add)
                    else:
                        chain.settle(tap_step[b])
                        ins = V.scalar_tensor_tensor(o_acc[:, b, :], src, w, o_acc[:, b, :], ALU.mult, ALU.add)
                    if taps:
                        tap_step[b] = chain.step(ins)
                    else:
                        ins.then_inc(o_conv.sem, 1)

            def odd_step(c, end):
                if c == 1:
                    dve.wait_ge(o_fsum.sem, o_fsum.at(1, 0))
                    V.tensor_tensor(o_f[:, 0, :, :], tb[:, 2, 0:NT * GATES].rearrange("p (t g) -> p t g", t=NT),
                                    fbias[:, :].unsqueeze(1).broadcast_to([P, NT, GATES]), ALU.add).then_inc(o_fbiased.sem, 1)
                    dve.wait_ge(a_out, out_at(1, 1, 1))
                    V.tensor_tensor(o_d1[:, :, :], o_d1[:, :, :], o_d2[:, :, :], ALU.mult).then_inc(o_gated.sem, 1)
                    feed(end)
                    dve.wait_ge(o_soft.sem, o_soft.at(1, 0))
                    z, soft = (o_f[:, i, :, :].rearrange("p t g -> p (t g)") for i in (0, 3))
                    V.scalar_tensor_tensor(z, z, 0.0, soft, ALU.min, ALU.subtract).then_inc(o_flog.sem, 1)
                    dve.wait_ge(o_turned.sem, o_turned.at(1, 1))
                    chain.step(V.memset(o_pad[:, :, 0:PADT], 0.0))
                    chain.settle()
                    dve.wait_ge(o_padded.sem, o_padded.at(1, 1))
                    convolve(8)
                if c == 2:
                    dve.wait_ge(o_cumhigh.sem, o_cumhigh.at(1, 0))
                    for at, n in ((0, P), (P, SEQ)):
                        ins = V.tensor_tensor(o_cum[:, 1, at:at + n], tb[0:GATES, 3, 0:n], o_cum[:, 0, at:at + n].bitcast(F32), ALU.subtract)
                        if at == 0:
                            chain.step(ins)
                    ins.then_inc(o_cumT.sem, 1)
                    convolve(8)
                    feed(end)
                    convolve(8)
                if c == 3:
                    feed(end)
                    convolve(10)
                if c == 4:
                    feed(end)
                    k_part(1)

            def odd_rest():
                attention(1, lambda h: convolve(8))
                share(1)
                split_y(1, (0, 1))
                convolve(len(taps))
                for t in range(NT):
                    dve.wait_ge(o_back.sem, o_back.at(1, t))
                    chain.step(V.bn_stats(c_bn[:, t, :], tb[:, 2 + t, :]))
                    chain.settle()
                    V.bn_aggr(c_mv[:, t, :], c_bn[:, t, :]).then_inc(o_spread.sem, 1)
                for t in range(NT):
                    dve.wait_ge(o_scaled.sem, o_scaled.at(1, t))
                    dve.wait_ge(o_spread.sem, o_spread.at(1, t))
                    V.tensor_scalar(o_z[:, t, :], tb[:, 2 + t, :], c_mv[:, t, 0:1], c_rstd[:, t:t + 1], ALU.subtract,
                                    ALU.mult).then_inc(o_normed.sem, 1)
                for t in range(NT):
                    dve.wait_ge(y_high.sem, y_high.at(1, 2 + t))
                    tok = slice(P * t, P * (t + 1))
                    V.tensor_tensor(h_lo[:, Y_LO + 4:Y_LO + 8, tok], o_y[:, t, :, :], h_hi[:, 4:8, tok].bitcast(F32),
                                    ALU.subtract).then_inc(y_low.sem, 1)

            def rope(l):
                dve.wait_ge(a_out, out_at(l, 2, 1))
                v = p_qk[:, :, :].rearrange("p t (h d) -> p t h d", d=HD)
                x1, x2 = v[:, :, :, 0:ROPE_HALF], v[:, :, :, ROPE_HALF:2 * ROPE_HALF]
                full = [P, NT, 2 * HEADS, ROPE_HALF]

                def table(at):
                    return const[:, at:at + NT * ROPE_HALF].rearrange("p (t d) -> p t d", t=NT).unsqueeze(2).broadcast_to(full)

                prod = nbuf[:, :].rearrange("p (i t h d) -> p i t h d", i=4, t=NT, h=2 * HEADS)
                for i, (u, at) in enumerate(((x1, C_COS), (x2, C_SIN), (x2, C_COS), (x1, C_SIN))):
                    chain.step(V.tensor_tensor(prod[:, i], u, table(at), ALU.mult))
                chain.settle()
                chain.step(V.tensor_tensor(x1, prod[:, 0], prod[:, 1], ALU.subtract))
                V.tensor_tensor(x2, prod[:, 2], prod[:, 3], ALU.add).then_inc(roped.sem, 1)

            def hyb_step(l, c, end):
                if c == 1:
                    feed(end)
                    dve.wait_ge(z_log.sem, z_log.at(l, 0))
                    chain.step(V.scalar_tensor_tensor(g_z[:, :, :], g_z[:, :, :], 0.0, g_e[:, :, :], ALU.min, ALU.subtract))
                    chain.settle()
                    ones = const[:, C_TRI + P:C_TRI + P + 1].broadcast_to([P, SEQ])
                    for b in range(2):
                        chain.step(V.tensor_tensor_scan(g_b[:, b, :], ones, g_z[:, b, :], 0.0, ALU.mult, ALU.add))
                    chain.settle()
                for n in LEVELS_AFTER.get(c, ()):
                    level_distance(l, n)
                    keep(l, n)
                    feed(fed[0] + 1)
                    level_factors(l, n)
                if c == 2:
                    rope(l)
                if c == 4:
                    k_part(l)
                    feed(end)
                    keep(l, NL)
                if c == 5:
                    dve.wait_ge(a_out, out_at(l, 5, 1))
                    dve.wait_ge(rows_in, rows_at(2 * l))
                    chain.step(V.tensor_tensor(g_r[:, :, :], g_r[:, :, :],
                                               rows[:, 2, HALF:D].unsqueeze(1).broadcast_to([P, NT, HALF]), ALU.mult))
                feed(end)

            def level_distance(l, n):
                m = LEVELS[n]
                b, z = (level_view(u[:, :, :], m) for u in (g_b, g_z))
                mid = b[:, :, 0, m - 1:m].broadcast_to([P, NT * P // m, m])
                if n:
                    dve.wait_ge(g_exp.sem, g_exp.at(l, n - 1))
                chain.step(V.tensor_tensor(z[:, :, 1, :], b[:, :, 1, :], mid, ALU.subtract))
                V.tensor_tensor(z[:, :, 0, :], mid, b[:, :, 0, :], ALU.subtract).then_inc(g_diff.sem, 1)

            def level_factors(l, n):
                m = LEVELS[n]
                o, e = level_view(g_x[:, (n + 1) % 2, :, :], m), level_view(g_e[:, :, :], m)
                q, k = level_view(g_qkT[:, 0:2, :], m), level_view(g_qkT[:, 2:4, :], m)
                dve.wait_ge(g_exp.sem, g_exp.at(l, n))
                if n >= 2:
                    dve.wait_ge(g_pair.sem, g_pair.at(l, n - 1))
                chain.step(V.tensor_tensor(o[:, :, 1, :], e[:, :, 1, :], q[:, :, 1, :], ALU.mult))
                V.tensor_tensor(o[:, :, 0, :], e[:, :, 0, :], k[:, :, 0, :], ALU.mult).then_inc(g_scaled.sem, 1)

            def keep(l, n):
                dve.wait_ge(g_pair.sem, g_pair.at(l, n))
                for par in range(2):
                    pair = tb[:, par, :]
                    if n == 0:
                        ins = V.tensor_tensor(g_att[:, 4 * par:4 * par + 4, :], pair.rearrange("p (i n) -> p i n", i=4),
                                              ident.unsqueeze(1).broadcast_to([P, 4, P]), ALU.mult)
                    elif n == 1:
                        ins = V.tensor_copy(g_far[:, 2 * par:2 * par + 2, :], pair[:, 0:2 * P].rearrange("p (i n) -> p i n", i=2))
                    else:
                        m = LEVELS[n - 1]
                        dst = g_att[:, 4 * par:4 * par + 4, :].rearrange("p i (j s m) -> p i j s m", s=2, m=m)[:, :, :, 1, :]
                        mask = right(const[:, C_LEVEL + P * (n - 2):C_LEVEL + P * (n - 1)].bitcast(I32), m)
                        src = pair[:, 0:2 * P].rearrange("p (i j m) -> p i j m", i=4, m=m)
                        ins = V.copy_predicated(dst, mask.unsqueeze(1).broadcast_to([P, 4, P // (2 * m), m]), src)
                    if par == 0:
                        chain.step(ins)
                ins.then_inc(g_kept.sem, 1)

            def linear_norm(l):
                dve.wait_ge(g_rooted.sem, g_rooted.at(l, 0))
                for t in range(NT):
                    chain.step(V.tensor_tensor(heads(g_o[:, t, :], GLA_H), heads(acc[:, 1 + 2 * t, :], GLA_H),
                                               g_rstd[:, t, :].unsqueeze(2).broadcast_to([P, GLA_H, GLA_DV]), ALU.mult))
                chain.settle()
                for t in range(NT):
                    V.tensor_tensor(g_o[:, t, :], g_o[:, t, :], g_r[:, t, :], ALU.mult).then_inc(g_normed.sem, 1)

            def hyb_rest(l):
                attention(l, lambda h: linear_norm(l) if h == 5 else None)
                share(l)
                split_y(l, (0, 1))
                for t in range(NT):
                    dve.wait_ge(a_scaled.sem, a_scaled.at(l, t))
                    V.scalar_tensor_tensor(y_tok[:, t, :], y_tok[:, t, :], a_rstd[:, t:t + 1], rows[:, 2, 0:HALF], ALU.mult,
                                           ALU.mult).then_inc(a_normed.sem, 1)
                split_y(l, (2, 3))

            def k_part(l):
                for i in range(2):
                    dve.wait_ge(qk_turned.sem, qk_turned.at(l, 2 + i))
                    V.tensor_copy(kT[:, 2 * i:2 * i + 2, :], blocks(2 + i)).then_inc(k_out.sem, 1)

            def head_lows(l, h):
                bank = tb[:, h % 2, :]
                dve.wait_ge(logits.sem, logits.at(l, h))
                if h >= 2:
                    dve.wait_ge(weighed.sem, weighed.at(l, h - 2))
                chain.step(V.tensor_reduce(low_of[:, h % 2, 0:1], bank[:, 0:P], AX_X, ALU.min))
                V.tensor_reduce(low_of[:, h % 2, 1:2], bank[:, P:3 * P], AX_X, ALU.min).then_inc(lows.sem, 1)

            def attention(l, beside):
                tile_done(dve, 1, l, "A", NA[l] - 1)
                head_lows(l, 0)
                for h in range(HEADS):
                    if h + 1 < HEADS:
                        head_lows(l, h + 1)
                    beside(h)
                    dve.wait_ge(p_turned.sem, p_turned.at(l, h))
                    if h >= 2:
                        dve.wait_ge(attended.sem, attended.at(l, h - 2))
                    V.tensor_copy(probsT[:, h % 2, :], tb[:, 2 + h % 2, 0:3 * P]).then_inc(p_out.sem, 1)

            def share(l):
                dve.wait_ge(weighed.sem, weighed.at(l, HEADS - 1))
                chain.step(V.reciprocal(share_of[:, :, :], total[:, :, :]))
                chain.settle()
                dve.wait_ge(attended.sem, attended.at(l, HEADS - 1))
                for t in range(NT):
                    V.tensor_tensor(heads(y_tok[:, t, :], HEADS), heads(acc[:, 2 * t, :], HEADS),
                                    share_of[:, t, :].unsqueeze(2).broadcast_to([P, HEADS, HD]), ALU.mult).then_inc(shared.sem, 1)

            def split_y(l, which):
                for i in which:
                    b, t, bank = y_part(l, i)
                    tok = slice(P * t, P * (t + 1))
                    dve.wait_ge(y_high.sem, y_high.at(l, i))
                    V.tensor_tensor(h_lo[:, Y_LO + b:Y_LO + b + 4, tok], ps[:, bank, :].rearrange("p (b n) -> p b n", b=4),
                                    h_hi[:, b:b + 4, tok].bitcast(F32), ALU.subtract).then_inc(y_low.sem, 1)

            def glu_part(l, c, r, t):
                dve.wait_ge(silu_done, glu_at(l, c, t))
                if not isinstance(c, int):
                    dve.wait_ge(h_turned.sem, c + (h_turned.at(l, 0) - 1))
                V.tensor_tensor(glu[:, FFN_BUF[r], t, :], silu[:, FFN_BUF[r], t, :], ps[:, FFN_BANK[r][t], FC:2 * FC],
                                ALU.mult).then_inc(glu_done, 1)

            def ffn_split(l, c):
                dve.wait_ge(h_high.sem, c + h_high.at(l, 0))
                hi, lo = (u[:, :, :].rearrange("p (c b) n -> p c b n", b=2)[:, c, :, :] for u in (h_hi, h_lo))
                V.tensor_tensor(lo, blocks(0), hi.bitcast(F32), ALU.subtract).then_inc(h_low.sem, 1)

            for t in range(NT):
                x_split(0, t)
            feed(4)
            dve.wait_ge(tiny_high, 1)
            V.tensor_tensor(bias_lo[:, :], const[:, C_DIL:C_DIL + 3 * P], bias_hi[:, P:4 * P].bitcast(F32), ALU.subtract)
            V.tensor_tensor(tiny_lo[:, :, :], tiny_raw[:, :, :], tiny_hi[:, :, :].bitcast(F32), ALU.subtract).then_inc(tiny_done, 1)
            dve.wait_ge(params_out, 1)
            feed(N_W)
            for l in every:
                if l > 0:
                    feed(U_A[l] + N_W)
                    x_split(2 * l, 1)
                for c in range(1, NA[l]):
                    end = U_A[l] + 4 * (c + 1) + N_W
                    if LAYERS[l] == "odd":
                        odd_step(c, end)
                    elif LAYERS[l] == "hyb":
                        hyb_step(l, c, end)
                    else:
                        feed(end)
                if LAYERS[l] == "even":
                    even_rest()
                elif LAYERS[l] == "odd":
                    odd_rest()
                else:
                    hyb_rest(l)
                after_boundary(2 * l, U_C[l])
                glu_part(l, 0, 0, 0)
                feed(U_C[l] + N_W)
                x_split(2 * l + 1, 1)
                glu_part(l, 1, 1, 0)
                glu_part(l, 0, 0, 1)
                feed(U_C[l] + 4 + N_W)
                ffn_split(l, 0)
                glu_part(l, 1, 1, 1)
                feed(U_C[l] + 8 + N_W)
                with dve.Fori(0, (NC - 2) // LOOP) as j:
                    for r in range(LOOP):
                        ffn_split(l, j * LOOP + (1 + r))
                        for t in range(NT):
                            glu_part(l, j * LOOP + (2 + r), (2 + r) % LOOP, t)
                        for q in range(4):
                            low(Unit(U_C[l] + 4 * (2 + r) + N_W + q, j))
                fed[0] += 4 * (NC - 2)
                ffn_split(l, NC - 1)
                feed(U_D[l] + KF - KD + N_W)
                after_boundary(2 * l + 1, U_D[l] + KF)

        @block.gpsimd
        def _(pool):
            chain = Chain(pool, pool_step)
            nc.gpsimd.memset(minus_half, -0.5).then_inc(set_up, 1)
            pool.wait_ge(set_up, 1)

            def root(dst, src, scale, eps, st, n):
                chain.step(nc.gpsimd.tensor_scalar(dst, src, scale, eps, ALU.mult, ALU.add))
                chain.settle()
                nc.gpsimd.tensor_tensor(dst, dst, minus_half[:, 0:n], ALU.pow).then_inc(st.sem, 1)

            def boundary(k):
                for t in range(NT):
                    one = slice(t, t + 1)
                    if is_ln[k]:
                        pool.wait_ge(spread.sem, spread.at(k, t))
                        root(rstd[:, one], mv[:, t, 1:2], 1.0, LN_EPS, scaled, 1)
                    else:
                        pool.wait_ge(squared.sem, squared.at(k, t))
                        root(rstd[:, one], ssq[:, one], 1.0 / D, RMS_EPS, scaled, 1)
                    if pre[k]:
                        pool.wait_ge(spread2.sem, spread2.at(k, t))
                        root(rstd2[:, one], ssq2[:, one], 1.0 / D, RMS_EPS, scaled2, 1)

            for l in every:
                if LAYERS[l] == "odd":
                    for t in range(NT):
                        pool.wait_ge(o_spread.sem, o_spread.at(l, t))
                        root(c_rstd[:, t:t + 1], c_mv[:, t, 1:2], 1.0, LN_EPS, o_scaled, 1)
                if LAYERS[l] == "hyb":
                    pool.wait_ge(g_spread.sem, g_spread.at(l, 0))
                    root(g_rstd.rearrange("p t h -> p (t h)"), g_ssq.rearrange("p t h -> p (t h)"), 1.0 / GLA_DV, RMS_EPS,
                         g_rooted, NT * GLA_H)
                    for t in range(NT):
                        pool.wait_ge(a_spread.sem, a_spread.at(l, t))
                        root(a_rstd[:, t:t + 1], a_ssq[:, t:t + 1], 1.0 / HALF, RMS_EPS, a_scaled, 1)
                boundary(2 * l)
                boundary(2 * l + 1)


INPUTS = (
    "x", "ev_w_in", "ev_conv_w", "ev_pool_w", "ev_pool_scale", "ev_w_out", "od_w_in", "od_forget_b", "od_dw_w",
    "od_dw_b", "od_cn_g", "od_cn_b", "od_w_out", "ln_mix_g", "ln_mix_b", "ln_ffn_g", "ln_ffn_b", "ffn_w_in",
    "ffn_w_out", "mix_pre_norm_2", "mix_post_norm_2", "ffn_pre_norm_2", "ffn_post_norm_2", "w_in_2",
    "gla_w_gate_up_2", "gla_b_gate_2", "gla_out_norm_2", "attn_out_norm_2", "w_out_2", "w_gate_2", "w_up_2",
    "w_down_2",
)


def kernel(**inputs):
    import concourse.bacc as bacc
    import numpy as np
    from concourse.bass_utils import run_bass_kernel_spmd

    nc = bacc.Bacc("TRN2", target_bir_lowering=False, num_devices=1, dynamic_dma_scratch_size=1024)
    arrays = {name: np.ascontiguousarray(inputs[name]) for name in INPUTS}
    arrays["shape_consts"] = shape_constants()
    aps = {name: nc.dram_tensor(name, v.shape, mybir.dt.from_np(v.dtype), kind="ExternalInput").ap() for name, v in arrays.items()}
    out = nc.dram_tensor("out", (1, SEQ, D), F32, kind="ExternalOutput").ap()
    blocks_kernel(nc, aps, out)
    result = run_bass_kernel_spmd(nc, [arrays], core_ids=[0])
    return result.results[0]["out"]
```

```python
from contextlib import ExitStack

import concourse.bass as bass
from concourse import mybir

ALU = mybir.AluOpType
ACT = mybir.ActivationFunctionType
AX_X = mybir.AxisListType.X
F32 = mybir.dt.float32
F32R = mybir.dt.float32r
I32 = mybir.dt.int32

P = 128
D = 1024
SEQ = 256
NT = SEQ // P
KD = D // P
CH = 512
D_FF = 2816
FC = 256
NC = D_FF // FC
KF = D_FF // P
HALF = D // 2
DEPTH = 2
ALPHA = (2.0 * DEPTH) ** 0.25
LN_EPS = 1e-5
RMS_EPS = 1e-6
HEADS = 8
HD = 64
SCALE = HD ** -0.5
MASKED = -1e30
TAPS = 31
ROPE_HALF = 8
ROPE_THETA = 500000.0
RANK = 16
GLA_H = 4
GLA_DK = 64
GLA_DV = 128
GLA_SCALE = GLA_DK ** -0.5
GLA_TAU = 16.0
DILATED = ((128, 1), (512, 4), (2048, 16))
WINDOWS = (2, 4, 8, 16)
PAD = 16

LAYERS = ("even", "odd", "hyb", "hyb")
EV_COLS = (512, 1024, 1536, 0)
OD_COLS = (1544, 2056, 0, 512, 1024)
HY_COLS = (1536, 0, 512, 1024, 2048, 2560)
COLS = (EV_COLS, OD_COLS, HY_COLS, HY_COLS)
OD_F = 1536
HY_LOW = 3072
GATES = 8
TINY = {1: (0, GATES), 2: (GATES, RANK), 3: (GATES + RANK, RANK)}
TINY_W = GATES + 2 * RANK

LEVELS = (128, 64, 32, 16, 8, 4, 2, 1)

C_IDENT = 0
C_TRI = C_IDENT + P
C_CAUSAL = C_TRI + 2 * P
C_DIL = C_CAUSAL + P
C_COS = C_DIL + 3 * P
C_SIN = C_COS + NT * ROPE_HALF
C_LEVEL = C_SIN + NT * ROPE_HALF
C_POOL = C_LEVEL + (len(LEVELS) - 1) * P
N_CONST = C_POOL + len(WINDOWS) * PAD

R_EVCONV, R_PSCALE, R_DW, R_DWB, R_CNG, R_CNB, R_GLAB = 0, 3, 4, 35, 36, 37, 38
N_ROWS = 39

PROW = 16 * 7
PARAMS = 16 * 6

N_RAW = 4
N_W = 12
LOOP = 3


def shape_constants():
    import numpy as np

    c = np.zeros((P, N_CONST), np.float32)
    i = np.arange(P)
    c[:, C_IDENT:C_IDENT + P] = np.eye(P)
    c[:, C_TRI:C_TRI + P] = i[:, None] <= i[None, :]
    c[:, C_TRI + P:C_TRI + 2 * P] = 1.0
    c[:, C_CAUSAL:C_CAUSAL + P] = np.where(i[:, None] >= i[None, :], 0.0, -MASKED)

    def dilated(dist):
        n = sum(((dist >= 0) & (dist <= w) & (dist % d == 0)).astype(np.int64) for w, d in DILATED)
        return np.where(n > 0, -np.log(np.maximum(n, 1)), -MASKED)

    near = i[:, None] - i[None, :]
    c[:, C_DIL:C_DIL + P] = dilated(near)
    c[:, C_DIL + P:C_DIL + 2 * P] = dilated(near + P)
    c[:, C_DIL + 2 * P:C_DIL + 3 * P] = dilated(near)
    inv = np.float32(ROPE_THETA) ** (-(np.arange(ROPE_HALF, dtype=np.float32) * 2.0) / np.float32(2 * ROPE_HALF))
    ang = np.arange(SEQ, dtype=np.float32)[:, None] * inv.astype(np.float32)[None, :]
    for t in range(NT):
        c[:, C_COS + ROPE_HALF * t:C_COS + ROPE_HALF * (t + 1)] = np.cos(ang[P * t:P * (t + 1)])
        c[:, C_SIN + ROPE_HALF * t:C_SIN + ROPE_HALF * (t + 1)] = np.sin(ang[P * t:P * (t + 1)])
    for n, m in enumerate(LEVELS[1:]):
        blk = i // (2 * m)
        right = i // m % 2
        c[:, C_LEVEL + P * n:C_LEVEL + P * (n + 1)] = (
            (blk[:, None] == blk[None, :]) & (right[:, None] == 0) & (right[None, :] == 1))
    for g, w in enumerate(WINDOWS):
        c[:, C_POOL + PAD * g:C_POOL + PAD * (g + 1)] = 1.0 / np.minimum(np.arange(PAD) + 1, w)
    return c


class Stage:

    def __init__(self, sem, per, layers):
        self.sem, self.per, self.layers = sem, per, layers

    def at(self, layer, i):
        return self.layers.index(layer) * self.per + i + 1


class Chain:

    def __init__(self, eng, sem):
        self.eng, self.sem, self.n = eng, sem, 0

    def step(self, ins):
        self.n += 1
        ins.then_inc(self.sem, 1)
        return self.n

    def settle(self, n=None):
        self.eng.wait_ge(self.sem, self.n if n is None else n)


class Unit:

    def __init__(self, u, j=0):
        self.raw = u % N_RAW
        self.slot = u % N_W
        self.loads = u // N_RAW + (N_W // N_RAW) * j + 1
        self.n = u + N_W * j
        self.first = u < N_RAW
        self.fresh = u < N_W


def blocks_kernel(nc, a, out):
    ctx = ExitStack()
    with ctx:
        top = [1280]

        def place(name, shape, dt, at=None):
            size = 4
            for n in shape[1:]:
                size *= n
            if at is None:
                at = top[0]
                top[0] += (size + 31) // 32 * 32
            return nc.alloc_sbuf_tensor_at(name, list(shape), dt, offset=at), at

        raw, _ = place("raw", [P, N_RAW, 2 * CH], F32)
        w_hi, _ = place("w_hi", [P, N_W, 2 * CH], F32R)
        w_lo, _ = place("w_lo", [P, N_W, 2 * CH], F32R)
        x, _ = place("x", [P, NT, D], F32)
        a_hi, at_a = place("a_hi", [P, KD, SEQ], F32R)
        a_lo, _ = place("a_lo", [P, KD, SEQ], F32R)
        h_hi, at_h = place("h_hi", [P, KF, SEQ], F32R)
        h_lo, at_hl = place("h_lo", [P, KF, SEQ], F32R)
        rows, _ = place("rows", [P, 3, D], F32)
        nbuf, _ = place("nbuf", [P, D], F32)
        const, _ = place("const", [P, N_CONST], F32)
        pcol, _ = place("pcol", [P, 4, N_ROWS], F32)
        w_up, _ = place("w_up", [RANK, 2, SEQ], F32)
        tiny_hi, _ = place("tiny_hi", [P, KD, TINY_W], F32R)
        tiny_lo, _ = place("tiny_lo", [P, KD, TINY_W], F32R)
        bias_hi, _ = place("bias_hi", [P, 4 * P], F32R)
        bias_lo, _ = place("bias_lo", [P, 3 * P], F32R)
        ident_r, _ = place("ident_r", [P, P], F32R)
        fbias, _ = place("fbias", [GATES, 1], F32)
        stat, _ = place("stat", [P, 160], F32)
        silu, at_s = place("silu", [P, 2, NT, FC], F32)
        glu, _ = place("glu", [P, 2, NT, FC], F32)
        assert top[0] <= nc.SBUF_PARTITION_SIZE_BYTES, top[0]

        tiny_raw, _ = place("tiny_raw", [P, KD, TINY_W], F32, at_s)
        prow, _ = place("prow", [N_ROWS, HALF], F32, at_s + 4096)
        squares, _ = place("squares", [P, D], F32, at_s)
        Y_LO = KF - KD
        at_m = at_h + KD * SEQ * 4

        def scratch(name, shape, slot):
            return place(name, shape, F32, int(at_m + 4096 * slot))[0]

        def late(name, shape, byte):
            return place(name, shape, F32, at_a + byte)[0]

        p_qk = scratch("p_qk", [P, NT, D], 0)
        qT, _ = place("qT", [P, 4, SEQ], F32, at_hl + Y_LO * SEQ * 4)
        kT, _ = place("kT", [P, 4, SEQ], F32, at_h)
        p_v = scratch("p_v", [P, NT, CH], 2)
        y_tok = scratch("y_tok", [P, NT, CH], 6)
        probs = late("probs", [P, 2, 3 * P], 0)
        probsT = late("probsT", [P, 2, 3 * P], 3072)
        e_pc = scratch("e_pc", [P, NT, CH], 0)
        e_cT = scratch("e_cT", [P, 4, SEQ], 0)
        e_pv = scratch("e_pv", [P, NT, CH], 1)
        e_m = scratch("e_m", [P, 4, SEQ], 1)
        e_pu = scratch("e_pu", [P, NT, CH], 2)
        e_pb = scratch("e_pb", [P, NT, CH], 3)
        w_grp = scratch("w_grp", [P, 4, P], 4)
        e_sB = scratch("e_sB", [P, 4, PAD + SEQ], 4.5)
        e_pool = scratch("e_pool", [P, 4, SEQ], 5.75)
        e_y = scratch("e_y", [P, 4, SEQ], 0)
        e_u, _ = place("e_u", [P, 4, PAD + SEQ], F32, at_h)
        e_sA, _ = place("e_sA", [P, 4, PAD + SEQ], F32, at_hl + Y_LO * SEQ * 4)
        e_edge, _ = place("e_edge", [P, 4, PAD], F32, at_hl + (Y_LO + 5) * SEQ * 4)
        PADT = TAPS - 1
        o_d1 = scratch("o_d1", [P, NT, CH], 3)
        o_d2 = scratch("o_d2", [P, NT, CH], 4)
        o_pad = scratch("o_pad", [P, 4, PADT + SEQ], 3)
        o_acc = scratch("o_acc", [P, 4, SEQ], 5)
        o_z = late("o_z", [P, NT, CH], 6144)
        o_y = late("o_y", [P, NT, 4, P], 10240)
        N_DIAG = 16
        o_diag = scratch("o_diag", [P, N_DIAG, P], 0)
        o_f, _ = place("o_f", [GATES, 4, SEQ], F32, at_s)
        o_cum, _ = place("o_cum", [GATES, 2, 3 * P], F32R, at_s + 4096)
        g_pqk = scratch("g_pqk", [P, NT, CH], 3)
        g_qkT = scratch("g_qkT", [P, 4, SEQ], 3)
        g_v = scratch("g_v", [P, NT, CH], 4)
        g_r = scratch("g_r", [P, NT, CH], 5)
        g_o = scratch("g_o", [P, NT, CH], 0)
        g_z, _ = place("g_z", [P, 2, SEQ], F32, at_s)
        g_e, _ = place("g_e", [P, 2, SEQ], F32, at_s + 2048)
        g_b, _ = place("g_b", [P, 2, SEQ], F32, at_s + 4096)
        g_lowT, _ = place("g_lowT", [RANK, SEQ], F32, at_s + 6400)
        g_x = scratch("g_x", [P, 2, 2, SEQ], 6)
        g_att, _ = place("g_att", [P, 2 * GLA_H, P], F32, at_h + 4 * SEQ * 4)
        g_far, _ = place("g_far", [P, GLA_H, P], F32, at_hl + (Y_LO + 4) * SEQ * 4)

        ident = const[:, C_IDENT:C_IDENT + P]
        bn = stat[:, 0:24].rearrange("p (t h s) -> p t h s", t=NT, h=2)
        mv = stat[:, 24:28].rearrange("p (t s) -> p t s", t=NT)
        rstd = stat[:, 28:30]
        ssq = stat[:, 122:126].rearrange("p (t h) -> p t h", t=NT)
        ssq2 = stat[:, 32:34]
        rstd2 = stat[:, 34:36]
        minus_half = stat[:, 36:44]
        low_of = stat[:, 48:52].rearrange("p (b t) -> p b t", b=2)
        total = stat[:, 52:68].rearrange("p (t h) -> p t h", t=NT)
        share_of = stat[:, 68:84].rearrange("p (t h) -> p t h", t=NT)
        a_ssq = stat[:, 84:86]
        a_rstd = stat[:, 86:88]
        g_ssq = stat[:, 88:96].rearrange("p (t h) -> p t h", t=NT)
        g_rstd = stat[:, 96:104].rearrange("p (t h) -> p t h", t=NT)
        c_bn = stat[:, 104:116].rearrange("p (t s) -> p t s", t=NT)
        c_mv = stat[:, 116:120].rearrange("p (t s) -> p t s", t=NT)
        c_rstd = stat[:, 120:122]

        ps = ctx.enter_context(nc.psum_tensor("ps", [P, 8, CH], F32))
        acc, tb = ps[:, 0:4, :], ps[:, 4:8, :]
        IN_BANK = ((0, 2), (1, 3))
        FFN_BANK = ((0, 2), (6, 7), (1, 3))
        FFN_BUF = (0, 1, 0)

        NA = [len(c) for c in COLS]
        U_A, U_B, U_C, U_D, u = [], [], [], [], 0
        for l in range(len(LAYERS)):
            U_A.append(u)
            U_B.append(U_A[l] + 4 * NA[l])
            U_C.append(U_B[l] + KD)
            U_D.append(U_C[l] + 4 * NC)
            u = U_D[l] + KF
        U_END = u
        ACC0 = [sum(NA[:l]) + (NC + 2) * l for l in range(len(LAYERS))]

        def acc_at(l, phase, c=0):
            return ACC0[l] + {"A": 0, "B": NA[l], "C": NA[l] + 1, "D": NA[l] + 1 + NC}[phase] + c + 1

        def out_at(l, c, t):
            return 2 * sum(NA[:l]) + (2 * t + c if c < 2 else 2 * c + t) + 1

        def glu_at(l, c, t):
            if isinstance(c, int) and c < 2:
                return 2 * NC * l + 2 * t + c + 1
            return c * 2 + (2 * NC * l + t + 1)

        NB = 2 * len(LAYERS)
        is_ln = [LAYERS[k // 2] != "hyb" for k in range(NB)]
        pre = [k + 1 < NB and LAYERS[(k + 1) // 2] == "hyb" for k in range(NB)]

        def sem(name):
            return ctx.enter_context(nc.semaphore(name))

        every = list(range(len(LAYERS)))
        attn = [1, 2, 3]
        hyb = [2, 3]

        def stage(name, per, layers=None):
            return Stage(sem(name), per, every if layers is None else layers)

        raw_in = [sem(f"raw_in{i}") for i in range(N_RAW)]
        x_in = [sem(f"x_in{t}") for t in range(NT)]
        const_in, prow_in, params_in, rows_in, out_done = sem("const_in"), sem("prow_in"), sem("params_in"), sem("rows_in"), sem("out_done")
        w_high, w_low, w_used = sem("w_high"), sem("w_low"), sem("w_used")
        acc_done = sem("acc_done")
        a_out = sem("a_out")
        silu_done, glu_done = sem("silu_done"), sem("glu_done")
        h_turned, h_high, h_low = stage("h_turned", NC), stage("h_high", NC), stage("h_low", NC)
        bounds = list(range(NB))
        x_turned, x_high, x_low = (stage(n, 4, bounds) for n in ("x_turned", "x_high", "x_low"))
        acc_read = stage("acc_read", NT, bounds)
        spread = stage("spread", NT, [k for k in bounds if is_ln[k]])
        half_squared, half_gained, squared = (
            stage(n, NT, [k for k in bounds if not is_ln[k]]) for n in ("half_squared", "half_gained", "squared"))
        scaled = stage("scaled", NT, bounds)
        spread2 = stage("spread2", NT, [k for k in bounds if pre[k]])
        scaled2 = stage("scaled2", NT, [k for k in bounds if pre[k]])
        x_sum = stage("x_sum", NT, [k for k in bounds if pre[k]])
        x_ready = stage("x_ready", NT, bounds)
        act_step, dve_step, pool_step = sem("act_step"), sem("dve_step"), sem("pool_step")
        set_up, tiny_high, params_turned, params_out = sem("set_up"), sem("tiny_high"), sem("params_turned"), sem("params_out")
        tiny_done = sem("tiny_done")
        e_turned, e_act, e_dve = stage("e_turned", 10, [0]), stage("e_act", 4, [0]), stage("e_dve", 4, [0])
        e_pooled, e_high, e_low = stage("e_pooled", 1, [0]), stage("e_high", 6, [0]), stage("e_low", 6, [0])
        o_gated, o_turned, o_padded = stage("o_gated", 1, [1]), stage("o_turned", 2, [1]), stage("o_padded", 2, [1])
        o_fsum, o_fbiased, o_fcum, o_cumlow = (stage(n, 1, [1]) for n in ("o_fsum", "o_fbiased", "o_fcum", "o_cumlow"))
        o_soft, o_cumhigh = stage("o_soft", 1, [1]), stage("o_cumhigh", 1, [1])
        o_diagonal, o_tapped = stage("o_diagonal", TAPS, [1]), stage("o_tapped", TAPS, [1])
        o_fourth = stage("o_fourth", 1, [1])
        o_conv, o_back, o_spread, o_scaled = stage("o_conv", 1, [1]), stage("o_back", NT, [1]), stage("o_spread", NT, [1]), stage("o_scaled", NT, [1])
        o_normed, o_silu = stage("o_normed", NT, [1]), stage("o_silu", NT, [1])
        roped = stage("roped", 1, hyb)
        qk_turned, q_out, k_out = stage("qk_turned", 4, attn), stage("q_out", 2, attn), stage("k_out", 2, attn)
        logits, lows, weighed = stage("logits", HEADS, attn), stage("lows", HEADS, attn), stage("weighed", HEADS, attn)
        p_turned, p_out, attended = stage("p_turned", HEADS, attn), stage("p_out", HEADS, attn), stage("attended", HEADS, attn)
        shared = stage("shared", NT, attn)
        a_spread, a_scaled, a_normed = (stage(n, NT, hyb) for n in ("a_spread", "a_scaled", "a_normed"))
        y_turned, y_high, y_low = stage("y_turned", 4, attn), stage("y_high", 4, attn), stage("y_low", 4, attn)
        l_sum, l_out, z_done, z_out, z_log = (stage(n, 1, hyb) for n in ("l_sum", "l_out", "z_done", "z_out", "z_log"))
        gqk_turned, gqk_out = stage("gqk_turned", 2, hyb), stage("gqk_out", 2, hyb)
        NL = len(LEVELS)
        g_diff, g_exp, g_scaled = (stage(n, NL, hyb) for n in ("g_diff", "g_exp", "g_scaled"))
        g_pair, g_kept = stage("g_pair", NL + 1, hyb), stage("g_kept", NL + 1, hyb)
        g_done, g_spread, g_rooted, g_normed = stage("g_done", NT, hyb), stage("g_spread", 1, hyb), stage("g_rooted", 1, hyb), stage("g_normed", NT, hyb)

        def w_in(l):
            return a["ev_w_in"][0] if l == 0 else a["od_w_in"][0] if l == 1 else a["w_in_2"][l - 2]

        def w_out(l):
            return a["ev_w_out"][0] if l == 0 else a["od_w_out"][0] if l == 1 else a["w_out_2"][l - 2]

        def w_ffn(l):
            if l < 2:
                both = a["ffn_w_in"][l].rearrange("(k p) (h c n) -> h p k c n", p=P, h=2, n=FC)
                return both[0], both[1]
            return tuple(a[n][l - 2].rearrange("(k p) (c n) -> p k c n", p=P, n=FC) for n in ("w_gate_2", "w_up_2"))

        def w_down(l):
            return a["ffn_w_out"][l] if l < 2 else a["w_down_2"][l - 2]

        def norm_rows(k):
            l, ffn = divmod(k, 2)
            if is_ln[k]:
                g, b = ("ln_ffn_g", "ln_ffn_b") if ffn else ("ln_mix_g", "ln_mix_b")
                r = [(0, 0, a[g][l]), (1, 0, a[b][l])]
                if pre[k]:
                    r.append((2, 0, a["mix_pre_norm_2"][0]))
                return r
            j = l - 2
            r = [(0, 0, a["ffn_post_norm_2" if ffn else "mix_post_norm_2"][j])]
            if pre[k]:
                r.append((1, 0, a["mix_pre_norm_2"][j + 1] if ffn else a["ffn_pre_norm_2"][j]))
            if not ffn:
                r += [(2, 0, a["attn_out_norm_2"][j]), (2, HALF, a["gla_out_norm_2"][j])]
            return r

        def rows_at(k):
            return 16 * sum(len(norm_rows(i)) for i in range(k + 1))

        def pre_row(k):
            return rows[:, 2 if is_ln[k] else 1, :]

        def heads(ap, n):
            return ap.rearrange("p (h d) -> p h d", h=n)

        def level_view(ap, m):
            return ap.rearrange("p b (j s m) -> p (b j) s m", s=2, m=m)

        def tile_done(eng, t, l, phase, c=0):
            if t == 0:
                eng.wait_ge(acc_done, acc_at(l, phase, c))
            else:
                last = {"A": U_A[l] + 3, "B": U_B[l] + KD - 1, "C": U_C[l] + 3, "D": U_D[l] + KF - 1}[phase]
                eng.wait_ge(w_used, c * 4 + (last + 1) if phase in "AC" else last + 1)

        def out_order(l):
            return range(KD) if LAYERS[l] == "odd" else (4, 5, 6, 7, 0, 1, 2, 3)

        def y_part(l, i):
            t = i % 2
            if LAYERS[l] == "hyb":
                return (4, t, 1 + 2 * t) if i < 2 else (0, t, 4 + t)
            return (0 if i < 2 else 4), t, 4 + t

        LEVEL_STEP = ((2, 1), (2, 3), (3, 0), (3, 2), (3, 3), (4, 1), (4, 2), (5, 0), (5, 2))

        LEVELS_AFTER = {1: (0, 1), 2: (2, 3, 4), 3: (5, 6), 4: (7,)}

        def right(ap, m):
            return ap.rearrange("p (j s m) -> p j s m", s=2, m=m)[:, :, 1, :]

        def turn_after(k):
            if k % 2 == 0:
                return 8 if k == 2 else 7
            return 5 if is_ln[k] and not pre[k] else 7

        def level_rows(h):
            return slice(GLA_DK * (h % 2), GLA_DK * (h % 2 + 1)), h // 2

        def kept_at(h, t):
            return 4 * (h % 2) + 2 * (h // 2) + t

        def far_at(h):
            return 2 * (h % 2) + h // 2

        block = ctx.enter_context(nc.Block())

        @block.sync
        def _(sp):
            def load(v, left, right, split):
                if not v.first:
                    sp.wait_ge(w_low, v.n - N_RAW + 1)
                dst = raw[:, v.raw, :].rearrange("p (i h n) -> p i h n", i=2, h=2) if split else raw[:, v.raw, :]
                sp.dma_start(dst[:, :, 0, :] if split else dst[:, 0:CH], left).then_inc(raw_in[v.raw], 16)
                sp.dma_start(dst[:, :, 1, :] if split else dst[:, CH:2 * CH], right).then_inc(raw_in[v.raw], 16)

            def ffn_chunk(l, c, j, unit0):
                gate, up = w_ffn(l)
                for q in range(4):
                    k = slice(2 * q, 2 * q + 2)
                    load(Unit(unit0 + q, j), gate[:, k, c, :], up[:, k, c, :], True)

            def load_x(t):
                sp.dma_start(x[:, t, :], a["x"][0, P * t:P * (t + 1), :]).then_inc(x_in[t], 16)

            sp.dma_start(ident, a["shape_consts"][:, C_IDENT:C_IDENT + P]).then_inc(const_in, 16)
            load_x(0)
            for l in every:
                win = w_in(l).rearrange("(k p) n -> k p n", p=P)
                for c, col in enumerate(COLS[l]):
                    for q in range(4):
                        load(Unit(U_A[l] + 4 * c + q), win[2 * q, :, col:col + CH], win[2 * q + 1, :, col:col + CH], False)
                        if l == 0 and (c, q) == (1, 0):
                            load_x(1)
                wo = w_out(l).rearrange("(k p) n -> k p n", p=P)
                for i, k in enumerate(out_order(l)):
                    load(Unit(U_B[l] + i), wo[k, :, 0:CH], wo[k, :, CH:D], False)
                for c in range(2):
                    ffn_chunk(l, c, 0, U_C[l] + 4 * c)
                with sp.Fori(0, (NC - 2) // LOOP) as j:
                    for r in range(LOOP):
                        ffn_chunk(l, j * LOOP + (2 + r), j, U_C[l] + 4 * (2 + r))
                wd = w_down(l).rearrange("(k p) n -> k p n", p=P)
                for k in range(KF):
                    load(Unit(U_D[l] + k), wd[k, :, 0:CH], wd[k, :, CH:D], False)
            for t in range(NT):
                sp.wait_ge(x_ready.sem, x_ready.at(NB - 1, t))
                sp.dma_start(out[0, P * t:P * (t + 1), :], x[:, t, :]).then_inc(out_done, 16)
            sp.wait_ge(out_done, 16 * NT)

        @block.tensor
        def _(pe):
            def three_passes(bank, hi, lo, v, part, first, last):
                wh, wl = w_hi[:, v.slot, part], w_lo[:, v.slot, part]
                nc.tensor.matmul(ps[:, bank, :], hi, wh, start=first, stop=False)
                nc.tensor.matmul(ps[:, bank, :], hi, wl, start=False, stop=False)
                return nc.tensor.matmul(ps[:, bank, :], lo, wh, start=False, stop=last)

            def in_unit(v, q, bank, t):
                tok = slice(P * t, P * (t + 1))
                for i in range(2):
                    k = 2 * q + i
                    mm = three_passes(bank, a_hi[:, k, tok], a_lo[:, k, tok], v,
                                      slice(CH * i, CH * (i + 1)), k == 0, k == KD - 1)
                return mm

            def rows_unit(v, hi, lo, first, last, tiles):
                pe.wait_ge(w_low, v.n + 1)
                for t in tiles:
                    tok = slice(P * t, P * (t + 1))
                    for h in range(2):
                        mm = three_passes(2 * t + h, hi[:, tok], lo[:, tok], v, slice(CH * h, CH * (h + 1)), first, last)
                return mm

            def joint_chunk(units, c, banks, free_bank, hook):
                for t in range(NT):
                    free_bank(c, t)
                for q, v in enumerate(units):
                    pe.wait_ge(w_low, v.n + 1)
                    mm = in_unit(v, q, banks[0], 0)
                    if q == 3:
                        mm.then_inc(acc_done, 1)
                    in_unit(v, q, banks[1], 1).then_inc(w_used, 1)
                    hook(c, q)

            def first_chunks(l, phase, u0, banks, free_bank, hook):
                kk = 2 * l + (phase == "C")
                if kk > 0 and turn_after(kk - 1) == 8:
                    turn_x(kk, 0)
                for t in range(NT):
                    for c in range(2):
                        free_bank(c, t)
                        for q in range(4):
                            if c == 0 and q % 2 == 0:
                                pe.wait_ge(x_low.sem, x_low.at(kk, 2 * t + q // 2))
                            if t == 0 and c == 1 and q == 2:
                                turn_x(kk, 1)
                            v = Unit(u0 + 4 * c + q)
                            pe.wait_ge(w_low, v.n + 1)
                            mm = in_unit(v, q, banks[c][t], t)
                            if t == 1:
                                mm.then_inc(w_used, 1)
                            elif q == 3:
                                mm.then_inc(acc_done, 1)
                            if t == 1:
                                hook(c, q)

            def out_units(l, units, t):
                for i in units:
                    k = out_order(l)[i]
                    if t == 1 and i == turn_after(2 * l):
                        turn_x(2 * l + 1, 0)
                    mm = rows_unit(Unit(U_B[l] + i), h_hi[:, k, :], h_lo[:, Y_LO + k, :], i == 0, i == KD - 1, (t,))
                    if t == 1:
                        mm.then_inc(w_used, 1)
                    elif i == KD - 1:
                        mm.then_inc(acc_done, 1)

            def down(l):
                joint = KF - KD
                pe.wait_ge(glu_done, glu_at(l, NC - 2, 1))
                for k in range(joint):
                    if k == 2:
                        turn_ffn(l, NC - 1, FFN_BUF[(NC - 1) % LOOP])
                    if k % 2 == 0:
                        pe.wait_ge(h_low.sem, h_low.at(l, k // 2))
                    rows_unit(Unit(U_D[l] + k), h_hi[:, k, :], h_lo[:, k, :], k == 0, False, (0, 1)).then_inc(w_used, 1)
                for t in range(NT):
                    for k in range(joint, KF):
                        if t == 0 and k % 2 == 0:
                            pe.wait_ge(h_low.sem, h_low.at(l, k // 2))
                        if t == 1 and k == joint + turn_after(2 * l + 1) and l + 1 < len(LAYERS):
                            turn_x(2 * l + 2, 0)
                        mm = rows_unit(Unit(U_D[l] + k), h_hi[:, k, :], h_lo[:, k, :], False, k == KF - 1, (t,))
                        if t == 1:
                            mm.then_inc(w_used, 1)
                        elif k == KF - 1:
                            mm.then_inc(acc_done, 1)

            def turn_x(kk, t):
                if kk == 0:
                    pe.wait_ge(x_in[t], 16)
                    pe.wait_ge(const_in, 16)
                else:
                    pe.wait_ge(x_ready.sem, x_ready.at(kk - 1, t))
                src = nbuf[:, :] if kk > 0 and pre[kk - 1] else x[:, t, :]
                for h in range(2):
                    for b in range(4):
                        tr = nc.tensor.transpose(tb[:, h, P * b:P * (b + 1)],
                                                 src[:, CH * h + P * b:CH * h + P * (b + 1)], ident)
                    tr.then_inc(x_turned.sem, 1)

            def turn_blocks(bank, src, col, st):
                for b in range(2):
                    for t in range(NT):
                        tr = nc.tensor.transpose(tb[:, bank, SEQ * b + P * t:SEQ * b + P * (t + 1)],
                                                 src[:, t, col + P * b:col + P * (b + 1)], ident)
                tr.then_inc(st.sem, 1)

            def turn_tile(bank, src, st):
                for b in range(4):
                    tr = nc.tensor.transpose(ps[:, bank, P * b:P * (b + 1)], src[:, P * b:P * (b + 1)], ident)
                tr.then_inc(st.sem, 1)

            def tiny(l, bank, st):
                c0, w = TINY[l]
                pe.wait_ge(tiny_done, 1)
                o = tb[0:w, bank, 0:SEQ]
                for k in range(KD):
                    wh, wl = tiny_hi[:, k, c0:c0 + w], tiny_lo[:, k, c0:c0 + w]
                    nc.tensor.matmul(o, wh, a_hi[:, k, :], start=(k == 0), stop=False)
                    nc.tensor.matmul(o, wl, a_hi[:, k, :], start=False, stop=False)
                    mm = nc.tensor.matmul(o, wh, a_lo[:, k, :], start=False, stop=(k == KD - 1))
                mm.then_inc(st.sem, 1)

            def even_hook(c, q):
                if (c, q) == (1, 3):
                    pe.wait_ge(prow_in, PROW)
                    for b in range(4):
                        tr = nc.tensor.transpose(tb[:, 3, N_ROWS * b:N_ROWS * (b + 1)], prow[:, P * b:P * (b + 1)],
                                                 ident[0:N_ROWS, 0:N_ROWS])
                    tr.then_inc(params_turned, 1)
                if (c, q) == (2, 0):
                    pe.wait_ge(a_out, out_at(0, 1, 1))
                    for i in range(2):
                        turn_blocks(i, e_pc, 2 * P * i, e_turned)
                    pe.wait_ge(params_out, 1)
                    for i in range(2):
                        turn_blocks(2 + i, e_pv, 2 * P * i, e_turned)
                if (c, q) == (3, 0):
                    pe.wait_ge(a_out, out_at(0, 2, 1))
                    for i in range(2):
                        pe.wait_ge(e_act.sem, e_act.at(0, i))
                        turn_blocks(i, e_pu, 2 * P * i, e_turned)

            def even_rest():
                pe.wait_ge(e_pooled.sem, e_pooled.at(0, 0))
                pe.wait_ge(e_act.sem, e_act.at(0, 3))
                pe.wait_ge(params_in, PARAMS)
                for i in range(2):
                    for g in range(2 * i, 2 * i + 2):
                        mm = nc.tensor.matmul(tb[:, i, SEQ * (g % 2):SEQ * (g % 2 + 1)], w_grp[:, g, :], e_pool[:, g, :],
                                              start=True, stop=True)
                    mm.then_inc(e_turned.sem, 1)
                pe.wait_ge(a_out, out_at(0, 3, 1))
                for i in range(2):
                    pe.wait_ge(e_dve.sem, e_dve.at(0, i))
                    turn_blocks(2 + i, e_pb, 2 * P * i, e_turned)
                pe.wait_ge(e_low.sem, e_low.at(0, 1))
                out_units(0, range(2), 0)
                out_units(0, range(2), 1)
                pe.wait_ge(e_low.sem, e_low.at(0, 3))
                out_units(0, range(2, 4), 0)
                pe.wait_ge(e_low.sem, e_low.at(0, 5))
                out_units(0, range(4, KD), 0)
                out_units(0, range(2, KD), 1)

            def odd_hook(c, q):
                if (c, q) == (0, 2):
                    tiny(1, 2, o_fsum)
                if (c, q) == (2, 0):
                    pe.wait_ge(o_gated.sem, o_gated.at(1, 0))
                    for i in range(2):
                        turn_blocks(i, o_d1, 2 * P * i, o_turned)
                if (c, q) == (3, 2):
                    pe.wait_ge(o_fbiased.sem, o_fbiased.at(1, 0))
                    pe.wait_ge(a_out, out_at(1, 2, 1))
                    turn_qk(1, 0)
                if (c, q) == (4, 1):
                    pe.wait_ge(a_out, out_at(1, 3, 1))
                    pe.wait_ge(q_out.sem, q_out.at(1, 1))
                    turn_qk(1, 1)

            def odd_rest():
                for i in range(2):
                    pe.wait_ge(o_padded.sem, o_padded.at(1, i))
                pe.wait_ge(o_cumlow.sem, o_cumlow.at(1, 0))
                attention(1)
                pe.wait_ge(o_conv.sem, o_conv.at(1, 0))
                pe.wait_ge(o_fourth.sem, o_fourth.at(1, 0))
                for t in range(NT):
                    for b in range(4):
                        tr = nc.tensor.transpose(tb[:, 2 + t, P * b:P * (b + 1)], o_acc[:, b, P * t:P * (t + 1)], ident)
                    tr.then_inc(o_back.sem, 1)
                turn_y(1, shared, 0)
                pe.wait_ge(y_low.sem, y_low.at(1, 0))
                out_units(1, range(4), 0)
                pe.wait_ge(y_low.sem, y_low.at(1, 1))
                for t in range(NT):
                    pe.wait_ge(o_normed.sem, o_normed.at(1, t))
                    turn_tile(y_part(1, 2 + t)[2], o_z[:, t, :], y_turned)
                pe.wait_ge(shared.sem, shared.at(1, 1))
                out_units(1, range(4), 1)
                for t in range(NT):
                    pe.wait_ge(y_low.sem, y_low.at(1, 2 + t))
                    out_units(1, range(4, KD), t)

            def hyb_hook(l):
                def hook(c, q):
                    if (c, q) == (0, 2):
                        tiny(l, 0, l_sum)
                    if (c, q) == (1, 1):
                        pe.wait_ge(l_out.sem, l_out.at(l, 0))
                        for b in range(2):
                            mm = nc.tensor.matmul(tb[:, 2, SEQ * b:SEQ * (b + 1)], w_up[:, l - 2, P * b:P * (b + 1)], g_lowT[:, :],
                                                  start=True, stop=True)
                        mm.then_inc(z_done.sem, 1)
                    if (c, q) == (1, 3):
                        pe.wait_ge(a_out, out_at(l, 0, 1))
                        for i in range(2):
                            turn_blocks(i, g_pqk, 2 * P * i, gqk_turned)
                    if (c, q) == (4, 0):
                        pe.wait_ge(z_out.sem, z_out.at(l, 0))
                        pe.wait_ge(roped.sem, roped.at(l, 0))
                        turn_qk(l, 0)
                    if (c, q) == (5, 0):
                        pe.wait_ge(q_out.sem, q_out.at(l, 1))
                        turn_qk(l, 1)
                    if (c, q) in LEVEL_STEP:
                        level(l, LEVEL_STEP.index((c, q)))
                return hook

            def level(l, n):
                if n:
                    pe.wait_ge(g_scaled.sem, g_scaled.at(l, n - 1))
                    pe.wait_ge(g_kept.sem, g_kept.at(l, n - 1))
                else:
                    pe.wait_ge(gqk_out.sem, gqk_out.at(l, 1))
                for h in range(GLA_H):
                    r, b = level_rows(h)
                    for t in range(1 if n == 1 else NT):
                        tok = slice(P * t, P * (t + 1))
                        if n == 0:
                            ks, qs, at, w = g_qkT[r, 2 + b, tok], g_qkT[r, b, tok], kept_at(h, t) % 4, P
                        elif n == 1:
                            ks, qs, at, w = g_x[r, 1, b, 0:P], g_x[r, 1, b, P:SEQ], far_at(h) % 2, P
                        else:
                            ks, at, w = g_x[r, n % 2, b, tok], kept_at(h, t) % 4, P // 2
                            qs = right(ks, LEVELS[n - 1])
                        mm = nc.tensor.matmul(tb[:, h % 2, w * at:w * (at + 1)], ks, qs, start=True, stop=True)
                mm.then_inc(g_pair.sem, 1)

            def hyb_rest(l):
                attention(l)
                pe.wait_ge(shared.sem, shared.at(l, 0))
                pe.wait_ge(y_low.sem, y_low.at(l, 0))
                out_units(l, range(3), 0)
                turn_y(l, a_normed, 2)
                out_units(l, range(3, 4), 0)
                pe.wait_ge(y_low.sem, y_low.at(l, 2))
                out_units(l, range(4, KD), 0)
                pe.wait_ge(shared.sem, shared.at(l, 1))
                pe.wait_ge(y_low.sem, y_low.at(l, 3))
                out_units(l, range(KD), 1)

            def linear_values(l):
                pe.wait_ge(g_kept.sem, g_kept.at(l, NL))
                pe.wait_ge(a_out, out_at(l, NA[l] - 1, 1))
                for t in range(NT):
                    for h in range(GLA_H):
                        cols = slice(GLA_DV * h, GLA_DV * (h + 1))
                        if t == 1:
                            nc.tensor.matmul(acc[:, 3, cols], g_far[:, far_at(h), :], g_v[:, 0, cols], start=True, stop=False)
                        mm = nc.tensor.matmul(acc[:, 1 + 2 * t, cols], g_att[:, kept_at(h, t), :], g_v[:, t, cols],
                                              start=(t == 0), stop=True)
                    mm.then_inc(g_done.sem, 1)

            def turn_qk(l, part):
                for i in range(2):
                    turn_blocks(2 + i, p_qk, CH * part + 2 * P * i, qk_turned)

            def head_logits(l, h):
                bank, r, b = h % 2, slice(HD * (h % 2), HD * (h % 2 + 1)), h // 2
                if h >= 2:
                    pe.wait_ge(weighed.sem, weighed.at(l, h - 2))
                near, wide, late_half = tb[:, bank, 0:P], tb[:, bank, P:3 * P], tb[:, bank, 2 * P:3 * P]
                every_key = tb[:, bank, 0:3 * P]
                if l == 1:
                    one_hot = ident_r[0:GATES, h:h + 1].broadcast_to([GATES, P])
                    nc.tensor.matmul(every_key, one_hot, o_cum[:, 0, :], start=True, stop=False)
                    nc.tensor.matmul(every_key, one_hot, o_cum[:, 1, :], start=False, stop=False)
                    for part in (near, late_half):
                        nc.tensor.matmul(part, ident_r[:, :], bias_hi[:, 0:P], start=False, stop=False)
                else:
                    nc.tensor.matmul(every_key, ident_r[:, :], bias_hi[:, P:4 * P], start=True, stop=False)
                    nc.tensor.matmul(every_key, ident_r[:, :], bias_lo[:, :], start=False, stop=False)
                nc.tensor.matmul(near, qT[r, b, 0:P], kT[r, b, 0:P], start=False, stop=False)
                nc.tensor.matmul(wide, qT[r, b, P:SEQ], kT[r, b, :], start=False, stop=True).then_inc(logits.sem, 1)

            def head_turn(l, h):
                pe.wait_ge(weighed.sem, weighed.at(l, h))
                if h >= 2:
                    pe.wait_ge(p_out.sem, p_out.at(l, h - 2))
                for i in range(3):
                    tr = nc.tensor.transpose(tb[:, 2 + h % 2, P * i:P * (i + 1)], probs[:, h % 2, P * i:P * (i + 1)], ident)
                tr.then_inc(p_turned.sem, 1)

            def head_values(l, h):
                pe.wait_ge(p_out.sem, p_out.at(l, h))
                cols = slice(HD * h, HD * (h + 1))
                pT = probsT[:, h % 2, :]
                nc.tensor.matmul(acc[:, 0, cols], pT[:, 0:P], p_v[:, 0, cols], start=True, stop=True)
                nc.tensor.matmul(acc[:, 2, cols], pT[:, P:2 * P], p_v[:, 0, cols], start=True, stop=False)
                nc.tensor.matmul(acc[:, 2, cols], pT[:, 2 * P:3 * P], p_v[:, 1, cols], start=False,
                                 stop=True).then_inc(attended.sem, 1)

            def fourth_block(taps):
                for k in taps:
                    pe.wait_ge(o_diagonal.sem, o_diagonal.at(1, k))
                    nc.tensor.matmul(acc[:, 3, 0:SEQ], o_diag[:, k % N_DIAG, :], o_pad[:, 3, k:k + SEQ], start=(k == 0),
                                     stop=(k == TAPS - 1)).then_inc(o_tapped.sem, 1)

            def attention(l):
                pe.wait_ge(q_out.sem, q_out.at(l, 1))
                pe.wait_ge(k_out.sem, k_out.at(l, 1))
                if LAYERS[l] == "hyb":
                    pe.wait_ge(g_kept.sem, g_kept.at(l, NL))
                head_logits(l, 0)
                head_logits(l, 1)
                if LAYERS[l] == "hyb":
                    linear_values(l)
                else:
                    pe.wait_ge(a_out, out_at(l, NA[l] - 1, 1))
                for h in range(HEADS):
                    head_turn(l, h)
                    if h + 2 < HEADS:
                        head_logits(l, h + 2)
                    if LAYERS[l] == "odd":
                        fourth_block(range(4 * h, min(4 * h + 4, TAPS)))
                    if h:
                        head_values(l, h - 1)
                    if LAYERS[l] == "hyb" and h == 4:
                        turn_y(l, g_normed, 0)
                head_values(l, HEADS - 1)

            def turn_y(l, ready, first):
                src = g_o if ready is g_normed else y_tok
                for t in range(NT):
                    pe.wait_ge(ready.sem, ready.at(l, t))
                    turn_tile(y_part(l, first + t)[2], src[:, t, :], y_turned)

            def turn_ffn(l, c, buf):
                pe.wait_ge(glu_done, glu_at(l, c, 1))
                if not isinstance(c, int) or c > 0:
                    pe.wait_ge(h_low.sem, c + h_low.at(l, 0) - 1)
                for b in range(2):
                    for t in range(NT):
                        tr = nc.tensor.transpose(tb[:, 0, SEQ * b + P * t:SEQ * b + P * (t + 1)],
                                                 glu[:, buf, t, P * b:P * (b + 1)], ident)
                tr.then_inc(h_turned.sem, 1)

            turn_x(0, 0)
            for l in every:
                hook = {"even": even_hook, "odd": odd_hook, "hyb": hyb_hook(l)}[LAYERS[l]]

                def free_in(c, t):
                    if c >= 2:
                        pe.wait_ge(a_out, out_at(l, c - 2, t))
                    elif l > 0:
                        pe.wait_ge(acc_read.sem, acc_read.at(2 * l - 1, t))

                first_chunks(l, "A", U_A[l], IN_BANK, free_in, hook)
                for c in range(2, NA[l]):
                    joint_chunk([Unit(U_A[l] + 4 * c + q) for q in range(4)], c, IN_BANK[c % 2], free_in, hook)
                if LAYERS[l] == "even":
                    even_rest()
                elif LAYERS[l] == "odd":
                    odd_rest()
                else:
                    hyb_rest(l)

                def free_ffn(c, t):
                    if isinstance(c, int):
                        pe.wait_ge(acc_read.sem, acc_read.at(2 * l, t))
                    else:
                        pe.wait_ge(glu_done, c * 2 + (2 * NC * l + t - 3))

                first_chunks(l, "C", U_C[l], FFN_BANK, free_ffn, lambda c, q: turn_ffn(l, 0, 0) if (c, q) == (1, 1) else None)
                with pe.Fori(0, (NC - 2) // LOOP) as j:
                    for r in range(LOOP):
                        units = [Unit(U_C[l] + 4 * (2 + r) + q, j) for q in range(4)]
                        before = FFN_BUF[(1 + r) % LOOP]
                        joint_chunk(units, j * LOOP + (2 + r), FFN_BANK[(2 + r) % LOOP], free_ffn,
                                    lambda c, q: turn_ffn(l, j * LOOP + (1 + r), before) if q == 1 else None)

                down(l)
        @block.scalar
        def _(act):
            chain = Chain(act, act_step)
            fed = [0]

            def high(v):
                act.wait_ge(raw_in[v.raw], v.loads * 32)
                if not v.fresh:
                    act.wait_ge(w_used, v.n - N_W + 1)
                nc.scalar.activation(w_hi[:, v.slot, :], raw[:, v.raw, :], ACT.Copy).then_inc(w_high, 1)

            def feed(n):
                for u in range(fed[0], min(n, U_END)):
                    high(Unit(u))
                fed[0] = max(fed[0], min(n, U_END))

            def x_split(kk, t):
                for h in range(2):
                    act.wait_ge(x_turned.sem, x_turned.at(kk, 2 * t + h))
                    nc.scalar.activation(a_hi[:, 4 * h:4 * h + 4, P * t:P * (t + 1)],
                                         tb[:, h, :].rearrange("p (b n) -> p b n", b=4), ACT.Copy).then_inc(x_high.sem, 1)

            def load_rows(k):
                if k >= NB:
                    return
                if k:
                    act.wait_ge(x_ready.sem, x_ready.at(k - 1, 1))
                for slot, col, row in norm_rows(k):
                    act.dma_start(rows[:, slot, col:col + row.shape[0]], row.partition_broadcast(P)).then_inc(rows_in, 16)

            def boundary(k, t):
                l, ffn = divmod(k, 2)
                def settle(before):
                    if pre[k]:
                        act.wait_ge(spread2.sem, spread2.at(k, before))
                    elif not is_ln[k]:
                        act.wait_ge(squared.sem, squared.at(k, before))

                if t == 1:
                    settle(0)
                if not is_ln[k]:
                    tile_done(act, t, l, "D" if ffn else "B")
                    nc.scalar.activation(squares[:, 0:CH], acc[:, 2 * t, :], ACT.Square, scale=D ** -0.5,
                                         accum_out=ssq[:, t, 0:1]).then_inc(half_squared.sem, 1)
                    act.wait_ge(half_gained.sem, half_gained.at(k, t))
                    nc.scalar.activation(squares[:, CH:D], acc[:, 2 * t + 1, :], ACT.Square, scale=D ** -0.5,
                                         accum_out=ssq[:, t, 1:2]).then_inc(squared.sem, 1)
                if pre[k]:
                    act.wait_ge(x_sum.sem, x_sum.at(k, t))
                    if not is_ln[k]:
                        act.wait_ge(squared.sem, squared.at(k, t))
                    nc.scalar.activation(squares[:, :], x[:, t, :], ACT.Square,
                                         accum_out=ssq2[:, t:t + 1]).then_inc(spread2.sem, 1)
                if t == 1:
                    settle(1)

            def after_boundary(k, end):
                boundary(k, 0)
                feed(end + 6)
                if k + 1 < NB:
                    x_split(k + 1, 0)
                feed(end + 7)
                boundary(k, 1)
                feed(end + 8)

            def chunk_out(l, c, t):
                tile_done(act, t, l, "A", c)
                bank, f = acc[:, IN_BANK[c % 2][t], :], ACT.Copy
                if l == 0:
                    dst = (e_pc, e_pv, e_pu, e_pb)[c][:, t, :]
                elif l == 1:
                    dst = (o_d1[:, t, :], o_d2[:, t, :], p_qk[:, t, 0:CH], p_qk[:, t, CH:D], p_v[:, t, :])[c]
                    f = ACT.Sigmoid if c == 1 else f
                else:
                    dst = (g_pqk[:, t, :], p_qk[:, t, 0:CH], p_qk[:, t, CH:D], p_v[:, t, :], g_v[:, t, :], g_r[:, t, :])[c]
                    f = ACT.Silu if c == 5 else f
                nc.scalar.activation(dst, bank, f).then_inc(a_out, 1)

            def blocks(bank):
                return tb[:, bank, :].rearrange("p (b n) -> p b n", b=2)

            def even_step(c):
                if c == 1:
                    act.wait_ge(params_turned, 1)
                    nc.scalar.activation(pcol[:, :, :], tb[:, 3, 0:4 * N_ROWS].rearrange("p (b r) -> p b r", b=4),
                                         ACT.Copy).then_inc(params_out, 1)
                    act.wait_ge(e_turned.sem, e_turned.at(0, 1))
                    for i in range(2):
                        nc.scalar.activation(e_cT[:, 2 * i:2 * i + 2, :], blocks(i), ACT.Copy).then_inc(e_act.sem, 1)
                if c == 2:
                    for i in range(2):
                        act.wait_ge(e_turned.sem, e_turned.at(0, 4 + i))
                        nc.scalar.activation(e_u[:, 2 * i:2 * i + 2, PAD:], blocks(i), ACT.Copy).then_inc(e_act.sem, 1)

            def even_rest():
                for g in range(4):
                    act.wait_ge(e_turned.sem, e_turned.at(0, 8 + g // 2))
                    nc.scalar.activation(h_hi[:, 4 + g, :], tb[:, g // 2, SEQ * (g % 2):SEQ * (g % 2 + 1)], ACT.Copy,
                                         scale=pcol[:, g, R_PSCALE:R_PSCALE + 1]).then_inc(e_high.sem, 1)
                for i in range(2):
                    act.wait_ge(e_dve.sem, e_dve.at(0, 2 + i))
                    nc.scalar.activation(h_hi[:, 2 * i:2 * i + 2, :], e_y[:, 2 * i:2 * i + 2, :], ACT.Copy).then_inc(e_high.sem, 1)
                feed(U_C[0])
                act.wait_ge(const_in, 16 * 2)
                act.wait_ge(params_in, PARAMS)
                nc.scalar.activation(ident_r[:, :], ident, ACT.Copy)
                nc.scalar.activation(bias_hi[:, :], const[:, C_CAUSAL:C_CAUSAL + 4 * P], ACT.Copy)
                nc.scalar.activation(tiny_hi[:, :, :], tiny_raw[:, :, :], ACT.Copy).then_inc(tiny_high, 1)

            def odd_step(c, end):
                if c == 1:
                    act.wait_ge(o_fsum.sem, o_fsum.at(1, 0))
                    nc.scalar.activation(o_f[:, 0, :], tb[0:GATES, 2, 0:SEQ], ACT.Identity,
                                         bias=fbias[:, 0:1]).then_inc(o_fbiased.sem, 1)
                    log_sigmoid_part(o_f[:, 0], o_f[:, 1], o_f[:, 2], o_f[:, 3], o_fbiased, o_soft, 1)
                    act.wait_ge(o_turned.sem, o_turned.at(1, 1))
                    for i in range(2):
                        nc.scalar.activation(o_pad[:, 2 * i:2 * i + 2, PADT:], blocks(i), ACT.Copy).then_inc(o_padded.sem, 1)
                if c == 2:
                    act.wait_ge(o_fcum.sem, o_fcum.at(1, 0))
                    chain.step(nc.scalar.activation(o_cum[:, 0, 0:P], o_f[:, 1, 0:P], ACT.Copy))
                    nc.scalar.activation(o_cum[:, 0, P:3 * P], o_f[:, 1, :], ACT.Copy).then_inc(o_cumhigh.sem, 1)
                if c == 3:
                    q_part(1)
                feed(end)
                if c == 3:
                    k_part(1)

            def log_sigmoid_part(z, z_abs, e, soft, ready, done, l):
                act.wait_ge(ready.sem, ready.at(l, 0))
                chain.step(nc.scalar.activation(z_abs, z, ACT.Abs))
                chain.settle()
                chain.step(nc.scalar.activation(e, z_abs, ACT.Exp, scale=-1.0))
                chain.settle()
                nc.scalar.activation(soft, e, ACT.Ln, bias=1.0).then_inc(done.sem, 1)

            def odd_rest():
                attention(1)
                turned_weights(1, HEADS - 1)
                act.wait_ge(o_tapped.sem, o_tapped.at(1, TAPS - 1))
                nc.scalar.activation(o_acc[:, 3, :], acc[:, 3, 0:SEQ], ACT.Identity,
                                     bias=pcol[:, 3, R_DWB:R_DWB + 1]).then_inc(o_fourth.sem, 1)
                split_y(1, (0, 1))
                for t in range(NT):
                    act.wait_ge(y_turned.sem, y_turned.at(1, 2 + t))
                    for b in range(4):
                        ins = nc.scalar.activation(o_y[:, t, b, :], tb[:, t, P * b:P * (b + 1)], ACT.Silu,
                                                   scale=pcol[:, b, R_CNG:R_CNG + 1], bias=pcol[:, b, R_CNB:R_CNB + 1])
                        n = chain.step(ins) if b < 3 else None
                    ins.then_inc(o_silu.sem, 1)
                for t in range(NT):
                    chain.settle()
                    act.wait_ge(o_silu.sem, o_silu.at(1, t))
                    nc.scalar.activation(h_hi[:, 4:8, P * t:P * (t + 1)], o_y[:, t, :, :], ACT.Copy).then_inc(y_high.sem, 1)

            def hyb_step(l, c, end):
                if c == 0:
                    act.wait_ge(l_sum.sem, l_sum.at(l, 0))
                    nc.scalar.activation(g_lowT[:, :], tb[0:RANK, 0, 0:SEQ], ACT.Copy).then_inc(l_out.sem, 1)
                    feed(end)
                    act.wait_ge(z_done.sem, z_done.at(l, 0))
                    for b in range(2):
                        col = 2 * (l - 2) + b
                        ins = nc.scalar.activation(g_z[:, b, :], tb[:, 2, SEQ * b:SEQ * (b + 1)], ACT.Identity,
                                                   bias=pcol[:, col, R_GLAB:R_GLAB + 1])
                        if b == 0:
                            chain.step(ins)
                    ins.then_inc(z_out.sem, 1)
                    chain.settle()
                    log_sigmoid_part(g_z[:, :, :], g_e[:, :, :], g_b[:, :, :], g_e[:, :, :], z_out, z_log, l)
                if c == 1:
                    for i in range(2):
                        act.wait_ge(gqk_turned.sem, gqk_turned.at(l, 1))
                        nc.scalar.activation(g_qkT[:, 2 * i:2 * i + 2, :], blocks(i), ACT.Copy,
                                             scale=GLA_SCALE if i == 0 else 1.0).then_inc(gqk_out.sem, 1)
                for n in LEVELS_AFTER.get(c, ()):
                    level_decay(l, n)
                    if n == 5:
                        q_part(l)
                    feed(fed[0] + 1)
                feed(end)

            def level_decay(l, n):
                act.wait_ge(g_diff.sem, g_diff.at(l, n))
                if n:
                    act.wait_ge(g_scaled.sem, g_scaled.at(l, n - 1))
                nc.scalar.activation(g_e[:, :, :], g_z[:, :, :], ACT.Exp, scale=1.0 / GLA_TAU).then_inc(g_exp.sem, 1)

            def hyb_rest(l):
                attention(l)
                for t in range(NT):
                    act.wait_ge(shared.sem, shared.at(l, t))
                    nc.scalar.activation(squares[:, CH * t:CH * (t + 1)], y_tok[:, t, :], ACT.Square,
                                         accum_out=a_ssq[:, t:t + 1]).then_inc(a_spread.sem, 1)
                split_y(l, (2, 3))
                act.wait_ge(a_spread.sem, a_spread.at(l, 1))

            def linear_squares(l):
                for t in range(NT):
                    act.wait_ge(g_done.sem, g_done.at(l, t))
                    for h in range(GLA_H):
                        ins = nc.scalar.activation(nbuf[:, CH * t + P * h:CH * t + P * (h + 1)],
                                                   acc[:, 1 + 2 * t, GLA_DV * h:GLA_DV * (h + 1)], ACT.Square,
                                                   accum_out=g_ssq[:, t, h:h + 1])
                ins.then_inc(g_spread.sem, 1)

            def q_part(l):
                for i in range(2):
                    act.wait_ge(qk_turned.sem, qk_turned.at(l, i))
                    nc.scalar.activation(qT[:, 2 * i:2 * i + 2, :], blocks(2 + i), ACT.Copy, scale=-SCALE).then_inc(q_out.sem, 1)

            def diagonals(taps):
                for k in taps:
                    if k >= N_DIAG:
                        act.wait_ge(o_tapped.sem, o_tapped.at(1, k - N_DIAG))
                    nc.scalar.activation(o_diag[:, k % N_DIAG, :], ident, ACT.Copy,
                                         scale=pcol[:, 3, R_DW + k:R_DW + k + 1]).then_inc(o_diagonal.sem, 1)

            def k_part(l):
                for i in range(2):
                    act.wait_ge(qk_turned.sem, qk_turned.at(l, 2 + i))
                    nc.scalar.activation(kT[:, 2 * i:2 * i + 2, :], blocks(2 + i), ACT.Copy).then_inc(k_out.sem, 1)

            def turned_weights(l, h):
                act.wait_ge(p_turned.sem, p_turned.at(l, h))
                if h >= 2:
                    act.wait_ge(attended.sem, attended.at(l, h - 2))
                nc.scalar.activation(probsT[:, h % 2, :], tb[:, 2 + h % 2, 0:3 * P], ACT.Copy).then_inc(p_out.sem, 1)

            def attention(l):
                if LAYERS[l] == "odd":
                    diagonals(range(8))
                for h in range(HEADS):
                    bank = tb[:, h % 2, :]
                    act.wait_ge(lows.sem, lows.at(l, h))
                    if h >= 2:
                        act.wait_ge(p_turned.sem, p_turned.at(l, h - 2))
                    nc.scalar.activation(probs[:, h % 2, 0:P], bank[:, 0:P], ACT.Exp, scale=-1.0,
                                         bias=low_of[:, h % 2, 0:1], accum_out=total[:, 0, h:h + 1])
                    nc.scalar.activation(probs[:, h % 2, P:3 * P], bank[:, P:3 * P], ACT.Exp, scale=-1.0,
                                         bias=low_of[:, h % 2, 1:2], accum_out=total[:, 1, h:h + 1]).then_inc(weighed.sem, 1)
                    if LAYERS[l] == "hyb" and h == 1:
                        linear_squares(l)
                    if LAYERS[l] == "hyb" and h == 5:
                        split_y(l, (0, 1))
                    if LAYERS[l] == "odd":
                        if h:
                            turned_weights(l, h - 1)
                        diagonals(range(4 * h + 8, min(4 * h + 12, TAPS)))
                    if h < 4:
                        feed(fed[0] + 1)

            def split_y(l, which):
                for i in which:
                    b, t, bank = y_part(l, i)
                    act.wait_ge(y_turned.sem, y_turned.at(l, i))
                    nc.scalar.activation(h_hi[:, b:b + 4, P * t:P * (t + 1)],
                                         ps[:, bank, :].rearrange("p (b n) -> p b n", b=4), ACT.Copy).then_inc(y_high.sem, 1)

            def silu_part(l, c, r, t):
                tile_done(act, t, l, "C", c)
                if not isinstance(c, int):
                    act.wait_ge(glu_done, c * 2 + (2 * NC * l + t - 1))
                nc.scalar.activation(silu[:, FFN_BUF[r], t, :], ps[:, FFN_BANK[r][t], 0:FC], ACT.Silu).then_inc(silu_done, 1)

            def ffn_split(l, c):
                act.wait_ge(h_turned.sem, c + h_turned.at(l, 0))
                dst = h_hi[:, :, :].rearrange("p (c b) n -> p c b n", b=2)[:, c, :, :]
                nc.scalar.activation(dst, blocks(0), ACT.Copy).then_inc(h_high.sem, 1)

            params = [(prow[row:row + src.shape[0], :], src, prow_in) for row, src in (
                (R_EVCONV, a["ev_conv_w"][0]), (R_PSCALE, a["ev_pool_scale"]), (R_DW, a["od_dw_w"][0]), (R_DWB, a["od_dw_b"]),
                (R_CNG, a["od_cn_g"]), (R_CNB, a["od_cn_b"]), (R_GLAB, a["gla_b_gate_2"].rearrange("(o l) n -> o (l n)", o=1)))]
            params.append((const[:, P:N_CONST], a["shape_consts"][:, P:N_CONST], const_in))
            params.append((w_grp[:, :, :], a["ev_pool_w"][0].rearrange("g c d -> c g d"), params_in))
            for l, col in ((1, OD_F), (2, HY_LOW), (3, HY_LOW)):
                c0, w = TINY[l]
                params.append((tiny_raw[:, :, c0:c0 + w], w_in(l)[:, col:col + w].rearrange("(k p) n -> p k n", p=P), params_in))
            params.append((fbias[:, :], a["od_forget_b"].rearrange("o g -> g o"), params_in))
            params.append((w_up[:, :, :], a["gla_w_gate_up_2"].rearrange("l k n -> k l n"), params_in))

            def load_params(n):
                for dst, src, landed in params[:n]:
                    act.dma_start(dst, src).then_inc(landed, 16)
                del params[:n]

            x_split(0, 0)
            for u in range(8):
                feed(u + 1)
                if u >= 2:
                    load_params(1)
            for l in every:
                order = [(0, 0), (1, 0), (0, 1), (1, 1)] + [(c, t) for c in range(2, NA[l]) for t in range(NT)]
                for c, t in order:
                    chunk_out(l, c, t)
                    if (c, t) == (0, 0):
                        x_split(2 * l, 1)
                        if l == 0:
                            load_params(2)
                            feed(N_W)
                            load_params(len(params))
                            load_rows(0)
                        feed(U_A[l] + N_W)
                    if t == 1:
                        if c == 1:
                            load_rows(2 * l) if l else None
                        end = U_A[l] + 4 * (c + 1) + N_W
                        if c == NA[l] - 1:
                            end -= 4
                        if LAYERS[l] == "odd":
                            odd_step(c, end)
                        elif LAYERS[l] == "hyb":
                            hyb_step(l, c, end)
                        elif 0 < c < NA[l] - 1:
                            even_step(c)
                            feed(end - 4)
                if LAYERS[l] == "even":
                    even_rest()
                    feed(U_C[l] + 4)
                elif LAYERS[l] == "odd":
                    odd_rest()
                else:
                    hyb_rest(l)
                after_boundary(2 * l, U_C[l])
                silu_part(l, 0, 0, 0)
                x_split(2 * l + 1, 1)
                feed(U_C[l] + N_W)
                silu_part(l, 1, 1, 0)
                silu_part(l, 0, 0, 1)
                feed(U_C[l] + 4 + N_W)
                ffn_split(l, 0)
                silu_part(l, 1, 1, 1)
                feed(U_C[l] + 8 + N_W)
                load_rows(2 * l + 1)
                with act.Fori(0, (NC - 2) // LOOP) as j:
                    for r in range(LOOP):
                        c = j * LOOP + (2 + r)
                        ffn_split(l, j * LOOP + (1 + r))
                        for t in range(NT):
                            silu_part(l, c, (2 + r) % LOOP, t)
                        for q in range(4):
                            high(Unit(U_C[l] + 4 * (2 + r) + N_W + q, j))
                fed[0] += 4 * (NC - 2)
                ffn_split(l, NC - 1)
                feed(U_D[l] + KF - KD + N_W)
                after_boundary(2 * l + 1, U_D[l] + KF)

        @block.vector
        def _(dve):
            chain = Chain(dve, dve_step)
            fed = [0]
            V = nc.vector

            def low(v):
                dve.wait_ge(w_high, v.n + 1)
                V.tensor_tensor(w_lo[:, v.slot, :], raw[:, v.raw, :], w_hi[:, v.slot, :].bitcast(F32), ALU.subtract).then_inc(w_low, 1)

            def feed(n):
                for u in range(fed[0], min(n, U_END)):
                    low(Unit(u))
                fed[0] = max(fed[0], min(n, U_END))

            def x_split(kk, t):
                for h in range(2):
                    dve.wait_ge(x_high.sem, x_high.at(kk, 2 * t + h))
                    part = slice(4 * h, 4 * h + 4), slice(P * t, P * (t + 1))
                    V.tensor_tensor(a_lo[:, part[0], part[1]], tb[:, h, :].rearrange("p (b n) -> p b n", b=4),
                                    a_hi[:, part[0], part[1]].bitcast(F32), ALU.subtract).then_inc(x_low.sem, 1)

            def boundary(k, t):
                l, ffn = divmod(k, 2)
                xt = x[:, t, :]
                dve.wait_ge(rows_in, rows_at(k))
                tile_done(dve, t, l, "D" if ffn else "B")
                if is_ln[k]:
                    for h in range(2):
                        xh = x[:, t, CH * h:CH * (h + 1)]
                        ins = V.scalar_tensor_tensor(xh, xh, ALPHA, acc[:, 2 * t + h, :], ALU.mult, ALU.add)
                        if h == 0:
                            chain.step(ins)
                    ins.then_inc(acc_read.sem, 1)
                    for h in range(2):
                        if h == 0:
                            chain.settle()
                        else:
                            dve.wait_ge(acc_read.sem, acc_read.at(k, t))
                        chain.step(V.bn_stats(bn[:, t, h, :], x[:, t, CH * h:CH * (h + 1)]))
                    chain.settle()
                    V.bn_aggr(mv[:, t, :], bn[:, t, :, :].rearrange("p h s -> p (h s)")).then_inc(spread.sem, 1)
                    dve.wait_ge(spread.sem, spread.at(k, t))
                    chain.step(V.scalar_tensor_tensor(xt, xt, mv[:, t, 0:1], rows[:, 0, :], ALU.subtract, ALU.mult))
                    chain.settle()
                    dve.wait_ge(scaled.sem, scaled.at(k, t))
                    ins = V.scalar_tensor_tensor(xt, xt, rstd[:, t:t + 1], rows[:, 1, :], ALU.mult, ALU.add)
                else:
                    if t == 1 and k + 1 < NB:
                        dve.wait_ge(x_turned.sem, x_turned.at(k + 1, 1))
                    V.tensor_tensor(nbuf[:, CH:D], acc[:, 2 * t + 1, :], rows[:, 0, CH:D], ALU.mult).then_inc(half_gained.sem, 1)
                    dve.wait_ge(half_squared.sem, half_squared.at(k, t))
                    V.tensor_tensor(nbuf[:, 0:CH], acc[:, 2 * t, :], rows[:, 0, 0:CH], ALU.mult).then_inc(acc_read.sem, 1)
                    dve.wait_ge(acc_read.sem, acc_read.at(k, t))
                    dve.wait_ge(scaled.sem, scaled.at(k, t))
                    ins = V.scalar_tensor_tensor(xt, nbuf[:, :], rstd[:, t:t + 1], xt, ALU.mult, ALU.add)
                if not pre[k]:
                    ins.then_inc(x_ready.sem, 1)
                    dve.wait_ge(x_ready.sem, x_ready.at(k, t))
                else:
                    ins.then_inc(x_sum.sem, 1)
                    dve.wait_ge(x_sum.sem, x_sum.at(k, t))
                    if is_ln[k] and t == 1:
                        dve.wait_ge(x_turned.sem, x_turned.at(k + 1, 1))
                    chain.step(V.tensor_tensor(nbuf[:, :], xt, pre_row(k), ALU.mult))
                    chain.settle()
                    dve.wait_ge(scaled2.sem, scaled2.at(k, t))
                    V.tensor_scalar(nbuf[:, :], nbuf[:, :], rstd2[:, t:t + 1], None, ALU.mult).then_inc(x_ready.sem, 1)

            def after_boundary(k, end):
                boundary(k, 0)
                feed(end + 6)
                if k + 1 < NB:
                    x_split(k + 1, 0)
                feed(end + 7)
                boundary(k, 1)
                feed(end + 8)

            def blocks(bank):
                return tb[:, bank, :].rearrange("p (b n) -> p b n", b=2)

            def even_step(c):
                if c == 1:
                    for i in range(2):
                        dve.wait_ge(e_act.sem, e_act.at(0, i))
                        dve.wait_ge(e_turned.sem, e_turned.at(0, 3))
                        V.tensor_tensor(e_m[:, 2 * i:2 * i + 2, :], blocks(2 + i), e_cT[:, 2 * i:2 * i + 2, :], ALU.mult).then_inc(e_dve.sem, 1)
                    dve.wait_ge(e_dve.sem, e_dve.at(0, 1))
                    for tap in range(3):
                        chain.settle()
                        for b in range(4):
                            w = pcol[:, b, R_EVCONV + 2 - tap:R_EVCONV + 3 - tap]
                            if tap == 0:
                                chain.step(V.tensor_scalar(e_y[:, b, :], e_m[:, b, :], w, None, ALU.mult))
                            else:
                                chain.step(V.scalar_tensor_tensor(e_y[:, b, tap:], e_m[:, b, 0:SEQ - tap], w, e_y[:, b, tap:],
                                                                  ALU.mult, ALU.add))
                if c == 2:
                    chain.step(V.memset(e_u[:, :, 0:PAD], 0.0))
                    chain.step(V.memset(e_sA[:, :, 0:1], 0.0))
                    dve.wait_ge(e_act.sem, e_act.at(0, 3))
                    chain.settle()
                    W = PAD + SEQ
                    chain.step(V.tensor_tensor(e_sA[:, :, 1:W], e_u[:, :, 1:W], e_u[:, :, 0:W - 1], ALU.add))
                    chain.settle()
                    chain.step(V.tensor_tensor(e_sB[:, 1:4, 3:W], e_sA[:, 1:4, 3:W], e_sA[:, 1:4, 1:W - 2], ALU.add))
                    chain.settle()
                    chain.step(V.tensor_tensor(e_sA[:, 2:4, 7:W], e_sB[:, 2:4, 7:W], e_sB[:, 2:4, 3:W - 4], ALU.add))
                    chain.settle()
                    chain.step(V.tensor_tensor(e_sB[:, 3, 15:W], e_sA[:, 3, 15:W], e_sA[:, 3, 7:W - 8], ALU.add))
                    chain.settle()
                    dve.wait_ge(const_in, 16 * 2)
                    sums = (e_sA, e_sB, e_sA, e_sB)
                    for g in range(4):
                        chain.step(V.tensor_tensor(e_edge[:, g, :], sums[g][:, g, PAD:2 * PAD],
                                                   const[:, C_POOL + PAD * g:C_POOL + PAD * (g + 1)], ALU.mult))
                        chain.step(V.scalar_tensor_tensor(e_pool[:, g, :], sums[g][:, g, PAD:], 1.0 / WINDOWS[g], e_u[:, g, PAD:],
                                                          ALU.mult, ALU.subtract))
                    chain.settle()
                    V.tensor_tensor(e_pool[:, :, 0:PAD], e_edge[:, :, :], e_u[:, :, PAD:2 * PAD], ALU.subtract).then_inc(e_pooled.sem, 1)

            def even_rest():
                for g in range(4):
                    dve.wait_ge(e_high.sem, e_high.at(0, 1 + 2 * (g // 2)))
                    V.scalar_tensor_tensor(h_lo[:, Y_LO + 4 + g, :], tb[:, g // 2, SEQ * (g % 2):SEQ * (g % 2 + 1)],
                                           pcol[:, g, R_PSCALE:R_PSCALE + 1], h_hi[:, 4 + g, :].bitcast(F32),
                                           ALU.mult, ALU.subtract).then_inc(e_low.sem, 1)
                for i in range(2):
                    dve.wait_ge(e_turned.sem, e_turned.at(0, 6 + i))
                    V.tensor_tensor(e_y[:, 2 * i:2 * i + 2, :], blocks(2 + i), e_y[:, 2 * i:2 * i + 2, :], ALU.mult).then_inc(e_dve.sem, 1)
                for i in range(2):
                    dve.wait_ge(e_high.sem, e_high.at(0, 4 + i))
                    V.tensor_tensor(h_lo[:, Y_LO + 2 * i:Y_LO + 2 * i + 2, :], e_y[:, 2 * i:2 * i + 2, :],
                                    h_hi[:, 2 * i:2 * i + 2, :].bitcast(F32), ALU.subtract).then_inc(e_low.sem, 1)
                feed(U_C[0])
                dve.wait_ge(tiny_high, 1)
                V.tensor_tensor(bias_lo[:, :], const[:, C_DIL:C_DIL + 3 * P], bias_hi[:, P:4 * P].bitcast(F32), ALU.subtract)
                V.tensor_tensor(tiny_lo[:, :, :], tiny_raw[:, :, :], tiny_hi[:, :, :].bitcast(F32), ALU.subtract).then_inc(tiny_done, 1)

            taps = [(k, b) for k in range(TAPS) for b in range(3)]
            tap_step = {}

            def convolve(n):
                for _ in range(min(n, len(taps))):
                    k, b = taps.pop(0)
                    w, src = pcol[:, b, R_DW + k:R_DW + k + 1], o_pad[:, b, k:k + SEQ]
                    if k == 0:
                        ins = V.tensor_scalar(o_acc[:, b, :], src, w, pcol[:, b, R_DWB:R_DWB + 1], ALU.mult, ALU.add)
                    else:
                        chain.settle(tap_step[b])
                        ins = V.scalar_tensor_tensor(o_acc[:, b, :], src, w, o_acc[:, b, :], ALU.mult, ALU.add)
                    if taps:
                        tap_step[b] = chain.step(ins)
                    else:
                        ins.then_inc(o_conv.sem, 1)

            def odd_step(c, end):
                if c == 1:
                    dve.wait_ge(a_out, out_at(1, 1, 1))
                    V.tensor_tensor(o_d1[:, :, :], o_d1[:, :, :], o_d2[:, :, :], ALU.mult).then_inc(o_gated.sem, 1)
                    feed(end)
                    dve.wait_ge(o_soft.sem, o_soft.at(1, 0))
                    chain.step(V.scalar_tensor_tensor(o_f[:, 0, :], o_f[:, 0, :], 0.0, o_f[:, 3, :], ALU.min, ALU.subtract))
                    chain.settle()
                    ones = const[0:GATES, C_TRI + P:C_TRI + P + 1].broadcast_to([GATES, SEQ])
                    V.tensor_tensor_scan(o_f[:, 1, :], ones, o_f[:, 0, :], 0.0, ALU.mult, ALU.add).then_inc(o_fcum.sem, 1)
                    dve.wait_ge(o_turned.sem, o_turned.at(1, 1))
                    chain.step(V.memset(o_pad[:, :, 0:PADT], 0.0))
                    chain.settle()
                    dve.wait_ge(o_padded.sem, o_padded.at(1, 1))
                    convolve(8)
                if c == 2:
                    dve.wait_ge(o_cumhigh.sem, o_cumhigh.at(1, 0))
                    for at, n in ((0, P), (P, SEQ)):
                        ins = V.tensor_tensor(o_cum[:, 1, at:at + n], o_f[:, 1, 0:n], o_cum[:, 0, at:at + n].bitcast(F32), ALU.subtract)
                        if at == 0:
                            chain.step(ins)
                    ins.then_inc(o_cumlow.sem, 1)
                    convolve(8)
                    feed(end)
                    convolve(8)
                if c == 3:
                    feed(end)
                    convolve(10)
                if c == 4:
                    feed(end)

            def odd_rest():
                attention(1, lambda h: convolve(7))
                convolve(len(taps))
                share(1)
                for t in range(NT):
                    dve.wait_ge(o_back.sem, o_back.at(1, t))
                    chain.step(V.bn_stats(c_bn[:, t, :], tb[:, 2 + t, :]))
                    chain.settle()
                    V.bn_aggr(c_mv[:, t, :], c_bn[:, t, :]).then_inc(o_spread.sem, 1)
                split_y(1, (0, 1))
                for t in range(NT):
                    dve.wait_ge(o_scaled.sem, o_scaled.at(1, t))
                    dve.wait_ge(o_spread.sem, o_spread.at(1, t))
                    V.tensor_scalar(o_z[:, t, :], tb[:, 2 + t, :], c_mv[:, t, 0:1], c_rstd[:, t:t + 1], ALU.subtract,
                                    ALU.mult).then_inc(o_normed.sem, 1)
                for t in range(NT):
                    dve.wait_ge(y_high.sem, y_high.at(1, 2 + t))
                    tok = slice(P * t, P * (t + 1))
                    V.tensor_tensor(h_lo[:, Y_LO + 4:Y_LO + 8, tok], o_y[:, t, :, :], h_hi[:, 4:8, tok].bitcast(F32),
                                    ALU.subtract).then_inc(y_low.sem, 1)
                feed(U_C[1] + 4)

            def rope(l):
                dve.wait_ge(a_out, out_at(l, 2, 1))
                v = p_qk[:, :, :].rearrange("p t (h d) -> p t h d", d=HD)
                x1, x2 = v[:, :, :, 0:ROPE_HALF], v[:, :, :, ROPE_HALF:2 * ROPE_HALF]
                full = [P, NT, 2 * HEADS, ROPE_HALF]

                def table(at):
                    return const[:, at:at + NT * ROPE_HALF].rearrange("p (t d) -> p t d", t=NT).unsqueeze(2).broadcast_to(full)

                prod = nbuf[:, :].rearrange("p (i t h d) -> p i t h d", i=4, t=NT, h=2 * HEADS)
                for i, (u, at) in enumerate(((x1, C_COS), (x2, C_SIN), (x2, C_COS), (x1, C_SIN))):
                    chain.step(V.tensor_tensor(prod[:, i], u, table(at), ALU.mult))
                chain.settle()
                chain.step(V.tensor_tensor(x1, prod[:, 0], prod[:, 1], ALU.subtract))
                V.tensor_tensor(x2, prod[:, 2], prod[:, 3], ALU.add).then_inc(roped.sem, 1)

            def hyb_step(l, c, end):
                if c == 1:
                    feed(end - 4)
                    dve.wait_ge(z_log.sem, z_log.at(l, 0))
                    chain.step(V.scalar_tensor_tensor(g_z[:, :, :], g_z[:, :, :], 0.0, g_e[:, :, :], ALU.min, ALU.subtract))
                    chain.settle()
                    ones = const[:, C_TRI + P:C_TRI + P + 1].broadcast_to([P, SEQ])
                    for b in range(2):
                        chain.step(V.tensor_tensor_scan(g_b[:, b, :], ones, g_z[:, b, :], 0.0, ALU.mult, ALU.add))
                    chain.settle()
                for n in LEVELS_AFTER.get(c, ()):
                    level_distance(l, n)
                    if n == 3:
                        rope(l)
                    keep(l, n)
                    level_factors(l, n)
                    feed(fed[0] + 1)
                if c == 4:
                    k_part(l)
                    feed(end)
                    keep(l, NL)
                feed(end)

            def output_gate(l, t):
                dve.wait_ge(a_out, out_at(l, 5, t))
                dve.wait_ge(rows_in, rows_at(2 * l))
                chain.step(V.tensor_tensor(g_r[:, t, :], g_r[:, t, :], rows[:, 2, HALF:D], ALU.mult))

            def level_distance(l, n):
                m = LEVELS[n]
                b, z = (level_view(u[:, :, :], m) for u in (g_b, g_z))
                mid = b[:, :, 0, m - 1:m].broadcast_to([P, NT * P // m, m])
                if n:
                    dve.wait_ge(g_exp.sem, g_exp.at(l, n - 1))
                chain.step(V.tensor_tensor(z[:, :, 1, :], b[:, :, 1, :], mid, ALU.subtract))
                V.tensor_tensor(z[:, :, 0, :], mid, b[:, :, 0, :], ALU.subtract).then_inc(g_diff.sem, 1)

            def level_factors(l, n):
                m = LEVELS[n]
                o, e = level_view(g_x[:, (n + 1) % 2, :, :], m), level_view(g_e[:, :, :], m)
                q, k = level_view(g_qkT[:, 0:2, :], m), level_view(g_qkT[:, 2:4, :], m)
                dve.wait_ge(g_exp.sem, g_exp.at(l, n))
                if n >= 2:
                    dve.wait_ge(g_pair.sem, g_pair.at(l, n - 1))
                chain.step(V.tensor_tensor(o[:, :, 1, :], e[:, :, 1, :], q[:, :, 1, :], ALU.mult))
                V.tensor_tensor(o[:, :, 0, :], e[:, :, 0, :], k[:, :, 0, :], ALU.mult).then_inc(g_scaled.sem, 1)

            def keep(l, n):
                dve.wait_ge(g_pair.sem, g_pair.at(l, n))
                for par in range(2):
                    pair = tb[:, par, :]
                    if n == 0:
                        ins = V.tensor_tensor(g_att[:, 4 * par:4 * par + 4, :], pair.rearrange("p (i n) -> p i n", i=4),
                                              ident.unsqueeze(1).broadcast_to([P, 4, P]), ALU.mult)
                    elif n == 1:
                        ins = V.tensor_copy(g_far[:, 2 * par:2 * par + 2, :], pair[:, 0:2 * P].rearrange("p (i n) -> p i n", i=2))
                    else:
                        m = LEVELS[n - 1]
                        dst = g_att[:, 4 * par:4 * par + 4, :].rearrange("p i (j s m) -> p i j s m", s=2, m=m)[:, :, :, 1, :]
                        mask = right(const[:, C_LEVEL + P * (n - 2):C_LEVEL + P * (n - 1)].bitcast(I32), m)
                        src = pair[:, 0:2 * P].rearrange("p (i j m) -> p i j m", i=4, m=m)
                        ins = V.copy_predicated(dst, mask.unsqueeze(1).broadcast_to([P, 4, P // (2 * m), m]), src)
                    if par == 0:
                        chain.step(ins)
                ins.then_inc(g_kept.sem, 1)

            def linear_norm(l, t):
                dve.wait_ge(g_rooted.sem, g_rooted.at(l, 0))
                chain.step(V.tensor_tensor(heads(g_o[:, t, :], GLA_H), heads(acc[:, 1 + 2 * t, :], GLA_H),
                                           g_rstd[:, t, :].unsqueeze(2).broadcast_to([P, GLA_H, GLA_DV]), ALU.mult))
                chain.settle()
                V.tensor_tensor(g_o[:, t, :], g_o[:, t, :], g_r[:, t, :], ALU.mult).then_inc(g_normed.sem, 1)

            def hyb_rest(l):
                def beside(h):
                    if h == 0:
                        output_gate(l, 1)
                    elif h in (2, 3):
                        linear_norm(l, h - 2)
                    elif h in (5, 6):
                        split_y(l, (h - 5,))

                output_gate(l, 0)
                attention(l, beside)
                share(l)
                for t in range(NT):
                    dve.wait_ge(a_scaled.sem, a_scaled.at(l, t))
                    V.scalar_tensor_tensor(y_tok[:, t, :], y_tok[:, t, :], a_rstd[:, t:t + 1], rows[:, 2, 0:HALF], ALU.mult,
                                           ALU.mult).then_inc(a_normed.sem, 1)
                feed(U_C[l] + 4)
                split_y(l, (2, 3))

            def k_part(l):
                for i in range(2):
                    dve.wait_ge(qk_turned.sem, qk_turned.at(l, 2 + i))
                    V.tensor_copy(kT[:, 2 * i:2 * i + 2, :], blocks(2 + i)).then_inc(k_out.sem, 1)

            def head_lows(l, h):
                bank = tb[:, h % 2, :]
                dve.wait_ge(logits.sem, logits.at(l, h))
                if h >= 2:
                    dve.wait_ge(weighed.sem, weighed.at(l, h - 2))
                chain.step(V.tensor_reduce(low_of[:, h % 2, 0:1], bank[:, 0:P], AX_X, ALU.min))
                V.tensor_reduce(low_of[:, h % 2, 1:2], bank[:, P:3 * P], AX_X, ALU.min).then_inc(lows.sem, 1)

            def attention(l, beside):
                tile_done(dve, 1, l, "A", NA[l] - 1)
                head_lows(l, 0)
                for h in range(HEADS):
                    if h + 1 < HEADS:
                        head_lows(l, h + 1)
                    beside(h)
                    if LAYERS[l] == "odd":
                        continue
                    dve.wait_ge(p_turned.sem, p_turned.at(l, h))
                    if h >= 2:
                        dve.wait_ge(attended.sem, attended.at(l, h - 2))
                    V.tensor_copy(probsT[:, h % 2, :], tb[:, 2 + h % 2, 0:3 * P]).then_inc(p_out.sem, 1)
                    if h in (1, 4):
                        feed(fed[0] + 1)

            def share(l):
                dve.wait_ge(weighed.sem, weighed.at(l, HEADS - 1))
                chain.step(V.reciprocal(share_of[:, :, :], total[:, :, :]))
                chain.settle()
                dve.wait_ge(attended.sem, attended.at(l, HEADS - 1))
                for t in range(NT):
                    V.tensor_tensor(heads(y_tok[:, t, :], HEADS), heads(acc[:, 2 * t, :], HEADS),
                                    share_of[:, t, :].unsqueeze(2).broadcast_to([P, HEADS, HD]), ALU.mult).then_inc(shared.sem, 1)

            def split_y(l, which):
                for i in which:
                    b, t, bank = y_part(l, i)
                    tok = slice(P * t, P * (t + 1))
                    dve.wait_ge(y_high.sem, y_high.at(l, i))
                    V.tensor_tensor(h_lo[:, Y_LO + b:Y_LO + b + 4, tok], ps[:, bank, :].rearrange("p (b n) -> p b n", b=4),
                                    h_hi[:, b:b + 4, tok].bitcast(F32), ALU.subtract).then_inc(y_low.sem, 1)

            def glu_part(l, c, r, t):
                dve.wait_ge(silu_done, glu_at(l, c, t))
                if not isinstance(c, int):
                    dve.wait_ge(h_turned.sem, c + (h_turned.at(l, 0) - 1))
                V.tensor_tensor(glu[:, FFN_BUF[r], t, :], silu[:, FFN_BUF[r], t, :], ps[:, FFN_BANK[r][t], FC:2 * FC],
                                ALU.mult).then_inc(glu_done, 1)

            def ffn_split(l, c):
                dve.wait_ge(h_high.sem, c + h_high.at(l, 0))
                hi, lo = (u[:, :, :].rearrange("p (c b) n -> p c b n", b=2)[:, c, :, :] for u in (h_hi, h_lo))
                V.tensor_tensor(lo, blocks(0), hi.bitcast(F32), ALU.subtract).then_inc(h_low.sem, 1)

            x_split(0, 0)
            feed(8)
            for l in every:
                x_split(2 * l, 1)
                feed(U_A[l] + N_W)
                for c in range(1, NA[l]):
                    end = U_A[l] + 4 * (c + 1) + N_W
                    if c == NA[l] - 1:
                        end -= 4
                    if LAYERS[l] == "odd":
                        odd_step(c, end)
                    elif LAYERS[l] == "hyb":
                        hyb_step(l, c, end)
                    elif c < NA[l] - 1:
                        even_step(c)
                        feed(end - 4)
                if LAYERS[l] == "even":
                    even_rest()
                    feed(U_C[l] + 4)
                elif LAYERS[l] == "odd":
                    odd_rest()
                else:
                    hyb_rest(l)
                after_boundary(2 * l, U_C[l])
                glu_part(l, 0, 0, 0)
                x_split(2 * l + 1, 1)
                feed(U_C[l] + N_W)
                glu_part(l, 1, 1, 0)
                glu_part(l, 0, 0, 1)
                feed(U_C[l] + 4 + N_W)
                ffn_split(l, 0)
                glu_part(l, 1, 1, 1)
                feed(U_C[l] + 8 + N_W)
                with dve.Fori(0, (NC - 2) // LOOP) as j:
                    for r in range(LOOP):
                        ffn_split(l, j * LOOP + (1 + r))
                        for t in range(NT):
                            glu_part(l, j * LOOP + (2 + r), (2 + r) % LOOP, t)
                        for q in range(4):
                            low(Unit(U_C[l] + 4 * (2 + r) + N_W + q, j))
                fed[0] += 4 * (NC - 2)
                ffn_split(l, NC - 1)
                feed(U_D[l] + KF - KD + N_W)
                after_boundary(2 * l + 1, U_D[l] + KF)

        @block.gpsimd
        def _(pool):
            chain = Chain(pool, pool_step)
            nc.gpsimd.memset(minus_half, -0.5).then_inc(set_up, 1)
            pool.wait_ge(set_up, 1)

            def root(dst, src, scale, eps, st, n):
                chain.step(nc.gpsimd.tensor_scalar(dst, src, scale, eps, ALU.mult, ALU.add))
                chain.settle()
                nc.gpsimd.tensor_tensor(dst, dst, minus_half[:, 0:n], ALU.pow).then_inc(st.sem, 1)

            def boundary(k):
                for t in range(NT):
                    one = slice(t, t + 1)
                    if is_ln[k]:
                        pool.wait_ge(spread.sem, spread.at(k, t))
                        root(rstd[:, one], mv[:, t, 1:2], 1.0, LN_EPS, scaled, 1)
                    else:
                        pool.wait_ge(squared.sem, squared.at(k, t))
                        chain.step(nc.gpsimd.tensor_scalar(rstd[:, one], ssq[:, t, 0:1], ssq[:, t, 1:2], RMS_EPS, ALU.add, ALU.add))
                        chain.settle()
                        nc.gpsimd.tensor_tensor(rstd[:, one], rstd[:, one], minus_half[:, 0:1], ALU.pow).then_inc(scaled.sem, 1)
                    if pre[k]:
                        pool.wait_ge(spread2.sem, spread2.at(k, t))
                        root(rstd2[:, one], ssq2[:, one], 1.0 / D, RMS_EPS, scaled2, 1)

            for l in every:
                if LAYERS[l] == "odd":
                    for t in range(NT):
                        pool.wait_ge(o_spread.sem, o_spread.at(l, t))
                        root(c_rstd[:, t:t + 1], c_mv[:, t, 1:2], 1.0, LN_EPS, o_scaled, 1)
                if LAYERS[l] == "hyb":
                    pool.wait_ge(g_spread.sem, g_spread.at(l, 0))
                    root(g_rstd.rearrange("p t h -> p (t h)"), g_ssq.rearrange("p t h -> p (t h)"), 1.0 / GLA_DV, RMS_EPS,
                         g_rooted, NT * GLA_H)
                    for t in range(NT):
                        pool.wait_ge(a_spread.sem, a_spread.at(l, t))
                        root(a_rstd[:, t:t + 1], a_ssq[:, t:t + 1], 1.0 / HALF, RMS_EPS, a_scaled, 1)
                boundary(2 * l)
                boundary(2 * l + 1)


INPUTS = (
    "x", "ev_w_in", "ev_conv_w", "ev_pool_w", "ev_pool_scale", "ev_w_out", "od_w_in", "od_forget_b", "od_dw_w",
    "od_dw_b", "od_cn_g", "od_cn_b", "od_w_out", "ln_mix_g", "ln_mix_b", "ln_ffn_g", "ln_ffn_b", "ffn_w_in",
    "ffn_w_out", "mix_pre_norm_2", "mix_post_norm_2", "ffn_pre_norm_2", "ffn_post_norm_2", "w_in_2",
    "gla_w_gate_up_2", "gla_b_gate_2", "gla_out_norm_2", "attn_out_norm_2", "w_out_2", "w_gate_2", "w_up_2",
    "w_down_2",
)


def kernel(**inputs):
    import concourse.bacc as bacc
    import numpy as np
    from concourse.bass_utils import run_bass_kernel_spmd

    nc = bacc.Bacc("TRN2", target_bir_lowering=False, num_devices=1, dynamic_dma_scratch_size=1024)
    arrays = {name: np.ascontiguousarray(inputs[name]) for name in INPUTS}
    arrays["shape_consts"] = shape_constants()
    aps = {name: nc.dram_tensor(name, v.shape, mybir.dt.from_np(v.dtype), kind="ExternalInput").ap() for name, v in arrays.items()}
    out = nc.dram_tensor("out", (1, SEQ, D), F32, kind="ExternalOutput").ap()
    blocks_kernel(nc, aps, out)
    result = run_bass_kernel_spmd(nc, [arrays], core_ids=[0])
    return result.results[0]["out"]
```
